# Optimizing a Trainium2 kernel written in Bass

```python
import math
import jax, jax.numpy as jnp
from jax import lax
import numpy as np

D_MODEL = 1024
BATCH = 1
SEQ = 512
DEPTH = 2

PLE_DIM = 256
ROPE_THETA = 500000.0
MAX_POS_OFFSET = 4096
A_HEAD_DIM = 64
A_HEADS = D_MODEL // (2 * A_HEAD_DIM)
A_ROT = A_HEAD_DIM // 4
A_PATTERNS = ((128, 1), (512, 4), (2048, 16))
B_HEADS = D_MODEL // 128
B_Q_LORA = 3 * D_MODEL // 8
B_KV_LORA = D_MODEL // 4
B_NOPE = 64
B_ROPE = 32
B_V = 64
C_HEAD_DIM = 64
C_HEADS = D_MODEL // (2 * C_HEAD_DIM)
C_ROT = C_HEAD_DIM // 4
D_FF = 256 * math.ceil(8 * D_MODEL / 3 / 256)
CONV_WIDTH = 3
Q_BLOCK = 128
LN_EPS = 1e-5
RMS_EPS = 1e-6
NEG_INF = -1e30
N_AB = (DEPTH + 1) // 2
N_C = DEPTH // 2
ALPHA = (2 * DEPTH) ** 0.25
BETA = (8 * DEPTH) ** -0.25
A_WIDTH = A_HEADS * A_HEAD_DIM
AB_IN = 3 * A_WIDTH + B_Q_LORA + B_KV_LORA + B_ROPE
AB_MIX = A_WIDTH + B_HEADS * B_V
C_QK = C_HEADS * 2 * C_HEAD_DIM
C_MIX = C_HEADS * 2 * C_HEAD_DIM


def layer_norm(x, g, b):
    xf = x.astype(jnp.float32)
    mu = jnp.mean(xf, axis=-1, keepdims=True)
    var = jnp.mean(jnp.square(xf - mu), axis=-1, keepdims=True)
    y = (xf - mu) * lax.rsqrt(var + LN_EPS)
    return (y * g.astype(jnp.float32) + b.astype(jnp.float32)).astype(x.dtype)

def rms_norm(x, g, eps):
    xf = x.astype(jnp.float32)
    y = xf * lax.rsqrt(jnp.mean(jnp.square(xf), axis=-1, keepdims=True) + eps)
    return (y * g.astype(jnp.float32)).astype(x.dtype)

def rope_tables(positions, rot):
    inv_freq = 1.0 / (ROPE_THETA ** (jnp.arange(0, rot, 2, dtype=jnp.float32) / rot))
    ang = positions.astype(jnp.float32)[..., None] * inv_freq
    return jnp.cos(ang), jnp.sin(ang)

def apply_rope(x, cos, sin, rot):
    bshape = cos.shape[:2] + (1,) * (x.ndim - 3) + cos.shape[-1:]
    c = cos.reshape(bshape).astype(x.dtype)
    s = sin.reshape(bshape).astype(x.dtype)
    half = rot // 2
    x1, x2, rest = x[..., :half], x[..., half:rot], x[..., rot:]
    return jnp.concatenate([x1 * c - x2 * s, x2 * c + x1 * s, rest], axis=-1)

def dilated_window_attention(q, k, v, window, dilation):
    B, H, S, dh = q.shape
    n_side = window // (2 * dilation)
    L = S // dilation
    blk = n_side
    nb = -(-L // blk)
    Lp = nb * blk

    def strided(t):
        return t.reshape(B, H, L, dilation, dh).transpose(0, 1, 3, 2, 4)

    def slabs(t):
        tp = jnp.pad(t, ((0, 0), (0, 0), (0, 0), (blk, Lp - L + blk), (0, 0)))
        tp = tp.reshape(B, H, dilation, nb + 2, blk, dh)
        return jnp.concatenate([tp[:, :, :, 0:nb], tp[:, :, :, 1:nb + 1], tp[:, :, :, 2:nb + 2]], axis=4)

    qb = jnp.pad(strided(q), ((0, 0), (0, 0), (0, 0), (0, Lp - L), (0, 0))).reshape(B, H, dilation, nb, blk, dh)
    kb = slabs(strided(k))
    vb = slabs(strided(v))
    s = jnp.einsum("bhrnqd,bhrnkd->bhrnqk", qb, kb) * (dh ** -0.5)
    qi = jnp.arange(nb)[:, None, None] * blk + jnp.arange(blk)[None, :, None]
    ki = jnp.arange(nb)[:, None, None] * blk - blk + jnp.arange(3 * blk)[None, None, :]
    valid = (ki >= 0) & (ki < L) & (jnp.abs(ki - qi) <= n_side)
    s = jnp.where(valid, s, NEG_INF)
    m = jnp.max(s, axis=-1, keepdims=True)
    e = jnp.exp(s - m)
    l = jnp.sum(e, axis=-1)
    o = jnp.einsum("bhrnqk,bhrnkd->bhrnqd", e, vb) / l[..., None]
    lse = m[..., 0] + jnp.log(l)
    o = o.reshape(B, H, dilation, Lp, dh)[:, :, :, :L].transpose(0, 1, 3, 2, 4).reshape(B, H, S, dh)
    lse = lse.reshape(B, H, dilation, Lp)[..., :L].transpose(0, 1, 3, 2).reshape(B, H, S)
    return o, lse

def dilated_mixture(q, k, v):
    B, S, H, dh = q.shape
    qf, kf, vf = (t.astype(jnp.float32).transpose(0, 2, 1, 3) for t in (q, k, v))
    outs, lses = [], []
    for window, dilation in A_PATTERNS:
        o, lse = dilated_window_attention(qf, kf, vf, window, dilation)
        outs.append(o)
        lses.append(lse)
    w = jax.nn.softmax(jnp.stack(lses), axis=0)
    o = jnp.sum(w[..., None] * jnp.stack(outs), axis=0)
    return o.transpose(0, 2, 1, 3).reshape(B, S, H * dh)

def dense_attention(q, k, v, scale):
    B, S, H, dq = q.shape
    dv = v.shape[-1]
    nq = S // Q_BLOCK
    kf = k.astype(jnp.float32).transpose(0, 2, 1, 3)
    vf = v.astype(jnp.float32).transpose(0, 2, 1, 3)
    qb = q.astype(jnp.float32).transpose(0, 2, 1, 3).reshape(B, H, nq, Q_BLOCK, dq).transpose(2, 0, 1, 3, 4)

    def block(qi):
        s = jnp.einsum("bhqd,bhkd->bhqk", qi, kf) * scale
        return jnp.einsum("bhqk,bhkd->bhqd", jax.nn.softmax(s, axis=-1), vf)

    o = lax.map(block, qb)
    return o.transpose(1, 0, 3, 2, 4).reshape(B, S, H * dv)

def diff_attention(q, k, v, lam):
    B, S, H, _, dh = q.shape
    dv = v.shape[-1]
    nq = S // Q_BLOCK
    kf = k.astype(jnp.float32).transpose(0, 2, 3, 1, 4)
    vf = v.astype(jnp.float32).transpose(0, 2, 1, 3)
    qb = q.astype(jnp.float32).transpose(0, 2, 3, 1, 4).reshape(B, H, 2, nq, Q_BLOCK, dh).transpose(3, 0, 1, 2, 4, 5)

    def block(qi):
        s = jnp.einsum("bhcqd,bhckd->bhcqk", qi, kf) * (dh ** -0.5)
        a = jax.nn.softmax(s, axis=-1)
        return jnp.einsum("bhqk,bhkd->bhqd", a[:, :, 0] - lam * a[:, :, 1], vf)

    o = lax.map(block, qb)
    return o.transpose(1, 0, 3, 2, 4).reshape(B, S, H, dv)

def mixer_ab(x, cos_a, sin_a, cos_b, sin_b, w_in, q_norm, w_q_up, kv_norm, w_kv_up, w_out):
    B, S, _ = x.shape
    h = x @ w_in
    o1 = A_WIDTH
    o2 = 2 * A_WIDTH
    o3 = 3 * A_WIDTH
    o4 = o3 + B_Q_LORA
    o5 = o4 + B_KV_LORA
    shape_a = (B, S, A_HEADS, A_HEAD_DIM)
    qa = apply_rope(h[..., :o1].reshape(shape_a), cos_a, sin_a, A_ROT)
    ka = apply_rope(h[..., o1:o2].reshape(shape_a), cos_a, sin_a, A_ROT)
    va = h[..., o2:o3].reshape(shape_a)
    out_a = dilated_mixture(qa, ka, va).astype(x.dtype)
    cq = rms_norm(h[..., o3:o4], q_norm, RMS_EPS)
    qb = (cq @ w_q_up).reshape(B, S, B_HEADS, B_NOPE + B_ROPE)
    q_pe = apply_rope(qb[..., B_NOPE:], cos_b, sin_b, B_ROPE)
    qb = jnp.concatenate([qb[..., :B_NOPE], q_pe], axis=-1)
    ckv = rms_norm(h[..., o4:o5], kv_norm, RMS_EPS)
    kv = (ckv @ w_kv_up).reshape(B, S, B_HEADS, B_NOPE + B_V)
    k_pe = apply_rope(h[..., o5:].reshape(B, S, 1, B_ROPE), cos_b, sin_b, B_ROPE)
    kb = jnp.concatenate([kv[..., :B_NOPE], jnp.broadcast_to(k_pe, (B, S, B_HEADS, B_ROPE))], axis=-1)
    vb = kv[..., B_NOPE:]
    out_b = dense_attention(qb, kb, vb, (B_NOPE + B_ROPE) ** -0.5).astype(x.dtype)
    return jnp.concatenate([out_a, out_b], axis=-1) @ w_out

def mixer_c(x, cos_c, sin_c, w_qkv, lam_params, subln, w_out, lambda_init):
    B, S, _ = x.shape
    h = x @ w_qkv
    q = apply_rope(h[..., :C_QK].reshape(B, S, C_HEADS, 2, C_HEAD_DIM), cos_c, sin_c, C_ROT)
    k = apply_rope(h[..., C_QK:2 * C_QK].reshape(B, S, C_HEADS, 2, C_HEAD_DIM), cos_c, sin_c, C_ROT)
    v = h[..., 2 * C_QK:].reshape(B, S, C_HEADS, 2 * C_HEAD_DIM)
    lp = lam_params.astype(jnp.float32)
    lam = jnp.exp(jnp.sum(lp[0] * lp[1])) - jnp.exp(jnp.sum(lp[2] * lp[3])) + lambda_init
    o = diff_attention(q, k, v, lam)
    o = rms_norm(o, subln, LN_EPS) * (1.0 - lambda_init)
    return o.reshape(B, S, C_MIX).astype(x.dtype) @ w_out

def conv_ffn(x, w_gate, w_up, conv_w, conv_b, w_down):
    S = x.shape[1]
    a = x @ w_gate
    u = x @ w_up
    pad = CONV_WIDTH // 2
    ap = jnp.pad(a, ((0, 0), (pad, pad), (0, 0)))
    c = conv_b
    for j in range(CONV_WIDTH):
        c = c + conv_w[j] * ap[:, j:j + S]
    return (jax.nn.gelu(c) * u) @ w_down

def first_inputs(seed: int = 0) -> dict:
    key = jax.random.key(seed)
    ks = jax.random.split(key, 24)
    f32 = jnp.float32

    def w(k, shape, fan_in, gain=1.0):
        return jax.random.normal(k, shape, f32) * (gain * fan_in ** -0.5)

    def gain_init(k, shape):
        return 1.0 + 0.02 * jax.random.normal(k, shape, f32)

    def bias_init(k, shape):
        return 0.02 * jax.random.normal(k, shape, f32)

    x = jax.random.normal(ks[0], (BATCH, SEQ, D_MODEL), f32)
    p = jax.random.normal(ks[1], (DEPTH, BATCH, SEQ, PLE_DIM), f32)
    positions = (jnp.arange(SEQ, dtype=jnp.int32)[None, :]
                 + jax.random.randint(ks[2], (BATCH, 1), 0, MAX_POS_OFFSET, dtype=jnp.int32))
    return {
        "x": x,
        "p": p,
        "positions": positions,
        "ab_w_in": w(ks[3], (N_AB, D_MODEL, AB_IN), D_MODEL),
        "ab_q_norm": gain_init(ks[4], (N_AB, B_Q_LORA)),
        "ab_w_q_up": w(ks[5], (N_AB, B_Q_LORA, B_HEADS * (B_NOPE + B_ROPE)), B_Q_LORA),
        "ab_kv_norm": gain_init(ks[6], (N_AB, B_KV_LORA)),
        "ab_w_kv_up": w(ks[7], (N_AB, B_KV_LORA, B_HEADS * (B_NOPE + B_V)), B_KV_LORA),
        "ab_w_out": w(ks[8], (N_AB, AB_MIX, D_MODEL), AB_MIX, BETA),
        "c_w_qkv": w(ks[9], (N_C, D_MODEL, 2 * C_QK + C_MIX), D_MODEL),
        "c_lambda": 0.1 * jax.random.normal(ks[10], (N_C, 4, C_HEAD_DIM), f32),
        "c_subln": gain_init(ks[11], (N_C, 2 * C_HEAD_DIM)),
        "c_w_out": w(ks[12], (N_C, C_MIX, D_MODEL), C_MIX, BETA),
        "ln_mix_g": gain_init(ks[13], (DEPTH, D_MODEL)),
        "ln_mix_b": bias_init(ks[14], (DEPTH, D_MODEL)),
        "ffn_w_gate": w(ks[15], (DEPTH, D_MODEL, D_FF), D_MODEL),
        "ffn_w_up": w(ks[16], (DEPTH, D_MODEL, D_FF), D_MODEL),
        "ffn_conv_w": w(ks[17], (DEPTH, CONV_WIDTH, D_FF), CONV_WIDTH),
        "ffn_conv_b": bias_init(ks[18], (DEPTH, D_FF)),
        "ffn_w_down": w(ks[19], (DEPTH, D_FF, D_MODEL), D_FF, BETA),
        "ln_ffn_g": gain_init(ks[20], (DEPTH, D_MODEL)),
        "ln_ffn_b": bias_init(ks[21], (DEPTH, D_MODEL)),
        "ple_w_gate": w(ks[22], (DEPTH, D_MODEL, D_MODEL), D_MODEL),
        "ple_w_proj": w(ks[23], (DEPTH, PLE_DIM, D_MODEL), PLE_DIM),
    }

def first_block(x, p, positions, ab_w_in, ab_q_norm, ab_w_q_up, ab_kv_norm, ab_w_kv_up, ab_w_out,
              c_w_qkv, c_lambda, c_subln, c_w_out, ln_mix_g, ln_mix_b, ffn_w_gate, ffn_w_up,
              ffn_conv_w, ffn_conv_b, ffn_w_down, ln_ffn_g, ln_ffn_b, ple_w_gate, ple_w_proj):
    cos_a, sin_a = rope_tables(positions, A_ROT)
    cos_b, sin_b = rope_tables(positions, B_ROPE)
    cos_c, sin_c = rope_tables(positions, C_ROT)
    for i in range(DEPTH):
        j = i // 2
        if i % 2 == 0:
            y = mixer_ab(x, cos_a, sin_a, cos_b, sin_b, ab_w_in[j], ab_q_norm[j], ab_w_q_up[j],
                         ab_kv_norm[j], ab_w_kv_up[j], ab_w_out[j])
        else:
            lambda_init = 0.8 - 0.6 * math.exp(-0.3 * i)
            y = mixer_c(x, cos_c, sin_c, c_w_qkv[j], c_lambda[j], c_subln[j], c_w_out[j], lambda_init)
        x = layer_norm(ALPHA * x + y, ln_mix_g[i], ln_mix_b[i])
        f = conv_ffn(x, ffn_w_gate[i], ffn_w_up[i], ffn_conv_w[i], ffn_conv_b[i], ffn_w_down[i])
        x = layer_norm(ALPHA * x + f, ln_ffn_g[i], ln_ffn_b[i])
        x = x + jax.nn.sigmoid(x @ ple_w_gate[i]) * (p[i] @ ple_w_proj[i])
    return x


N_BRANCH = 4
BRANCH_WIDTH = D_MODEL // N_BRANCH
HEAD_DIM = 64
NSA_HEADS = BRANCH_WIDTH // HEAD_DIM
NSA_CMP_LEN = 32
NSA_CMP_STRIDE = 16
NSA_CMP_HIDDEN = 2 * HEAD_DIM
NSA_SEL_LEN = 64
NSA_N_SEL = 16
NSA_WINDOW = 512
NSA_FORCE_BONUS = 1.0e4
POOL_WINDOWS = (2, 4, 8, 16)
POOL_GROUP = BRANCH_WIDTH // len(POOL_WINDOWS)
FOX_HEADS = BRANCH_WIDTH // HEAD_DIM
ROPE_DIM = HEAD_DIM // 4
NORM_EPS = 1e-6
MASK_VALUE = -1e30

IN_SPLITS = (
    NSA_HEADS * HEAD_DIM,
    6 * HEAD_DIM,
    3 * NSA_HEADS,
    BRANCH_WIDTH,
    3 * BRANCH_WIDTH,
    3 * BRANCH_WIDTH,
    FOX_HEADS,
    N_BRANCH * BRANCH_WIDTH,
    N_BRANCH * D_MODEL,
)
D_IN = sum(IN_SPLITS)


def rmsnorm(x, g):
    xf = x.astype(jnp.float32)
    y = xf * lax.rsqrt(jnp.mean(xf * xf, axis=-1, keepdims=True) + NORM_EPS)
    return (y * g.astype(jnp.float32)).astype(x.dtype)

def rope(x, pos):
    half = ROPE_DIM // 2
    inv = ROPE_THETA ** (-jnp.arange(half, dtype=jnp.float32) / half)
    ang = pos.astype(jnp.float32)[:, None] * inv[None, :]
    cos = jnp.cos(ang)[None, :, None, :].astype(x.dtype)
    sin = jnp.sin(ang)[None, :, None, :].astype(x.dtype)
    x1, x2, rest = x[..., :half], x[..., half:ROPE_DIM], x[..., ROPE_DIM:]
    return jnp.concatenate([x1 * cos - x2 * sin, x2 * cos + x1 * sin, rest], axis=-1)

def masked_softmax(s, mask):
    s = jnp.where(mask, s.astype(jnp.float32), MASK_VALUE)
    p = jax.nn.softmax(s, axis=-1)
    return jnp.where(mask, p, 0.0)

def to_blocks(a):
    B, T = a.shape[:2]
    a = a.reshape((B, T // Q_BLOCK, Q_BLOCK) + a.shape[2:])
    return jnp.moveaxis(a, 1, 0)

def from_blocks(a):
    a = jnp.moveaxis(a, 0, 1)
    return a.reshape((a.shape[0], a.shape[1] * a.shape[2]) + a.shape[3:])

def nsa_compress(k, pos_emb, w1, b1, w2, b2):
    B, T, hd = k.shape
    nc = (T - NSA_CMP_LEN) // NSA_CMP_STRIDE + 1
    idx = np.arange(nc)[:, None] * NSA_CMP_STRIDE + np.arange(NSA_CMP_LEN)[None, :]
    blocks = k[:, idx] + pos_emb
    flat = blocks.reshape(B, nc, NSA_CMP_LEN * hd)
    return jax.nn.silu(flat @ w1 + b1) @ w2 + b2

def nsa_mixer(q, kv, gate_logits, cmp_pos, cmp_w1, cmp_b1, cmp_w2, cmp_b2):
    B, T = q.shape[:2]
    pos = jnp.arange(T)
    q = rope(q.reshape(B, T, NSA_HEADS, HEAD_DIM), pos) * (HEAD_DIM ** -0.5)
    k_c, v_c, k_s, v_s, k_w, v_w = jnp.split(kv, 6, axis=-1)
    k_s = rope(k_s[:, :, None], pos)[:, :, 0]
    k_w = rope(k_w[:, :, None], pos)[:, :, 0]
    kc = nsa_compress(k_c, cmp_pos[0], cmp_w1[0], cmp_b1[0], cmp_w2[0], cmp_b2[0])
    vc = nsa_compress(v_c, cmp_pos[1], cmp_w1[1], cmp_b1[1], cmp_w2[1], cmp_b2[1])
    nc = kc.shape[1]
    cmp_end_np = np.arange(nc) * NSA_CMP_STRIDE + NSA_CMP_LEN - 1
    cmp_end = jnp.asarray(cmp_end_np)
    kc = rope(kc[:, :, None], cmp_end)[:, :, 0]
    n_blk = T // NSA_SEL_LEN
    n_sel = min(NSA_N_SEL, n_blk)
    ci = np.arange(nc)[:, None] * NSA_CMP_STRIDE
    sj = np.arange(n_blk)[None, :] * NSA_SEL_LEN
    overlap = jnp.asarray((ci < sj + NSA_SEL_LEN) & (ci + NSA_CMP_LEN > sj), jnp.float32)
    k_blk = k_s.reshape(B, n_blk, NSA_SEL_LEN, HEAD_DIM)
    v_blk = v_s.reshape(B, n_blk, NSA_SEL_LEN, HEAD_DIM)
    pad = ((0, 0), (NSA_WINDOW, 0), (0, 0))
    k_wp, v_wp = jnp.pad(k_w, pad), jnp.pad(v_w, pad)
    blk_ids = jnp.arange(n_blk)

    def one_block(args):
        qi, q_blk = args
        t = qi * Q_BLOCK + jnp.arange(Q_BLOCK)
        s = jnp.einsum('bqhd,bnd->bhqn', q_blk, kc)
        p_c = masked_softmax(s, (cmp_end[None, :] <= t[:, None])[None, None])
        o_cmp = jnp.einsum('bhqn,bnd->bqhd', p_c.astype(vc.dtype), vc)
        imp = jnp.einsum('bhqn,nj->bqj', p_c, overlap)
        jt = (t // NSA_SEL_LEN)[:, None]
        j = blk_ids[None, :]
        forced = (j == 0) | (j == jt) | (j == jt - 1)
        valid = j * NSA_SEL_LEN <= t[:, None]
        imp = jnp.where(valid, jnp.where(forced, imp + NSA_FORCE_BONUS, imp), MASK_VALUE)
        _, sel = lax.top_k(imp, n_sel)
        ks = jax.vmap(lambda kb, ib: kb[ib])(k_blk, sel)
        vs = jax.vmap(lambda vb, ib: vb[ib])(v_blk, sel)
        kpos = sel[..., None] * NSA_SEL_LEN + jnp.arange(NSA_SEL_LEN)
        m_s = (kpos <= t[None, :, None, None]).reshape(B, 1, Q_BLOCK, n_sel * NSA_SEL_LEN)
        s = jnp.einsum('bqhd,bqnkd->bhqnk', q_blk, ks).reshape(B, NSA_HEADS, Q_BLOCK, n_sel * NSA_SEL_LEN)
        p_s = masked_softmax(s, m_s).reshape(B, NSA_HEADS, Q_BLOCK, n_sel, NSA_SEL_LEN)
        o_slc = jnp.einsum('bhqnk,bqnkd->bqhd', p_s.astype(vs.dtype), vs)
        kw = lax.dynamic_slice_in_dim(k_wp, qi * Q_BLOCK, Q_BLOCK + NSA_WINDOW, axis=1)
        vw = lax.dynamic_slice_in_dim(v_wp, qi * Q_BLOCK, Q_BLOCK + NSA_WINDOW, axis=1)
        wpos = qi * Q_BLOCK - NSA_WINDOW + jnp.arange(Q_BLOCK + NSA_WINDOW)
        m_w = (wpos[None, :] <= t[:, None]) & (wpos[None, :] > t[:, None] - NSA_WINDOW) & (wpos[None, :] >= 0)
        s = jnp.einsum('bqhd,bkd->bhqk', q_blk, kw)
        p_w = masked_softmax(s, m_w[None, None])
        o_win = jnp.einsum('bhqk,bkd->bqhd', p_w.astype(vw.dtype), vw)
        return o_cmp, o_slc, o_win

    o_cmp, o_slc, o_win = lax.map(one_block, (jnp.arange(T // Q_BLOCK), to_blocks(q)))
    g = jax.nn.sigmoid(gate_logits.reshape(B, T, 3, NSA_HEADS))[..., None]
    o = (g[:, :, 0] * from_blocks(o_cmp) + g[:, :, 1] * from_blocks(o_slc)
         + g[:, :, 2] * from_blocks(o_win))
    return o.reshape(B, T, NSA_HEADS * HEAD_DIM)

def pool_mixer(u, pool_w, pool_scale):
    B, T, C = u.shape
    cs = jnp.concatenate([jnp.zeros((B, 1, C), jnp.float32),
                          jnp.cumsum(u.astype(jnp.float32), axis=1)], axis=1)
    outs = []
    for gi, w in enumerate(POOL_WINDOWS):
        sl = slice(gi * POOL_GROUP, (gi + 1) * POOL_GROUP)
        csg = cs[..., sl]
        lag = jnp.concatenate([jnp.zeros((B, w - 1, POOL_GROUP), jnp.float32),
                               csg[:, :T + 1 - w]], axis=1)
        cnt = jnp.minimum(jnp.arange(1, T + 1), w).astype(jnp.float32)[None, :, None]
        outs.append(((csg[:, 1:] - lag) / cnt).astype(u.dtype) - u[..., sl])
    pooled = jnp.stack(outs, axis=2)
    mixed = jnp.einsum('btgc,gcd->btgd', pooled, pool_w).reshape(B, T, C)
    return mixed * pool_scale

def conv_mixer(xin, b_gate, c_gate, conv_w):
    T = xin.shape[1]
    u = jnp.pad(c_gate * xin, ((0, 0), (CONV_WIDTH - 1, 0), (0, 0)))
    y = sum(u[:, k:k + T] * conv_w[k] for k in range(CONV_WIDTH))
    return b_gate * y

def fox_mixer(q, k, v, f_logit, f_bias):
    B, T = q.shape[:2]
    q = q.reshape(B, T, FOX_HEADS, HEAD_DIM) * (HEAD_DIM ** -0.5)
    k = k.reshape(B, T, FOX_HEADS, HEAD_DIM)
    v = v.reshape(B, T, FOX_HEADS, HEAD_DIM)
    logf = jax.nn.log_sigmoid(f_logit.astype(jnp.float32) + f_bias.astype(jnp.float32))
    c = jnp.cumsum(logf, axis=1)
    c_keys = jnp.transpose(c, (0, 2, 1))
    kpos = jnp.arange(T)

    def one_block(args):
        qi, q_blk, c_blk = args
        t = qi * Q_BLOCK + jnp.arange(Q_BLOCK)
        s = jnp.einsum('bqhd,bkhd->bhqk', q_blk, k).astype(jnp.float32)
        s = s + jnp.transpose(c_blk, (0, 2, 1))[..., None] - c_keys[:, :, None, :]
        p = masked_softmax(s, (kpos[None, :] <= t[:, None])[None, None])
        return jnp.einsum('bhqk,bkhd->bqhd', p.astype(v.dtype), v)

    o = lax.map(one_block, (jnp.arange(T // Q_BLOCK), to_blocks(q), to_blocks(c)))
    return from_blocks(o).reshape(B, T, FOX_HEADS * HEAD_DIM)

def hybrid_layer(x, norm_g, w_in, fox_f_bias, cmp_pos, cmp_w1, cmp_b1, cmp_w2, cmp_b2,
                 pool_w, pool_scale, conv_w, w_branch, w_out):
    B, T, _ = x.shape
    h = rmsnorm(x, norm_g)
    proj = h @ w_in
    split_at = np.cumsum(IN_SPLITS)[:-1].tolist()
    (nsa_q, nsa_kv, nsa_g, pool_in, conv_in, fox_qkv, fox_f,
     gate_in, merge_in) = jnp.split(proj, split_at, axis=-1)
    o_nsa = nsa_mixer(nsa_q, nsa_kv, nsa_g, cmp_pos, cmp_w1, cmp_b1, cmp_w2, cmp_b2)
    o_pool = pool_mixer(pool_in, pool_w, pool_scale)
    c_x, c_b, c_c = jnp.split(conv_in, 3, axis=-1)
    o_conv = conv_mixer(c_x, c_b, c_c, conv_w)
    f_q, f_k, f_v = jnp.split(fox_qkv, 3, axis=-1)
    o_fox = fox_mixer(f_q, f_k, f_v, fox_f, fox_f_bias)
    gates = gate_in.reshape(B, T, N_BRANCH, BRANCH_WIDTH)
    merge = merge_in.reshape(B, T, N_BRANCH, D_MODEL)
    acc = None
    for i, o in enumerate((o_nsa, o_pool, o_conv, o_fox)):
        branch = (o * jax.nn.silu(gates[:, :, i])) @ w_branch[i]
        term = jax.nn.sigmoid(merge[:, :, i]) * branch
        acc = term if acc is None else acc + term
    return x + acc @ w_out

def second_inputs(seed: int = 0) -> dict:
    key = jax.random.key(seed)
    ks = jax.random.split(key, 20)
    f32 = jnp.float32
    nrm = lambda k, shape, scale: jax.random.normal(k, shape, f32) * scale
    cmp_in = NSA_CMP_LEN * HEAD_DIM
    return {
        "x": nrm(ks[0], (BATCH, SEQ, D_MODEL), 1.0),
        "norm_g": 1.0 + nrm(ks[1], (DEPTH, D_MODEL), 0.05),
        "w_in": nrm(ks[2], (DEPTH, D_MODEL, D_IN), D_MODEL ** -0.5),
        "fox_f_bias": 3.0 + nrm(ks[3], (DEPTH, FOX_HEADS), 0.5),
        "cmp_pos": nrm(ks[4], (DEPTH, 2, NSA_CMP_LEN, HEAD_DIM), 0.1),
        "cmp_w1": nrm(ks[5], (DEPTH, 2, cmp_in, NSA_CMP_HIDDEN), cmp_in ** -0.5),
        "cmp_b1": nrm(ks[6], (DEPTH, 2, NSA_CMP_HIDDEN), 0.02),
        "cmp_w2": nrm(ks[7], (DEPTH, 2, NSA_CMP_HIDDEN, HEAD_DIM), NSA_CMP_HIDDEN ** -0.5),
        "cmp_b2": nrm(ks[8], (DEPTH, 2, HEAD_DIM), 0.02),
        "pool_w": nrm(ks[9], (DEPTH, len(POOL_WINDOWS), POOL_GROUP, POOL_GROUP), POOL_GROUP ** -0.5),
        "pool_scale": 1.0 + nrm(ks[10], (DEPTH, BRANCH_WIDTH), 0.1),
        "conv_w": nrm(ks[11], (DEPTH, CONV_WIDTH, BRANCH_WIDTH), CONV_WIDTH ** -0.5),
        "w_branch": nrm(ks[12], (DEPTH, N_BRANCH, BRANCH_WIDTH, D_MODEL), BRANCH_WIDTH ** -0.5),
        "w_out": nrm(ks[13], (DEPTH, D_MODEL, D_MODEL), D_MODEL ** -0.5),
        "final_norm_g": 1.0 + nrm(ks[14], (D_MODEL,), 0.05),
    }

def second_block(x, norm_g, w_in, fox_f_bias, cmp_pos, cmp_w1, cmp_b1, cmp_w2, cmp_b2,
              pool_w, pool_scale, conv_w, w_branch, w_out, final_norm_g):
    for l in range(DEPTH):
        x = hybrid_layer(x, norm_g[l], w_in[l], fox_f_bias[l], cmp_pos[l], cmp_w1[l],
                         cmp_b1[l], cmp_w2[l], cmp_b2[l], pool_w[l], pool_scale[l],
                         conv_w[l], w_branch[l], w_out[l])
    return rmsnorm(x, final_norm_g)


def setup_inputs(seed=0):
    out = dict(first_inputs(seed))
    for name, value in second_inputs(seed + 1).items():
        if name != "x":
            out[name + "_2"] = value
    return out


def reference(
    x, p, positions, ab_w_in, ab_q_norm, ab_w_q_up, ab_kv_norm, ab_w_kv_up, ab_w_out, c_w_qkv,
    c_lambda, c_subln, c_w_out, ln_mix_g, ln_mix_b, ffn_w_gate, ffn_w_up, ffn_conv_w,
    ffn_conv_b, ffn_w_down, ln_ffn_g, ln_ffn_b, ple_w_gate, ple_w_proj, norm_g_2, w_in_2,
    fox_f_bias_2, cmp_pos_2, cmp_w1_2, cmp_b1_2, cmp_w2_2, cmp_b2_2, pool_w_2, pool_scale_2,
    conv_w_2, w_branch_2, w_out_2, final_norm_g_2,
):
    x = first_block(
        x, p, positions, ab_w_in, ab_q_norm, ab_w_q_up, ab_kv_norm, ab_w_kv_up, ab_w_out,
        c_w_qkv, c_lambda, c_subln, c_w_out, ln_mix_g, ln_mix_b, ffn_w_gate, ffn_w_up,
        ffn_conv_w, ffn_conv_b, ffn_w_down, ln_ffn_g, ln_ffn_b, ple_w_gate, ple_w_proj,
    )
    return second_block(
        x, norm_g_2, w_in_2, fox_f_bias_2, cmp_pos_2, cmp_w1_2, cmp_b1_2, cmp_w2_2, cmp_b2_2,
        pool_w_2, pool_scale_2, conv_w_2, w_branch_2, w_out_2, final_norm_g_2,
    )


_drawn_inputs = setup_inputs


def setup_inputs(seed=0):
    import zlib

    import numpy as np

    out = dict(_drawn_inputs(seed))
    spreads = {}
    factors = {'ab_q_norm': 8.0,
     'ab_kv_norm': 8.0,
     'c_subln': 8.0,
     'ffn_conv_b': 7.645,
     'cmp_pos_2': 5.358,
     'cmp_b1_2': 21.996,
     'cmp_b2_2': 8.0}
    for name, (base, spread) in spreads.items():
        noise = np.random.default_rng([zlib.crc32(name.encode()), seed]).standard_normal(out[name].shape)
        drawn = base * np.exp(spread * noise) if base else spread * noise
        out[name] = __import__('jax').numpy.asarray(drawn.astype(out[name].dtype))
    for name, factor in factors.items():
        out[name] = (out[name] * factor).astype(out[name].dtype)
    return out
```

```python
import math
from contextlib import ExitStack

import numpy as np

import concourse.bass as bass
from concourse import mybir

F32 = mybir.dt.float32
BF16 = mybir.dt.bfloat16
I32 = mybir.dt.int32
ALU = mybir.AluOpType
ACT = mybir.ActivationFunctionType
AX_X = mybir.AxisListType.X

P = 128
S = 512
D = 1024
KD = D // P
ST = S // P
DEPTH = 2
HD = 64
A_HEADS = 8
B_HEADS, B_NOPE, B_ROPE, B_QK = 8, 64, 32, 96
Q_LORA, KV_LORA = 384, 256
C_HEADS = 8
FF = 256 * math.ceil(8 * D / 3 / 256)
KF = FF // P
PLE = 256
LN_EPS, RMS_EPS = 1e-5, 1e-6
ALPHA = (2 * DEPTH) ** 0.25
LAMBDA_INIT = 0.8 - 0.6 * math.exp(-0.3)
ROPE_THETA, MASK = 500000.0, -1e30
N_BRANCH, BW = 4, 256
CMP_N, CMP_LEN, CMP_STRIDE = 32, 32, 16
PAD = 16
RING = 4
BLK = 1024


class Tally:

    def __init__(self, keys=()):
        self.value = {}
        for key in keys:
            self.add(key)

    def add(self, key):
        assert key not in self.value, key
        self.value[key] = len(self.value) + 1

    def __getitem__(self, key):
        return self.value[key]


def block_plan():
    keys = []
    keys += [("vA", i) for i in range(4)] + [("qkA", t) for t in range(8)]
    keys += [("lat", t) for t in range(5)] + [("kpe", 0)]
    keys += [("qup", i) for i in range(3)] + [("kvk", 0), ("kvv", 0)]
    for layer in range(DEPTH):
        if layer == 1:
            keys += [("vC", i) for i in range(8)] + [("qkC", t) for t in range(16)]
        keys += [("mixout", layer, n) for n in range(KD)]
        for f in range(KF):
            keys += [("gate", layer, f), ("up", layer, f)]
        keys += [("down", layer, h, i) for h in range(2) for i in range(KF // 2)]
        for half in range(2):
            keys += [("pleproj", layer, half)] + [("plegate", layer, half * 4 + n) for n in range(4)]
    for layer in range(DEPTH):
        keys += [("small", layer), ("kcvc", layer), ("vsvw", layer), ("ks", layer), ("kw", layer)]
        keys += [("nq", layer, t) for t in range(2)] + [("w1", layer, i) for i in range(4)]
        keys += [("fq", layer, t) for t in range(2)] + [("fk", layer, t) for t in range(2)]
        keys += [("fv", layer, t) for t in range(2)] + [("pool", layer, t) for t in range(2)]
        keys += [("conv", layer, t) for t in range(6)] + [("sgate", layer, t) for t in range(8)]
        for n in range(KD):
            keys += [("merge", layer, n, i) for i in range(N_BRANCH)] + [("branch", layer, n)]
        keys += [("out2", layer, n) for n in range(KD)]
    return keys


BLOCKS = block_plan()
AT = {key: n for n, key in enumerate(BLOCKS)}

COLS = {}
_at = 0
for _name, _width in [
    ("q_norm", 3), ("kv_norm", 2), ("subln", 1), ("ln_mix_g", 16), ("ln_mix_b", 16), ("conv_w", 2 * 3 * KF),
    ("conv_b", 2 * KF), ("ln_ffn_g", 16), ("ln_ffn_b", 16), ("norm2_g", 16), ("fox_bias", 2), ("cmp_b1", 4),
    ("cmp_b2k", 2), ("pool_scale", 4), ("conv2_w", 12), ("final_g", 8), ("inv_a", 1), ("inv_b", 1),
    ("eps_ln", 1), ("eps_rms", 1), ("cq_mul", 1), ("cq_add", 1), ("ck_mul", 1), ("ck_add", 1),
]:
    COLS[_name] = _at
    _at += _width
NCOLS = _at

TABS = {}
_at = 0
for _name, _width in [
    ("ident", P), ("ones", P), ("perm_a", P), ("perm_b", P), ("log_count", ST * S), ("cmp_bias", S), ("tri", P), ("cos2", S), ("sin2", S),
    ("cos2c", CMP_N), ("sin2c", CMP_N), ("inv_count", 2 * S), ("cmp_mask", S),
    ("sel", 6 * P), ("ones_bd", 2 * P),
]:
    TABS[_name] = _at
    _at += _width
NTABS = _at


def _tile(w):
    k, n = w.shape
    return w.reshape(k // P, P, n).transpose(1, 0, 2).reshape(P, -1)


def _column(v):
    return v.reshape(-1, P).T


def weight_stream(a):
    w_in, w_qkv = a["ab_w_in"][0], a["c_w_qkv"][0]
    o3 = 3 * A_HEADS * HD
    made = np.zeros((len(BLOCKS), P, BLK), np.float32)
    split2 = np.cumsum([256, 384, 12, 256, 768, 768, 4, 1024, 4096])

    def put(n, w):
        made[n, :, :w.shape[1]] = w

    for n, key in enumerate(BLOCKS):
        kind, at = key[0], key[1:]
        if kind == "vA":
            put(n, _tile(w_in[256 * at[0]:256 * at[0] + 256, 1024:1536]))
        elif kind == "qkA":
            put(n, _tile(w_in[:, P * at[0]:P * at[0] + P]))
        elif kind == "lat":
            put(n, _tile(w_in[:, o3 + P * at[0]:o3 + P * at[0] + P]))
        elif kind == "kpe":
            w = np.zeros((D, B_QK), np.float32)
            w[:, B_NOPE:] = w_in[:, o3 + Q_LORA + KV_LORA:]
            put(n, _tile(w))
        elif kind == "qup":
            heads = range(3 * at[0], min(3 * at[0] + 3, B_HEADS))
            put(n, np.concatenate([_tile(a["ab_w_q_up"][0][:, B_QK * h:B_QK * h + B_QK]) for h in heads], 1))
        elif kind == "kvk":
            w = a["ab_w_kv_up"][0].reshape(KV_LORA, B_HEADS // 2, 2, 2, HD)[:, :, :, 0]
            put(n, np.concatenate([_tile(w[:, j].reshape(KV_LORA, P)) for j in range(B_HEADS // 2)], 1))
        elif kind == "kvv":
            put(n, _tile(a["ab_w_kv_up"][0].reshape(KV_LORA, B_HEADS, 2, HD)[:, :, 1].reshape(KV_LORA, -1)))
        elif kind == "vC":
            half, i = divmod(at[0], 4)
            put(n, _tile(w_qkv[256 * i:256 * i + 256, 2048 + S * half:2048 + S * half + S]))
        elif kind == "qkC":
            put(n, _tile(w_qkv[:, P * at[0]:P * at[0] + P]))
        elif kind == "mixout":
            put(n, _tile((a["ab_w_out"][0], a["c_w_out"][0])[at[0]][:, P * at[1]:P * at[1] + P]))
        elif kind in ("gate", "up"):
            put(n, _tile(a["ffn_w_" + kind][at[0]][:, P * at[1]:P * at[1] + P]))
        elif kind == "down":
            layer, half, i = at
            put(n, _tile(a["ffn_w_down"][layer][256 * i:256 * i + 256, S * half:S * half + S]))
        elif kind == "plegate":
            put(n, _tile(a["ple_w_gate"][at[0]][:, P * at[1]:P * at[1] + P]))
        elif kind == "pleproj":
            put(n, _tile(a["ple_w_proj"][at[0]][:, S * at[1]:S * at[1] + S]))
        elif kind == "w1":
            w = a["cmp_w1_2"][at[0]].reshape(2, CMP_LEN, HD, P)[:, 8 * at[1]:8 * at[1] + 8]
            put(n, w.transpose(0, 2, 1, 3).reshape(P, BLK))
        elif kind == "branch":
            w = a["w_branch_2"][at[0]][:, :, P * at[1]:P * at[1] + P]
            put(n, _tile(w.reshape(N_BRANCH * BW, P)))
        elif kind == "out2":
            put(n, _tile(a["w_out_2"][at[0]][:, P * at[1]:P * at[1] + P]))
        else:
            nq, kv, ng, pool, conv, fox, ff, gate, merge = np.split(a["w_in_2"][at[0]], split2[:-1], axis=1)
            if kind == "small":
                w = np.zeros((D, P), np.float32)
                w[:, 0::32], w[:, 1::32], w[:, 8:20] = ff, ff, ng
            elif kind == "kcvc":
                w = kv[:, 0:P]
            elif kind == "vsvw":
                w = np.concatenate([kv[:, 192:256], kv[:, 320:384]], 1)
            elif kind == "ks":
                w = np.concatenate([kv[:, 128:192]] * 2, 1)
            elif kind == "kw":
                w = np.concatenate([kv[:, 256:320]] * 2, 1)
            elif kind == "nq":
                w = nq[:, P * at[1]:P * at[1] + P]
            elif kind == "fq":
                w = fox[:, P * at[1]:P * at[1] + P]
            elif kind == "fk":
                w = fox[:, 256 + P * at[1]:256 + P * at[1] + P]
            elif kind == "fv":
                w = fox[S * at[1]:S * at[1] + S, 512:768]
            elif kind == "pool":
                w = pool[:, P * at[1]:P * at[1] + P]
            elif kind == "conv":
                w = conv[:, P * at[1]:P * at[1] + P]
            elif kind == "sgate":
                w = gate[:, P * at[1]:P * at[1] + P]
            elif kind == "merge":
                lo = D * at[2] + P * at[1]
                w = merge[:, lo:lo + P]
            put(n, _tile(w))
    return made


def column_pack(a):
    made = np.zeros((P, NCOLS), np.float32)

    def put(name, v):
        made[:, COLS[name]:COLS[name] + v.shape[1]] = v

    put("q_norm", _column(a["ab_q_norm"][0]))
    put("kv_norm", _column(a["ab_kv_norm"][0]))
    put("subln", _column(a["c_subln"][0]))
    for name in ("ln_mix_g", "ln_mix_b", "ln_ffn_g", "ln_ffn_b"):
        put(name, _column(a[name].reshape(-1)))
    put("conv_w", _column(a["ffn_conv_w"].reshape(-1)))
    put("conv_b", _column(a["ffn_conv_b"].reshape(-1)))
    put("norm2_g", _column(a["norm_g_2"].reshape(-1)))
    bias = np.zeros((P, DEPTH), np.float32)
    bias[0::32], bias[1::32] = a["fox_f_bias_2"].T, a["fox_f_bias_2"].T
    put("fox_bias", bias)
    put("cmp_b1", _column(a["cmp_b1_2"].reshape(-1)))
    put("cmp_b2k", np.concatenate([a["cmp_b2_2"][:, 0].T] * 2, 0))
    put("pool_scale", _column(a["pool_scale_2"].reshape(-1)))
    put("conv2_w", _column(a["conv_w_2"].reshape(-1)))
    put("final_g", _column(a["final_norm_g_2"]))
    for name, rot, width in (("inv_a", HD // 4, HD), ("inv_b", B_ROPE, B_QK)):
        inv = (np.float32(1.0) / np.float32(ROPE_THETA) ** (np.arange(0, rot, 2, dtype=np.float32) / np.float32(rot)))
        col = np.zeros(P, np.float32)
        for lo in ((0, HD) if name == "inv_a" else (B_NOPE,)):
            col[lo:lo + rot] = np.concatenate([inv, inv])
        put(name, col[:, None])
    put("eps_ln", np.full((P, 1), LN_EPS, np.float32))
    put("eps_rms", np.full((P, 1), RMS_EPS, np.float32))
    for h in range(4):
        made[32 * h, COLS["cq_mul"]] = 1.0
        made[32 * h + 1, COLS["cq_add"]] = 1.0
        made[32 * h, COLS["ck_add"]] = 1.0
        made[32 * h + 1, COLS["ck_mul"]] = -1.0
    return made


def table_pack():
    made = np.zeros((P, NTABS), np.float32)

    def put(name, v):
        made[:v.shape[0], TABS[name]:TABS[name] + v.shape[1]] = v

    def swap(lo, half, m):
        for i in range(half):
            m[lo + half + i, lo + i] = -1.0
            m[lo + i, lo + half + i] = 1.0

    put("ident", np.eye(P, dtype=np.float32))
    put("ones", np.ones((P, P), np.float32))
    perm = np.zeros((P, P), np.float32)
    swap(0, 8, perm)
    swap(HD, 8, perm)
    put("perm_a", perm)
    perm = np.zeros((P, P), np.float32)
    swap(B_NOPE, 16, perm)
    put("perm_b", perm)
    i, j = np.arange(S)[:, None], np.arange(S)[None, :]
    count = np.zeros((S, S))
    for window, dilation in ((128, 1), (512, 4), (2048, 16)):
        side = window // (2 * dilation)
        count += ((i - j) % dilation == 0) & (np.abs(i - j) <= side * dilation)
    bias = np.where(count > 0, np.log(np.maximum(count, 1)), MASK).astype(np.float32)
    put("log_count", bias.reshape(ST, P, S).transpose(1, 0, 2).reshape(P, -1))
    half = HD // 8
    inv = np.float32(ROPE_THETA) ** (-np.arange(half, dtype=np.float32) / np.float32(half))
    full = np.zeros(P, np.float32)
    for lo in (0, HD):
        full[lo:lo + 2 * half] = np.concatenate([inv, inv])
    for tag, pos in (("", np.arange(S)), ("c", np.arange(CMP_N) * CMP_STRIDE + CMP_LEN - 1)):
        ang = (pos.astype(np.float32)[None, :] * full[:, None]).astype(np.float64)
        put("cos2" + tag, np.cos(ang).astype(np.float32))
        put("sin2" + tag, np.sin(ang).astype(np.float32))
    inv_count = np.zeros((P, 2, S), np.float32)
    for g, w in enumerate((2, 4, 8, 16)):
        inv_count[64 * (g % 2):64 * (g % 2) + 64, g // 2] = 1.0 / np.minimum(np.arange(1, S + 1), w)
    put("inv_count", inv_count.reshape(P, -1))
    n = np.arange(CMP_N)
    end = n * CMP_STRIDE + CMP_LEN - 1
    seen = (end[None, :] <= np.arange(S)[:, None]) & (n < CMP_N - 1)[None, :]
    put("cmp_mask", np.tile(seen.T, (4, 1)).astype(np.float32))
    bias = np.where(seen, 0.0, MASK).astype(np.float32).reshape(ST, P, 1, CMP_N)
    put("cmp_bias", np.broadcast_to(bias, (ST, P, 4, CMP_N)).transpose(1, 0, 2, 3).reshape(P, -1))
    put("tri", np.where(np.arange(P)[None, :] <= np.arange(P)[:, None], 0.0, MASK).astype(np.float32))
    sel = np.zeros((P, 3, 2, P), np.float32)
    for b in range(3):
        for h in range(4):
            sel[8 + 4 * b + h, b, h // 2, 64 * (h % 2):64 * (h % 2) + 64] = 1.0
    put("sel", sel.reshape(P, -1))
    bd = np.zeros((P, 2, P), np.float32)
    for h in range(4):
        bd[32 * h:32 * h + 32, h // 2, 64 * (h % 2):64 * (h % 2) + 64] = 1.0
    put("ones_bd", bd.reshape(P, -1))
    return made


def small_weights(a):
    made = np.zeros((P, DEPTH, 320), np.float32)
    for l in range(DEPTH):
        made[:, l, 0:64] = made[:, l, 64:128] = a["cmp_w2_2"][l, 0]
        made[:, l, 128:192] = a["cmp_w2_2"][l, 1]
        for g in range(4):
            made[64 * (g % 2):64 * (g % 2) + 64, l, 192 + 64 * (g // 2):256 + 64 * (g // 2)] = a["pool_w_2"][l, g]
    return made.reshape(P, -1)


def host_layout(a):
    cmp_pos = a["cmp_pos_2"].transpose(1, 3, 0, 2).reshape(P, DEPTH * CMP_LEN)
    b2v = np.broadcast_to(a["cmp_b2_2"][:, 1].reshape(1, -1), (P, DEPTH * HD))
    c = np.ascontiguousarray
    return {
        "weights": weight_stream(a),
        "x_t": c(_tile(c(a["x"][0].T))),
        "p_t": c(np.concatenate([_tile(c(a["p"][l, 0].T)) for l in range(DEPTH)], 1)),
        "positions": c(np.broadcast_to(a["positions"], (P, S))),
        "columns": column_pack(a),
        "tables": table_pack(),
        "small_w": small_weights(a),
        "cmp_pos": c(cmp_pos),
        "b2v": c(b2v),
        "lam": c(np.broadcast_to(a["c_lambda"].reshape(1, -1), (P, 4 * HD))),
    }


def attention_units():
    units = [("A", h) for h in range(A_HEADS)] + [("B", h) for h in range(B_HEADS)]
    units += [("C", h) for h in range(C_HEADS)]
    for layer in range(DEPTH):
        units += [("slc", layer, h) for h in range(4)] + [("win", layer, h) for h in range(4)]
        units += [("fox", layer, h) for h in range(4)]
    return units


UNITS = attention_units()
SCORES = [(u, q, c) for u in UNITS for q in range(ST) for c in range(2 if u[0] == "C" else 1)]
SCORE_AT = {key: n for n, key in enumerate(SCORES)}
TURNS = [(u, q) for u in UNITS for q in range(ST)]
TURN_AT = {key: n for n, key in enumerate(TURNS)}
UNIT_AT = {u: n for n, u in enumerate(UNITS)}


def rope_jobs():
    jobs = [("qkA", t) for t in range(8)] + [("kpe",)] + [("qB", h) for h in range(B_HEADS)]
    jobs += [("qkC", t) for t in range(16)]
    for layer in range(DEPTH):
        jobs += [(kind, layer) for kind in ("ks", "kw", "nq0", "nq1", "kc")]
    return jobs


ROPES = rope_jobs()
ROPE_AT = {key: n for n, key in enumerate(ROPES)}

N_INPUTS = 11
N_CLEAR = 10
SETUP = {"rest": 8, "lam_sums": 10, "all": 13}
_c2 = round((2 * math.pi - 6.28125) * 2 ** 21) / 2 ** 21
TWO_PI = (6.28125, _c2, 2 * math.pi - 6.28125 - _c2)


def build(nc, dram, out):
    ctx = ExitStack()
    with ctx:
        def sb(name, shape, dt=F32):
            return ctx.enter_context(nc.sbuf_tensor(name, shape, dt))

        def sem(name):
            return ctx.enter_context(nc.semaphore(name))

        ring = sb("ring", [P, RING, BLK])
        x = sb("x", [P, KD, S])
        z = sb("z", [P, KD, S])
        mix = sb("mix", [P, KD, S])
        arena = sb("arena", [P, 21 * 1024])
        early = sb("early", [P, 4096])
        cols = sb("cols", [P, NCOLS])
        n_first = TABS["cos2"] - TABS["log_count"]
        n_late = NTABS - n_first
        tabs = sb("tabs", [P, n_late])
        small_w = sb("small_w", [P, DEPTH * 320])
        cmp_pos = sb("cmp_pos", [P, DEPTH * CMP_LEN])
        b2v = sb("b2v", [P, DEPTH * HD])
        prob = sb("prob", [P, 4, S])
        rope_tmp = sb("rope_tmp", [P, 2, S])
        std = sb("std", [P, 2, S])
        rstd = sb("rstd", [P, 2, S])
        negmax = sb("negmax", [P, 8])
        rowsum = sb("rowsum", [P, 8])
        rownorm = sb("rownorm", [P, 8])
        cmp_negmax = sb("cmp_negmax", [P, 16])
        neg_lam = sb("neg_lam", [P, 8])
        ident_bf = sb("ident_bf", [P, P], BF16)
        tri_bf = sb("tri_bf", [P, P], BF16)
        cmp_bias_bf = sb("cmp_bias_bf", [P, S], BF16)
        psum = [ctx.enter_context(nc.psum_tensor(f"bank{i}", [P, S], F32)) for i in range(8)]

        def col(name, i=0, rows=slice(0, P)):
            return cols[rows, COLS[name] + i:COLS[name] + i + 1]

        def tab(name, width):
            at = TABS[name] - (n_first if TABS[name] > TABS["log_count"] else 0)
            return tabs[:, at:at + width]

        ident, ones = tab("ident", P), tab("ones", P)
        perm_a, perm_b = tab("perm_a", P), tab("perm_b", P)
        log_count = early[:, 0:ST * S].rearrange("p (q k) -> p q k", q=ST)
        cos_a, sin_a, cos_b, sin_b = (early[:, ST * S + i * S:ST * S + i * S + S] for i in range(4))
        gates = early[:, 0:6 * S].rearrange("p (b j s) -> p b j s", b=3, j=2)
        sel = tab("sel", 6 * P).rearrange("p (b j m) -> p b j m", b=3, j=2)
        ones_bd = tab("ones_bd", 2 * P).rearrange("p (j m) -> p j m", j=2)
        inv_count = tab("inv_count", 2 * S).rearrange("p (t s) -> p t s", t=2)
        pt = z[:, :, :].rearrange("p (u k) q -> p u k q", u=2)

        def place(at, *shape):
            n = int(np.prod(shape))
            assert at + n <= 21 * 1024
            v = arena[:, at:at + n]
            if len(shape) == 2:
                return v.rearrange("p (a b) -> p a b", a=shape[0])
            if len(shape) == 3:
                return v.rearrange("p (a b c) -> p a b c", a=shape[0], b=shape[1])
            if len(shape) == 4:
                return v.rearrange("p (a b c d) -> p a b c d", a=shape[0], b=shape[1], c=shape[2])
            return v

        pos_raw, pos_f = mix[:, 0, :].bitcast(I32), mix[:, 1, :]
        angle, turns, rest = z[:, 0:2, :], z[:, 2:4, :], z[:, 4:6, :]
        masks_in = mix[:, 3:5, :].rearrange("p t s -> p (t s)")[:, 0:S + P]
        lam_in = mix[:, 2, 0:4 * HD]
        qk_a = place(0, 8, S)
        q_b = place(4096, 8, S)
        k_b = place(8192, 8, S)
        v_a = place(12288, ST, 4, 3 * HD)
        v_b = place(15360, ST, 4, 3 * HD)
        lat = place(18432, 5, S)
        kpe = z[:, 0, :]
        qk_c = place(0, 16, S)
        v_c = place(8192, ST, KD * P)
        hid = place(0, KF, S)
        conv_t = place(KF * S, 2, S)
        gelu_t = place(KF * S + 2 * S, 2, S)
        square = place(0, KD, S)
        sig_p = place(0, KD, S)
        p_in_t = place(16384, 2, S)
        h2 = place(0, KD, S)
        sg = place(4096, KD, S)
        nq = place(8192, 2, S)
        ksw = place(9216, 2, S)
        kcvc = place(10240, S)
        blocks_x = place(10752, CMP_LEN, CMP_N)
        fqk = place(11776, 4, S)
        v_s = place(13824, ST, 3 * HD)
        v_w = place(14592, ST, 3 * HD)
        v_f = place(15360, ST, 2, 3 * HD)
        cq = place(16896, S)
        ck = place(17408, S)
        gate_sig = place(17920, S)
        vc_bd = place(18432, 2, P)
        hid_k = place(18688, CMP_N)
        hid_v = place(18720, 4, CMP_N)
        kc = place(18848, CMP_N)
        conv_x = early[:, 6 * S:8 * S].rearrange("p (t s) -> p t s", t=2)
        conv_b = place(18880, 2, S)
        conv_u = place(19904, 2, 2 + S)
        pool_u, pool_a, pool_b = (z[:, :, :].rearrange("p t s -> p (t s)")[:, i * 2 * (PAD + S):(i + 1) * 2 * (PAD + S)]
                                  .rearrange("p (t s) -> p t s", t=2) for i in range(3))
        acc = place(8192, KD, S)
        sig_m = place(12288, 2, N_BRANCH, S)

        full = [sem(f"slot{i}_full") for i in range(RING)]
        block_done = sem("block_done")
        inputs_in = sem("inputs_in")
        tables_ready = sem("tables_ready")
        setup_dve, setup_act = sem("setup_dve"), sem("setup_act")
        link_dve, link_act, link_pool = sem("link_dve"), sem("link_act"), sem("link_pool")
        v_stored = sem("v_stored")
        ones_set = sem("ones_set")
        rope_raw, rope_perm, rope_cos, roped = sem("rope_raw"), sem("rope_perm"), sem("rope_cos"), sem("roped")
        lat_raw, kb_stored = sem("lat_raw"), sem("kb_stored")
        squared, summed, std_ready, normed = sem("squared"), sem("summed"), sem("std_ready"), sem("normed")
        scored, maxed, exped, blended = sem("scored"), sem("maxed"), sem("exped"), sem("blended")
        turned, pt_stored, weighed, attended = sem("turned"), sem("pt_stored"), sem("weighed"), sem("attended")
        z_ready, mean_ready, centered, x_ready = sem("z_ready"), sem("mean_ready"), sem("centered"), sem("x_ready")
        conv_mid, conv_done, gelu_done, hid_ready = (sem("conv_mid"), sem("conv_done"), sem("gelu_done"),
                                                     sem("hid_ready"))
        conv_mid2 = sem("conv_mid2")
        p_loaded, ple_sig, ple_term, x_ple = sem("p_loaded"), sem("ple_sig"), sem("ple_term"), sem("x_ple")
        kpe_spread = sem("kpe_spread")
        constants_bf = sem("constants_bf")
        stored, prepared, spread = sem("stored"), sem("prepared"), sem("spread")
        compress_step, cleared, gated = sem("compress_step"), sem("cleared"), sem("gated")
        sig_ready, merged, merge_link, x_next = sem("sig_ready"), sem("merged"), sem("merge_link"), sem("x_next")
        out_stored = sem("out_stored")

        T = {}
        T["v"] = Tally([("A", i) for i in range(4)] + [("B", i) for i in range(4)] + [("C", i) for i in range(8)])
        T["squared"], T["summed"], T["std"], T["normed"] = Tally(), Tally(), Tally(), Tally()
        for n in range(5):
            T["squared"].add(("lat", n))
        for j in range(2):
            T["summed"].add(("lat", j)), T["std"].add(("lat", j))
        for n in range(5):
            T["normed"].add(("lat", n))

        def plan_ln(i):
            for n in range(KD):
                T["squared"].add(("ln", i, n)), T["normed"].add(("ln", i, n))
            T["summed"].add(("ln", i)), T["std"].add(("ln", i))

        plan_ln(0), plan_ln(1)
        for n in range(C_HEADS):
            for t in ("squared", "summed", "std", "normed"):
                T[t].add(("C", n))
        plan_ln(2), plan_ln(3)
        for i in range(DEPTH + 1):
            for n in range(KD):
                T["squared"].add(("rms", i, n)), T["normed"].add(("rms", i, n))
            T["summed"].add(("rms", i)), T["std"].add(("rms", i))

        T["stored"], T["prepared"] = Tally(), Tally()
        for layer in range(DEPTH):
            for key in ["gsig", "fl", "kcvc", "vs", "vw", "hidk", "hidv", "fq0", "fq1", "fk0", "fk1", "fv0", "fv1",
                        "fv2", "fv3", "pool0", "pool1", "cx0", "cx1", "cb0", "cb1", *[f"sg{t}" for t in range(8)],
                        *[f"g{n}" for n in range(6)], "ln", "pm0", "pm1", "pm2", "pm3", "cmp_exp"]:
                T["stored"].add((key, layer))
            for key in ["blocks", "vc", "pooled", "cu0", "cu1", "convy0", "convy1", "decay", "cmp_shift", "cmp_pt",
                        "cmp_out0", "cmp_out"]:
                T["prepared"].add((key, layer))

        block = ctx.enter_context(nc.Block())

        def done(key):
            return AT[key] + 1

        @block.sync
        def _(sp):
            for s in range(RING):
                sp.dma_start(ring[:, s, :], dram["weights"][s]).then_inc(full[s], 16)
            with sp.Fori(1, len(BLOCKS) // RING) as it:
                for s in range(RING):
                    sp.wait_ge(block_done, RING * it + (s - RING + 1))
                    sp.dma_start(ring[:, s, :], dram["weights"][RING * it + s]).then_inc(full[s], 16)
            for n in range(len(BLOCKS) // RING * RING, len(BLOCKS)):
                sp.wait_ge(block_done, n - RING + 1)
                sp.dma_start(ring[:, n % RING, :], dram["weights"][n]).then_inc(full[n % RING], 16)

            for n in range(KD):
                sp.wait_ge(normed, T["normed"][("rms", DEPTH, n)])
                sp.dma_start(out[:, n, :], z[:, n, :]).then_inc(out_stored, 16)
            sp.wait_ge(out_stored, 16 * KD)

        @block.tensor
        def _(pe):
            def arrived(key):
                n = AT[key]
                pe.wait_ge(full[n % RING], 16 * (n // RING + 1))
                return ring[:, n % RING, :]

            def project(key, bank, rhs, kt=KD):
                w = arrived(key)
                for k in range(kt):
                    mm = pe.matmul(bank, w[:, k * P:k * P + P], rhs(k), start=(k == 0), stop=(k == kt - 1))
                mm.then_inc(block_done, 1)

            def turn_pairs(job, matrix, rows, raw, n=S):
                g = ROPE_AT[job]
                pe.wait_ge(rope_raw, g + 1)
                if g >= 2:
                    pe.wait_ge(roped, g - 1)
                pe.matmul(psum[4 + g % 2][0:rows, 0:n], matrix[0:rows, 0:rows], raw, start=True,
                          stop=True).then_inc(rope_perm, 1)

            def tokens_values(keys, lhs, banks, width, per):
                for i, key in enumerate(keys):
                    w = arrived(key)
                    for st in range(ST):
                        for j in range(per):
                            k = i * per + j
                            mm = pe.matmul(banks[st], lhs(k)[:, st * P:st * P + P], w[:, j * width:j * width + width],
                                           start=(k == 0), stop=(k == len(keys) * per - 1))
                    mm.then_inc(block_done, 1)

            def attention(units, q, k, v, extra, ahead, blend=False, causal=False):
                turns = [(u, i) for u in units for i in range(ST)]
                comps = 2 if blend else 1

                def scores(u, i):
                    for c in range(comps):
                        s = SCORE_AT[(u, i, c)]
                        if s >= 4:
                            pe.wait_ge(exped, s - 3)
                        w = (i + 1) * P if causal else S
                        bank = psum[s % 4]
                        more = extra(bank, u, i)
                        mm = pe.matmul(bank[:, 0:w], q(u, c)[:, i * P:i * P + P], k(u, c)[:, 0:w], start=True,
                                       stop=True)
                        for o, lhs, rhs in more:
                            mm = pe.matmul(o, lhs, rhs, start=False, stop=True, skip_group_check=True)
                        mm.then_inc(scored, 1)

                def values(u):
                    n = UNIT_AT[u]
                    pe.wait_ge(pt_stored, TURN_AT[(u, ST - 1)] + 1)
                    if n >= 2:
                        pe.wait_ge(attended, n - 1)
                    for t in range(ST):
                        lo = t * P if causal else 0
                        mm = pe.matmul(psum[6 + n % 2][:, lo:S], v(u, t), pt[:, n % 2, t, lo:S], start=(t == 0),
                                       stop=(t == ST - 1))
                    mm.then_inc(weighed, 1)

                for u, i in turns[:ahead]:
                    scores(u, i)
                for n, (u, i) in enumerate(turns):
                    if n + ahead < len(turns):
                        scores(*turns[n + ahead])
                    t = TURN_AT[(u, i)]
                    s = SCORE_AT[(u, i, 0)]
                    if blend:
                        pe.wait_ge(blended, t - TURN_AT[(("C", 0), 0)] + 1)
                    else:
                        pe.wait_ge(exped, s + 1)
                    if t >= 2:
                        pe.wait_ge(pt_stored, t - 1)
                    for kt in range(i + 1 if causal else ST):
                        mm = pe.transpose(psum[4 + t % 2][:, kt * P:kt * P + P], prob[:, s % 4, kt * P:kt * P + P], ident)
                    mm.then_inc(turned, 1)
                    if n and turns[n - 1][1] == ST - 1:
                        values(turns[n - 1][0])
                values(units[-1])

            def residual_norm(i, after=None):
                for n in range(KD):
                    pe.wait_ge(z_ready, KD * i + max(n, 3) + 1)
                    mm = pe.matmul(psum[6][:], ones, z[:, n, :], start=(n == 0), stop=(n == KD - 1))
                mm.then_inc(mean_ready, 1)
                sum_squares(("ln", i), psum[7], KD, lambda n: square[:, n, :])

            def sum_squares(key, bank, count, tile, names=None):
                for n in range(count):
                    pe.wait_ge(squared, T["squared"][names(n) if names else key + (n,)])
                    mm = pe.matmul(bank[:], ones, tile(n), start=(n == 0), stop=(n == count - 1))
                mm.then_inc(summed, 1)

            def mixer_out(i):
                layer = i // 2
                if layer == 0:
                    pe.wait_ge(attended, UNIT_AT[("B", B_HEADS - 1)] + 1)
                for n in range(KD):
                    if n >= 4:
                        pe.wait_ge(z_ready, KD * i + n - 3)
                    project(("mixout", layer, n), psum[n % 4][:], lambda k: mix[:, k, :])

            def feed_forward(i):
                layer = i // 2
                pe.wait_ge(x_ready, KD * (i - 1) + KD)
                n0 = AT[("gate", layer, 0)]
                with pe.Fori(0, KF // 2) as it:
                    for par in range(2):
                        pe.wait_ge(hid_ready, 2 * it + (par + 1 + KF * layer))
                        for half in range(2):
                            s = (n0 + 2 * par + half) % RING
                            pe.wait_ge(full[s], 16 * it + 16 * ((n0 + 2 * par + half) // RING + 1))
                            for k in range(KD):
                                mm = pe.matmul(psum[2 * half + par][:], ring[:, s, k * P:k * P + P], x[:, k, :],
                                               start=(k == 0), stop=(k == KD - 1))
                            mm.then_inc(block_done, 1)
                for h in range(2):
                    banks = psum[4:8] if h == 0 else psum[0:4]
                    d0 = AT[("down", layer, h, 0)]

                    def down(b, it, first=False, last=False):
                        s = (d0 + b) % RING
                        pe.wait_ge(full[s], 16 * it + 16 * ((d0 + b) // RING + 1))
                        if h == 0:
                            pe.wait_ge(hid_ready, 2 * RING * it + (2 * b + 2 + 2 + KF * layer))
                        for j in range(2):
                            for n in range(4):
                                tile = hid[:, 2 * RING * it + (2 * b + j), :]
                                mm = pe.matmul(banks[n][:], ring[:, s, j * S + n * P:j * S + n * P + P], tile,
                                               start=(first and j == 0), stop=(last and j == 1),
                                               skip_group_check=True)
                        mm.then_inc(block_done, 1)

                    for b in range(3):
                        down(b, 0, first=(b == 0))
                    with pe.Fori(0, 2) as it:
                        for b in range(3, 7):
                            down(b, it)

            def per_layer(layer):
                for half in range(2):
                    w = arrived(("pleproj", layer, half))
                    if half == 0:
                        pe.wait_ge(p_loaded, 16 * (layer + 1))
                        pe.wait_ge(std_ready, T["std"][("ln", 2 * layer + 1)])
                    else:
                        pe.wait_ge(ple_term, KD * layer + 4)
                    for n in range(4):
                        for k in range(2):
                            mm = pe.matmul(psum[4 + n][:], w[:, k * S + n * P:k * S + n * P + P], p_in_t[:, k, :],
                                           start=(k == 0), stop=(k == 1))
                    mm.then_inc(block_done, 1)
                    if half == 0:
                        pe.wait_ge(x_ready, KD * (2 * layer + 1) + KD)
                    for n in range(4 * half, 4 * half + 4):
                        if n >= 4:
                            pe.wait_ge(ple_sig, KD * layer + n - 3)
                        project(("plegate", layer, n), psum[n % 4][:], lambda k: x[:, k, :])

            def mixer_a():
                pe.wait_ge(inputs_in, 16 * N_INPUTS)
                tokens_values([("vA", i) for i in range(4)], lambda k: x[:, k, :], [psum[i][:] for i in range(4)], S, 2)
                for t in range(8):
                    if t < 4:
                        pe.wait_ge(v_stored, T["v"][("A", t)])
                    else:
                        pe.wait_ge(rope_raw, ROPE_AT[("qkA", t - 4)] + 1)
                    project(("qkA", t), psum[t % 4][:], lambda k: x[:, k, :])
                    if t:
                        turn_pairs(("qkA", t - 1), perm_a, P, qk_a[:, t - 1, :])
                for n in range(5):
                    if n < 4:
                        pe.wait_ge(rope_raw, ROPE_AT[("qkA", 4 + n)] + 1)
                    else:
                        pe.wait_ge(lat_raw, n - 3)
                    project(("lat", n), psum[n % 4][:], lambda k: x[:, k, :])
                    if n == 0:
                        turn_pairs(("qkA", 7), perm_a, P, qk_a[:, 7, :])
                w = arrived(("kpe", 0))
                pe.wait_ge(lat_raw, 2)
                for k in range(KD):
                    mm = pe.matmul(psum[1][0:B_QK, :], w[:, k * B_QK:k * B_QK + B_QK], x[:, k, :], start=(k == 0),
                                   stop=(k == KD - 1))
                mm.then_inc(block_done, 1)
                sum_squares(None, psum[6], 3, lambda n: mix[:, n, :], lambda n: ("lat", n))
                sum_squares(None, psum[7], 2, lambda n: mix[:, 3 + n, :], lambda n: ("lat", 3 + n))
                turn_pairs(("kpe",), perm_b, B_QK, kpe[0:B_QK, :])

            def mixer_b():
                pe.wait_ge(normed, T["normed"][("lat", 2)])
                for i in range(3):
                    w = arrived(("qup", i))
                    heads = range(3 * i, min(3 * i + 3, B_HEADS))
                    for h in heads:
                        if h < 4:
                            pe.wait_ge(lat_raw, 5)
                            pe.wait_ge(rope_raw, ROPE_AT[("kpe",)] + 1)
                        else:
                            pe.wait_ge(rope_raw, ROPE_AT[("qB", h - 4)] + 1)
                        for k in range(3):
                            lo = (h - 3 * i) * 3 * B_QK + k * B_QK
                            mm = pe.matmul(psum[h % 4][0:B_QK, :], w[:, lo:lo + B_QK], lat[:, k, :], start=(k == 0),
                                           stop=(k == 2))
                    mm.then_inc(block_done, 1)
                    if i:
                        for h in range(3 * i - 3, 3 * i):
                            turn_pairs(("qB", h), perm_b, B_QK, q_b[0:B_QK, h, :])
                pe.wait_ge(normed, T["normed"][("lat", 4)])
                w = arrived(("kvk", 0))
                pe.wait_ge(rope_raw, ROPE_AT[("qB", 7)] + 1)
                for j in range(4):
                    for k in range(2):
                        lo = j * 2 * P + k * P
                        mm = pe.matmul(psum[j][:], w[:, lo:lo + P], lat[:, 3 + k, :], start=(k == 0), stop=(k == 1))
                mm.then_inc(block_done, 1)
                for h in range(6, 8):
                    turn_pairs(("qB", h), perm_b, B_QK, q_b[0:B_QK, h, :])
                pe.wait_ge(kb_stored, 8)
                tokens_values([("kvv", 0)], lambda k: lat[:, 3 + k, :], [psum[i][:] for i in range(4)], S, 2)

            def heads_ab():
                pe.wait_ge(v_stored, T["v"][("B", 3)])
                pe.wait_ge(roped, ROPE_AT[("qB", 7)] + 1)
                pe.wait_ge(kpe_spread, 1)
                pe.wait_ge(cleared, 1)
                half = lambda h: slice(HD * (h % 2), HD * (h % 2) + HD)

                def q(u, c):
                    h = u[1]
                    return qk_a[half(h), h // 2, :] if u[0] == "A" else q_b[0:B_QK, h, :]

                def k(u, c):
                    h = u[1]
                    return qk_a[half(h), 4 + h // 2, :] if u[0] == "A" else k_b[0:B_QK, h, :]

                def v(u, t):
                    h = u[1]
                    return (v_a if u[0] == "A" else v_b)[:, t, h // 2, HD * (h % 2):HD * (h % 2) + P]

                def count(bank, u, i):
                    return [(bank[:], ident, log_count[:, i, :])] if u[0] == "A" else []

                attention([u for u in UNITS if u[0] in "AB"], q, k, v, count, ahead=2)

            def mixer_c():
                pe.wait_ge(x_ple, KD)
                for half in range(2):
                    tokens_values([("vC", 4 * half + i) for i in range(4)], lambda k: x[:, k, :],
                                  [psum[4 * half + i][:] for i in range(4)], S, 2)
                for t in range(16):
                    if t < 4:
                        pe.wait_ge(v_stored, T["v"][("C", t)])
                    else:
                        pe.wait_ge(rope_raw, ROPE_AT[("qkC", t - 4)] + 1)
                    project(("qkC", t), psum[t % 4][:], lambda k: x[:, k, :])
                    if t:
                        if t == 1:
                            pe.wait_ge(v_stored, T["v"][("C", 7)])
                        turn_pairs(("qkC", t - 1), perm_a, P, qk_c[:, t - 1, :])
                turn_pairs(("qkC", 15), perm_a, P, qk_c[:, 15, :])

            def heads_c():
                pe.wait_ge(roped, ROPE_AT[("qkC", 15)] + 1)
                half = lambda c: slice(HD * c, HD * c + HD)
                attention([u for u in UNITS if u[0] == "C"], lambda u, c: qk_c[half(c), u[1], :],
                          lambda u, c: qk_c[half(c), 8 + u[1], :], lambda u, t: v_c[:, t, u[1] * P:u[1] * P + P],
                          lambda bank, u, i: [], ahead=1, blend=True)
                for n in range(C_HEADS):
                    if n >= 4:
                        pe.wait_ge(std_ready, T["std"][("C", n - 4)])
                    sum_squares(None, psum[n % 4], 1, lambda _: square[:, n, :], lambda _: ("C", n))
                pe.wait_ge(normed, T["normed"][("C", C_HEADS - 1)])

            def sum_rms(i):
                sum_squares(("rms", i), psum[7], KD, lambda n: square[:, n, :])

            def project_second(layer):
                stored_at = lambda key: pe.wait_ge(stored, T["stored"][(key, layer)])
                raw_at = lambda key: pe.wait_ge(rope_raw, ROPE_AT[(key, layer)] + 1)
                rhs = lambda k: h2[:, k, :]
                pe.wait_ge(normed, T["normed"][("rms", layer, KD - 1)])
                project(("small", layer), psum[0][:], rhs)
                project(("kcvc", layer), psum[1][:], rhs)
                w = arrived(("vsvw", layer))
                for st in range(ST):
                    for k in range(KD):
                        mm = pe.matmul(psum[2][:, st * P:st * P + P], h2[:, k, st * P:st * P + P],
                                       w[:, k * P:k * P + P], start=(k == 0), stop=(k == KD - 1))
                mm.then_inc(block_done, 1)
                project(("ks", layer), psum[3][:], rhs)
                stored_at("fl")
                project(("kw", layer), psum[0][:], rhs)
                turn_pairs(("ks", layer), perm_a, P, ksw[:, 0, :])
                stored_at("kcvc")
                project(("nq", layer, 0), psum[1][:], rhs)
                turn_pairs(("kw", layer), perm_a, P, ksw[:, 1, :])
                stored_at("vw")
                project(("nq", layer, 1), psum[2][:], rhs)
                turn_pairs(("nq0", layer), perm_a, P, nq[:, 0, :])
                pe.wait_ge(prepared, T["prepared"][("blocks", layer)])
                for i in range(4):
                    w = arrived(("w1", layer, i))
                    for l in range(8):
                        for c, bank in ((0, psum[3]), (1, psum[6])):
                            rows = slice(HD * c, HD * c + HD)
                            mm = pe.matmul(bank[:, 0:CMP_N], w[rows, l * P:l * P + P], blocks_x[rows, 8 * i + l, :],
                                           start=(i == 0 and l == 0), stop=(i == 3 and l == 7))
                    mm.then_inc(block_done, 1)
                turn_pairs(("nq1", layer), perm_a, P, nq[:, 1, :])
                stored_at("hidk")
                lo = layer * 320
                pe.matmul(psum[7][:, 0:CMP_N], small_w[:, lo:lo + P], hid_k, start=True,
                          stop=True).then_inc(compress_step, 1)
                stored_at("hidv")
                pe.matmul(psum[3][:, 0:HD], hid_v.rearrange("p a n -> p (a n)"), small_w[:, lo + P:lo + P + HD],
                          start=True, stop=True).then_inc(compress_step, 1)
                raw_at("kw")
                project(("fq", layer, 0), psum[0][:], rhs)
                turn_pairs(("kc", layer), perm_a, P, kc, CMP_N)
                raw_at("nq0")
                project(("fq", layer, 1), psum[1][:], rhs)
                raw_at("nq1")
                project(("fk", layer, 0), psum[2][:], rhs)
                pe.wait_ge(prepared, T["prepared"][("vc", layer)])
                project(("fk", layer, 1), psum[3][:], rhs)
                stored_at("fk1")
                tokens_values([("fv", layer, i) for i in range(2)], rhs, [psum[i][:, 0:256] for i in range(4)], 256, 4)
                for n, (key, before) in enumerate([(("pool", layer, 0), "fv0"), (("pool", layer, 1), "fv1"),
                                                   (("conv", layer, 0), "fv2"), (("conv", layer, 1), "fv3"),
                                                   (("conv", layer, 2), "pool0"), (("conv", layer, 3), "pool1"),
                                                   (("conv", layer, 4), "cx0"), (("conv", layer, 5), "cx1"),
                                                   (("sgate", layer, 0), "cb0"), (("sgate", layer, 1), "cb1")]):
                    stored_at(before)
                    project(key, psum[n % 4][:], rhs)
                for n in range(2, 8):
                    if n < 4:
                        pe.wait_ge(prepared, T["prepared"][(f"cu{n - 2}", layer)])
                    else:
                        stored_at(f"sg{n - 4}")
                    project(("sgate", layer, n), psum[n % 4][:], rhs)
                stored_at("gsig")
                for n in range(6):
                    stored_at(f"sg{n + 4}" if n < 4 else f"g{n - 4}")
                    pe.matmul(psum[n % 4][:], sel[:, n // 2, n % 2, :], gate_sig, start=True,
                              stop=True).then_inc(spread, 1)
                pe.wait_ge(prepared, T["prepared"][("pooled", layer)])
                for g in range(4):
                    stored_at(f"g{(g + 2) if g < 2 else g + 2}")
                    rows = slice(HD * (g % 2), HD * (g % 2) + HD)
                    at = lo + 192 + HD * (g // 2)
                    pe.matmul(psum[(g + 2) % 4][rows, :], small_w[rows, at:at + HD], mix[rows, 2 + g // 2, :], start=True,
                              stop=True).then_inc(spread, 1)

            def heads_compressed(layer):
                pe.wait_ge(roped, ROPE_AT[("kc", layer)] + 1)
                pe.wait_ge(constants_bf, 3)
                for odd in range(2):
                    bank = psum[6 + odd]
                    mask = cmp_bias_bf[:].rearrange("p (i h n) -> p i h n", i=ST, h=4)[:, :, 0:2, :]
                    pe.matmul(bank[:, 0:2 * P], ident_bf[:], mask, start=True, stop=True)
                    rows = slice(HD * odd, HD * odd + HD)
                    for i in range(ST):
                        for j in range(2):
                            lo = (2 * i + j) * CMP_N
                            mm = pe.matmul(bank[:, lo:lo + CMP_N], nq[rows, j, i * P:i * P + P], kc[rows, :],
                                           start=False, stop=True, skip_group_check=True)
                mm.then_inc(compress_step, 1)
                pe.wait_ge(stored, T["stored"][("cmp_exp", layer)])
                for i in range(ST):
                    mm = pe.transpose(psum[7][:, i * P:i * P + P], rstd[:, 1, i * P:i * P + P], ident)
                mm.then_inc(compress_step, 1)
                pe.wait_ge(prepared, T["prepared"][("cmp_pt", layer)])
                pe.wait_ge(stored, T["stored"][("pm3", layer)])
                for j in range(2):
                    pe.matmul(psum[j][:], vc_bd[:, j, :], prob[:, 3, :], start=True, stop=True)
                    mm = pe.matmul(psum[2 + j][:], ones_bd[:, j, :], prob[:, 3, :], start=True, stop=True)
                mm.then_inc(compress_step, 1)

            def heads_second(layer):
                half = lambda h: slice(HD * (h % 2), HD * (h % 2) + HD)
                pe.wait_ge(prepared, T["prepared"][("cmp_out", layer)])
                pe.wait_ge(cleared, 1 + N_CLEAR * (layer + 1))

                def q(u, c):
                    h = u[2]
                    return nq[half(h), h // 2, :] if u[0] != "fox" else fqk[half(h), h // 2, :]

                def k(u, c):
                    h = u[2]
                    return fqk[half(h), 2 + h // 2, :] if u[0] == "fox" else ksw[half(h), int(u[0] == "win"), :]

                def v(u, t):
                    h = u[2]
                    if u[0] == "fox":
                        return v_f[:, t, h // 2, HD * (h % 2):HD * (h % 2) + P]
                    lo = HD * (1 - h % 2)
                    return (v_s if u[0] == "slc" else v_w)[:, t, lo:lo + P]

                def extra(bank, u, i):
                    more = []
                    if u[0] == "fox":
                        rows = slice(32 * u[2], 32 * u[2] + 2)
                        more.append((bank[:, 0:i * P + P], cq[rows, i * P:i * P + P], ck[rows, 0:i * P + P]))
                    more.append((bank[:, i * P:i * P + P], ident_bf[:], tri_bf[:]))
                    return more

                attention([u for u in UNITS if len(u) == 3 and u[1] == layer], q, k, v, extra, ahead=2, causal=True)

            def merge(layer):
                pe.wait_ge(gated, KD * (layer + 1))
                pe.wait_ge(attended, UNIT_AT[("fox", layer, 3)] + 1)
                n0 = AT[("merge", layer, 0, 0)]
                per = N_BRANCH + 1
                with pe.Fori(0, KD // 4) as it:
                    for d in range(4):
                        for i in range(N_BRANCH):
                            b = per * d + i
                            s = (n0 + b) % RING
                            pe.wait_ge(full[s], 16 * 5 * it + 16 * ((n0 + b) // RING + 1))
                            pe.wait_ge(sig_ready, 16 * it + (4 * d + i + 1 + 32 * layer))
                            for k in range(KD):
                                mm = pe.matmul(psum[i][:], ring[:, s, k * P:k * P + P], h2[:, k, :], start=(k == 0),
                                               stop=(k == KD - 1))
                            mm.then_inc(block_done, 1)
                        b = per * d + N_BRANCH
                        s = (n0 + b) % RING
                        pe.wait_ge(full[s], 16 * 5 * it + 16 * ((n0 + b) // RING + 1))
                        pe.wait_ge(merged, 4 * it + (d + 2 + KD * layer))
                        for i in range(N_BRANCH):
                            for k in range(2):
                                j = 2 * i + k
                                mm = pe.matmul(psum[4 + i][:], ring[:, s, j * P:j * P + P], mix[:, j, :], start=(k == 0),
                                               stop=(k == 1))
                        mm.then_inc(block_done, 1)
                pe.wait_ge(merged, 2 + KD * (layer + 1))
                for n in range(KD):
                    if n >= 4:
                        pe.wait_ge(x_next, KD * layer + n - 3)
                    project(("out2", layer, n), psum[n % 4][:], lambda k: acc[:, k, :])

            stages_pe2 = []
            for layer in range(DEPTH):
                stages_pe2 += [lambda l=layer: sum_rms(l), lambda l=layer: project_second(l),
                               lambda l=layer: heads_compressed(l), lambda l=layer: heads_second(l),
                               lambda l=layer: merge(l)]
            stages_pe2 += [lambda: sum_rms(DEPTH)]

            stages = [
                mixer_a, mixer_b, heads_ab, lambda: mixer_out(0), lambda: residual_norm(0),
                lambda: feed_forward(1), lambda: residual_norm(1), lambda: per_layer(0),
                mixer_c, heads_c, lambda: mixer_out(2), lambda: residual_norm(2),
                lambda: feed_forward(3), lambda: residual_norm(3), lambda: per_layer(1),
            ]
            stages += stages_pe2
            for stage in stages:
                stage()

        @block.scalar
        def _(act):
            linked = [0]

            def link(ins):
                linked[0] += 1
                ins.then_inc(link_act, 1)
                act.wait_ge(link_act, linked[0])

            def raw(job, dst, src, scale=1.0, bias=None):
                if bias is None:
                    ins = act.activation(dst, src, ACT.Copy, scale=scale)
                else:
                    ins = act.activation(dst, src, ACT.Identity, bias=bias, scale=scale)
                ins.then_inc(rope_raw, 1)

            def values(keys, blk, dst, src):
                act.wait_ge(block_done, done(blk))
                for i, _ in enumerate(keys):
                    act.activation(dst(i), src(i), ACT.Copy).then_inc(v_stored, 1)

            def pairs(v):
                return v.rearrange("p j (t d) -> p j t d", t=3)[:, :, 0:3:2, :]

            def deviation(key, bank, count, eps, buf):
                act.wait_ge(summed, T["summed"][key])
                act.activation(std[:, buf, :], bank[:], ACT.Sqrt, bias=eps, scale=1.0 / count).then_inc(std_ready, 1)

            def attention(units, blend=False, causal=False):
                turns = [(u, i) for u in units for i in range(ST)]
                comps = 2 if blend else 1

                def copy_turned(u, i):
                    t, n = TURN_AT[(u, i)], UNIT_AT[u]
                    act.wait_ge(turned, t + 1)
                    if i == 0 and n >= 2:
                        act.wait_ge(weighed, n - 1)
                    kt = i + 1 if causal else ST
                    act.activation(pt[:, n % 2, 0:kt, i * P:i * P + P],
                                   psum[4 + t % 2][:, 0:kt * P].rearrange("p (k q) -> p k q", k=kt),
                                   ACT.Copy).then_inc(pt_stored, 1)

                for n, (u, i) in enumerate(turns):
                    for c in range(comps):
                        s = SCORE_AT[(u, i, c)]
                        act.wait_ge(maxed, s + 1)
                        t = TURN_AT[(u, i)]
                        back = 2 if blend else 4
                        if t >= back:
                            act.wait_ge(turned, t - back + 1)
                        w = (i + 1) * P if causal else S
                        act.activation(prob[:, s % 4, 0:w], psum[s % 4][:, 0:w], ACT.Exp, bias=negmax[:, s % 8:s % 8 + 1],
                                       accum_out=rowsum[:, s % 8:s % 8 + 1] if blend else None).then_inc(exped, 1)
                    if n:
                        copy_turned(*turns[n - 1])
                copy_turned(*turns[-1])

            def setup():
                act.dma_start(x[:, :, :], dram["x_t"].rearrange("p (t s) -> p t s", t=KD)).then_inc(inputs_in, 16)
                act.dma_start(pos_raw, dram["positions"]).then_inc(inputs_in, 16)
                act.dma_start(cols[:, :], dram["columns"]).then_inc(inputs_in, 16)
                lo = TABS["log_count"]
                act.dma_start(tabs[:, 0:lo], dram["tables"][:, 0:lo]).then_inc(inputs_in, 16)
                act.dma_start(tabs[:, lo:n_late], dram["tables"][:, lo + n_first:NTABS]).then_inc(inputs_in, 16)
                act.dma_start(early[:, 0:ST * S], dram["tables"][:, lo:lo + ST * S]).then_inc(inputs_in, 16)
                act.dma_start(masks_in, dram["tables"][:, lo + ST * S:lo + n_first]).then_inc(inputs_in, 16)
                act.dma_start(small_w[:, :], dram["small_w"]).then_inc(inputs_in, 16)
                act.dma_start(cmp_pos[:, :], dram["cmp_pos"]).then_inc(inputs_in, 16)
                act.dma_start(b2v[:, :], dram["b2v"]).then_inc(inputs_in, 16)
                act.dma_start(lam_in, dram["lam"]).then_inc(inputs_in, 16)
                act.nop().then_inc(sig_ready, N_BRANCH)
                act.wait_ge(setup_dve, SETUP["rest"])
                act.activation(sin_a, rest[:, 0, :], ACT.Sin)
                act.activation(sin_b, rest[:, 1, :], ACT.Sin)
                act.activation(angle[:, :, :], rest[:, :, :], ACT.Sin, scale=0.5).then_inc(setup_act, 1)
                act.wait_ge(setup_dve, SETUP["lam_sums"])
                act.activation(neg_lam[:, 2:4], neg_lam[:, 0:2], ACT.Exp).then_inc(setup_act, 1)

            def mixer_a():
                act.wait_ge(cleared, 1)
                values(range(4), ("vA", 3), lambda i: pairs(v_a[:, i]),
                       lambda i: psum[i][:].rearrange("p (j t d) -> p j t d", j=4, t=2))
                for t in range(8):
                    act.wait_ge(block_done, done(("qkA", t)))
                    raw(("qkA", t), qk_a[:, t, :], psum[t % 4][:], HD ** -0.5 if t < 4 else 1.0)
                for n in range(5):
                    act.wait_ge(block_done, done(("lat", n)))
                    act.activation(lat[:, n, :], psum[n % 4][:], ACT.Copy).then_inc(lat_raw, 1)
                act.wait_ge(block_done, done(("kpe", 0)))
                raw(("kpe",), kpe[0:B_QK, :], psum[1][0:B_QK, :])
                act.wait_ge(lat_raw, 5)
                for n in range(5):
                    act.activation(mix[:, n, :], lat[:, n, :], ACT.Square).then_inc(squared, 1)
                deviation(("lat", 0), psum[6], Q_LORA, col("eps_rms"), 0)
                deviation(("lat", 1), psum[7], KV_LORA, col("eps_rms"), 1)

            def mixer_b():
                for h in range(B_HEADS):
                    act.wait_ge(block_done, done(("qup", h // 3)))
                    raw(("qB", h), q_b[0:B_QK, h, :], psum[h % 4][0:B_QK, :], B_QK ** -0.5)
                act.wait_ge(block_done, done(("kvk", 0)))
                for h in range(B_HEADS):
                    act.activation(k_b[0:B_NOPE, h, :], psum[h // 2][HD * (h % 2):HD * (h % 2) + HD, :],
                                   ACT.Copy).then_inc(kb_stored, 1)
                values(range(4), ("kvv", 0), lambda i: pairs(v_b[:, i]),
                       lambda i: psum[i][:].rearrange("p (j t d) -> p j t d", j=4, t=2))

            def norm_squares(i):
                for n in range(KD):
                    act.wait_ge(centered, KD * i + n + 1)
                    act.activation(square[:, n, :], z[:, n, :], ACT.Square).then_inc(squared, 1)
                deviation(("ln", i), psum[7], D, col("eps_ln"), 0)
                name = ("ln_mix_b", "ln_ffn_b")[i % 2]
                for n in range(KD):
                    act.wait_ge(normed, T["normed"][("ln", i, n)])
                    act.activation(x[:, n, :], z[:, n, :], ACT.Identity,
                                   bias=col(name, KD * (i // 2) + n)).then_inc(x_ready, 1)

            def feed_forward(i):
                layer = i // 2
                n0 = AT[("gate", layer, 0)]
                with act.Fori(0, KF // 2) as it:
                    for par in range(2):
                        w1 = COLS["conv_w"] + layer * 3 * KF + KF + par
                        b = COLS["conv_b"] + layer * KF + par
                        act.wait_ge(block_done, 4 * it + (n0 + 2 * par + 1))
                        act.activation(conv_t[:, par, :], psum[par][:], ACT.Identity,
                                       scale=cols[:, bass.ds(2 * it + w1, 1)],
                                       bias=cols[:, bass.ds(2 * it + b, 1)]).then_inc(conv_mid, 1)
                        act.wait_ge(conv_done, 2 * it + (par + 1 + KF * layer))
                        act.activation(gelu_t[:, par, :], conv_t[:, par, :], ACT.Gelu_apprx_tanh).then_inc(gelu_done, 1)

            def per_layer(layer):
                for n in range(KD):
                    act.wait_ge(block_done, done(("plegate", layer, n)))
                    act.activation(sig_p[:, n, :], psum[n % 4][:], ACT.Sigmoid).then_inc(ple_sig, 1)

            def heads_ab():
                attention([u for u in UNITS if u[0] in "AB"])

            def mixer_c():
                for half in range(2):
                    act.wait_ge(block_done, done(("vC", 4 * half + 3)))
                    for st in range(ST):
                        act.activation(v_c[:, st, S * half:S * half + S], psum[4 * half + st][:],
                                       ACT.Copy).then_inc(v_stored, 1)
                for t in range(16):
                    act.wait_ge(block_done, done(("qkC", t)))
                    raw(("qkC", t), qk_c[:, t, :], psum[t % 4][:], HD ** -0.5 if t < 8 else 1.0)

            def heads_c():
                units = [u for u in UNITS if u[0] == "C"]
                attention(units, blend=True)
                for n in range(C_HEADS):
                    act.wait_ge(attended, UNIT_AT[("C", n)] + 1)
                    act.activation(square[:, n, :], mix[:, n, :], ACT.Square).then_inc(squared, 1)
                for n in range(C_HEADS):
                    if n >= 2:
                        act.wait_ge(normed, T["normed"][("C", n - 2)])
                    deviation(("C", n), psum[n % 4], P, col("eps_ln"), n % 2)

            def rms(i):
                for n in range(KD):
                    if i == 0:
                        act.wait_ge(x_ple, KD * DEPTH - KD + n + 1)
                    else:
                        act.wait_ge(x_next, KD * (i - 1) + n + 1)
                    act.activation(square[:, n, :], x[:, n, :], ACT.Square).then_inc(squared, 1)
                deviation(("rms", i), psum[7], D, col("eps_rms"), 0)

            def store(dst, src, func=ACT.Copy, **more):
                act.activation(dst, src, func, **more).then_inc(stored, 1)

            def project_second(layer):
                at = lambda key: act.wait_ge(block_done, done(key))
                act.wait_ge(cleared, 1 + N_CLEAR * (layer + 1))
                at(("small", layer))
                store(gate_sig, psum[0][:], ACT.Sigmoid)
                store(mix[:, 6, :], psum[0][:], ACT.Identity, bias=col("fox_bias", layer))
                at(("kcvc", layer))
                store(kcvc, psum[1][:])
                at(("vsvw", layer))
                for c, v in ((0, v_s), (1, v_w)):
                    store(v[:, :, HD:2 * HD], psum[2][:].rearrange("p (t c d) -> p t c d", t=ST, c=2)[:, :, c, :])
                at(("ks", layer))
                raw(("ks", layer), ksw[:, 0, :], psum[3][:])
                at(("kw", layer))
                raw(("kw", layer), ksw[:, 1, :], psum[0][:])
                for t in range(2):
                    at(("nq", layer, t))
                    raw((f"nq{t}", layer), nq[:, t, :], psum[1 + t][:], HD ** -0.5)
                at(("w1", layer, 3))
                store(hid_k, psum[3][:, 0:CMP_N], ACT.Silu, bias=col("cmp_b1", 2 * layer))
                store(hid_v, psum[6][:, 0:CMP_N].unsqueeze(1).broadcast_to([P, 4, CMP_N]), ACT.Silu,
                      bias=col("cmp_b1", 2 * layer + 1))
                act.wait_ge(compress_step, 5 * layer + 1)
                raw(("kc", layer), kc, psum[7][:, 0:CMP_N], 1.0, col("cmp_b2k", layer))
                for t in range(2):
                    at(("fq", layer, t))
                    store(fqk[:, t, :], psum[t][:], scale=HD ** -0.5)
                for t in range(2):
                    at(("fk", layer, t))
                    store(fqk[:, 2 + t, :], psum[2 + t][:])
                at(("fv", layer, 1))
                for st in range(ST):
                    store(pairs(v_f[:, st]), psum[st][:, 0:256].rearrange("p (j t d) -> p j t d", j=2, t=2))
                for t in range(2):
                    at(("pool", layer, t))
                    store(pool_u[:, t, PAD:PAD + S], psum[t][:])
                for t in range(4):
                    at(("conv", layer, t))
                    store((conv_x if t < 2 else conv_b)[:, t % 2, :], psum[(2 + t) % 4][:])
                for t in range(8):
                    at(("sgate", layer, t))
                    store(sg[:, t, :], psum[t % 4][:], ACT.Silu)
                for n in range(6):
                    act.wait_ge(spread, 10 * layer + n + 1)
                    store(gates[:, n // 2, n % 2, :], psum[n % 4][:])
                act.wait_ge(stored, T["stored"][("fl", layer)])
                link(act.activation(mix[:, 7, :], mix[:, 6, :], ACT.Abs))
                link(act.activation(mix[:, 7, :], mix[:, 7, :], ACT.Exp, scale=-1.0))
                store(mix[:, 0, :], mix[:, 7, :], ACT.Ln, bias=ones[:, 0:1])
                for g in range(4):
                    act.wait_ge(spread, 10 * layer + 6 + g + 1)
                    rows = slice(HD * (g % 2), HD * (g % 2) + HD)
                    store(mix[rows, 2 + g // 2, :], psum[(g + 2) % 4][rows, :],
                          scale=col("pool_scale", 2 * layer + g // 2, rows))
                act.wait_ge(prepared, T["prepared"][("cmp_shift", layer)])
                store(rstd[:, 1, :], std[:, 1, :], ACT.Exp)

            def heads_second(layer):
                attention([u for u in UNITS if len(u) == 3 and u[1] == layer], causal=True)

            def merge(layer):
                n0 = AT[("merge", layer, 0, 0)]
                with act.Fori(0, KD // 4) as it:
                    for d in range(4):
                        act.wait_ge(merged, 4 * it + (d + 1 + KD * layer))
                        for i in range(N_BRANCH):
                            act.wait_ge(block_done, 20 * it + (n0 + 5 * d + i + 1))
                            act.activation(sig_m[:, d % 2, i, :], psum[i][:], ACT.Sigmoid).then_inc(sig_ready, 1)

            stages = [
                lambda: (setup(), mixer_a()), mixer_b, heads_ab, lambda: None, lambda: norm_squares(0),
                lambda: feed_forward(1), lambda: norm_squares(1), lambda: per_layer(0),
                mixer_c, heads_c, lambda: None, lambda: norm_squares(2),
                lambda: feed_forward(3), lambda: norm_squares(3), lambda: per_layer(1),
            ]
            for layer in range(DEPTH):
                stages += [lambda l=layer: rms(l), lambda l=layer: project_second(l), lambda: None,
                           lambda l=layer: heads_second(l), lambda l=layer: merge(l)]
            stages += [lambda: rms(DEPTH)]
            for stage in stages:
                stage()

        @block.vector
        def _(dve):
            linked = [0]

            def link(ins):
                linked[0] += 1
                ins.then_inc(link_dve, 1)
                dve.wait_ge(link_dve, linked[0])

            def rope(job, tile, rows, sin, n=S):
                g = ROPE_AT[job]
                dve.wait_ge(rope_perm, g + 1)
                tmp = rope_tmp[0:rows, g % 2, 0:n]
                link(dve.tensor_tensor(tmp, psum[4 + g % 2][0:rows, 0:n], sin, ALU.mult))
                dve.wait_ge(rope_cos, g + 1)
                dve.tensor_tensor(tile, tile, tmp, ALU.add).then_inc(roped, 1)

            def normalize(key, tiles, gains, buf, names):
                dve.wait_ge(std_ready, T["std"][key])
                link(dve.reciprocal(rstd[:, buf, :], std[:, buf, :]))
                for n, (dst, src) in enumerate(tiles):
                    dve.scalar_tensor_tensor(out=dst, in0=src, scalar=gains(n), in1=rstd[:, buf, :], op0=ALU.mult,
                                             op1=ALU.mult).then_inc(normed, 1)

            def attention(units, finish, blend=False, causal=False):
                turns = [(u, i) for u in units for i in range(ST)]
                comps = 2 if blend else 1

                def mixed(u, i):
                    s, t = SCORE_AT[(u, i, 0)], TURN_AT[(u, i)]
                    c = s % 8
                    dve.wait_ge(exped, s + 2)
                    link(dve.reciprocal(rownorm[:, c:c + 2], rowsum[:, c:c + 2]))
                    link(dve.tensor_tensor(rownorm[:, c + 1:c + 2], rownorm[:, c + 1:c + 2], neg_lam[:, 5:6], ALU.mult))
                    p0, p1 = prob[:, s % 4, :], prob[:, (s + 1) % 4, :]
                    link(dve.tensor_scalar(p0, p0, rownorm[:, c:c + 1], None, ALU.mult))
                    dve.scalar_tensor_tensor(out=p0, in0=p1, scalar=rownorm[:, c + 1:c + 2], in1=p0, op0=ALU.mult,
                                             op1=ALU.add).then_inc(blended, 1)

                pending = []
                for n, (u, i) in enumerate(turns):
                    for c in range(comps):
                        s = SCORE_AT[(u, i, c)]
                        w = (i + 1) * P if causal else S
                        dve.wait_ge(scored, s + 1)
                        dve.tensor_reduce(negmax[:, s % 8:s % 8 + 1], psum[s % 4][:, 0:w], AX_X, ALU.max,
                                          negate=True).then_inc(maxed, 1)
                    if blend and n:
                        mixed(*turns[n - 1])
                    if pending and i == 2:
                        finish(pending.pop(0))
                    if i == ST - 1:
                        pending.append(u)
                if blend:
                    mixed(*turns[-1])
                for u in pending:
                    finish(u)

            def divided(u, dst, odd, gate=None, add=False):
                n = UNIT_AT[u]
                own, other = (slice(HD, P), slice(0, HD)) if odd else (slice(0, HD), slice(HD, P))
                bank = psum[6 + n % 2]
                inv = rope_tmp[own, 0, :]
                dve.wait_ge(weighed, n + 1)
                link(dve.reciprocal(inv, bank[other, :]))
                if gate is not None:
                    link(dve.tensor_tensor(inv, inv, gate[own], ALU.mult))
                if add:
                    link(dve.tensor_tensor(inv, bank[own, :], inv, ALU.mult))
                    dve.tensor_tensor(dst[own], dst[own], inv, ALU.add).then_inc(attended, 1)
                else:
                    dve.tensor_tensor(dst[own], bank[own, :], inv, ALU.mult).then_inc(attended, 1)

            def setup():
                dve.nop().then_inc(hid_ready, 2)
                dve.nop().then_inc(merged, 2)
                dve.wait_ge(inputs_in, 16 * N_INPUTS)
                n = [0]

                def step(ins):
                    n[0] += 1
                    ins.then_inc(setup_dve, 1)
                    dve.wait_ge(setup_dve, n[0])

                step(dve.tensor_copy(pos_f, pos_raw))
                for j, name in ((0, "inv_a"), (1, "inv_b")):
                    dve.tensor_scalar(angle[:, j, :], pos_f, col(name), None, ALU.mult)
                step(dve.memset(std[:, 0, 0:1], 0.0))
                step(dve.tensor_scalar(turns_[:, :, :], angle[:, :, :], 1.0 / (2 * math.pi), 12582912.0, ALU.mult, ALU.add))
                step(dve.tensor_scalar(turns_[:, :, :], turns_[:, :, :], -12582912.0, None, ALU.add))
                step(dve.scalar_tensor_tensor(out=rest[:, :, :], in0=turns_[:, :, :], scalar=-TWO_PI[0],
                                              in1=angle[:, :, :], op0=ALU.mult, op1=ALU.add))
                for part in TWO_PI[1:]:
                    step(dve.scalar_tensor_tensor(out=rest[:, :, :], in0=turns_[:, :, :], scalar=-part,
                                                  in1=rest[:, :, :], op0=ALU.mult, op1=ALU.add))
                step(dve.tensor_scalar(rest[:, :, :], rest[:, :, :], 3.1415925, -3.1415925, ALU.min, ALU.max))
                assert n[0] == SETUP["rest"], n
                dve.tensor_tensor(lam_in[:, 0:HD], lam_in[:, 0:HD], lam_in[:, HD:2 * HD], ALU.mult)
                step(dve.tensor_tensor(lam_in[:, 2 * HD:3 * HD], lam_in[:, 2 * HD:3 * HD], lam_in[:, 3 * HD:4 * HD], ALU.mult))
                step(dve.tensor_reduce(neg_lam[:, 0:2], lam_in.rearrange("p (a b) -> p a b", a=2)[:, :, 0:HD], AX_X, ALU.add))
                assert n[0] == SETUP["lam_sums"], n
                dve.wait_ge(setup_act, 1)
                step(dve.tensor_tensor(angle[:, :, :], angle[:, :, :], angle[:, :, :], ALU.mult))
                step(dve.tensor_scalar(early[:, ST * S:ST * S + 4 * S].rearrange("p (j c s) -> p j c s", j=2, c=2)[:, :, 0, :],
                                       angle[:, :, :], -2.0, 1.0, ALU.mult, ALU.add))
                dve.wait_ge(setup_act, 2)
                step(dve.tensor_tensor(neg_lam[:, 4:5], neg_lam[:, 3:4], neg_lam[:, 2:3], ALU.subtract))
                dve.tensor_scalar(neg_lam[:, 5:6], neg_lam[:, 4:5], -LAMBDA_INIT, None, ALU.add)
                dve.tensor_scalar(neg_lam[:, 6:7], col("subln"), 1.0 - LAMBDA_INIT, None, ALU.mult)
                dve.tensor_copy(ident_bf[:], ident).then_inc(constants_bf, 1)
                dve.tensor_copy(tri_bf[:], masks_in[:, S:S + P]).then_inc(constants_bf, 1)
                dve.tensor_copy(cmp_bias_bf[:], masks_in[:, 0:S]).then_inc(constants_bf, 1)
                dve.wait_ge(constants_bf, 3)

            def mixer_a():
                for t in range(8):
                    rope(("qkA", t), qk_a[:, t, :], P, sin_a)
                normalize(("lat", 0), [(lat[:, n, :], lat[:, n, :]) for n in range(3)], lambda n: col("q_norm", n), 0, None)
                normalize(("lat", 1), [(lat[:, 3 + n, :], lat[:, 3 + n, :]) for n in range(2)],
                          lambda n: col("kv_norm", n), 1, None)
                rope(("kpe",), kpe[0:B_QK, :], B_QK, sin_b[0:B_QK, :])
                dve.wait_ge(roped, ROPE_AT[("kpe",)] + 1)
                dve.tensor_copy(k_b[B_NOPE:B_QK, :, :], kpe[B_NOPE:B_QK, :].unsqueeze(1).broadcast_to(
                    [B_ROPE, B_HEADS, S])).then_inc(kpe_spread, 1)

            def mixer_b():
                for h in range(B_HEADS):
                    rope(("qB", h), q_b[0:B_QK, h, :], B_QK, sin_b[0:B_QK, :])

            def heads_ab():
                attention([u for u in UNITS if u[0] in "AB"],
                          lambda u: divided(u, mix[:, (0 if u[0] == "A" else 4) + u[1] // 2, :], u[1] % 2))

            def residual(i):
                layer = i // 2
                for n in range(KD):
                    if i % 2 == 0:
                        dve.wait_ge(block_done, done(("mixout", layer, n)))
                        bank = psum[n % 4]
                    else:
                        dve.wait_ge(block_done, done(("down", layer, n // 4, KF // 2 - 1)))
                        bank = psum[4 + n] if n < 4 else psum[n - 4]
                    dve.scalar_tensor_tensor(out=z[:, n, :], in0=x[:, n, :], scalar=ALPHA, in1=bank[:], op0=ALU.mult,
                                             op1=ALU.add).then_inc(z_ready, 1)

            def norm(i):
                dve.wait_ge(mean_ready, i + 1)
                for n in range(KD):
                    dve.scalar_tensor_tensor(out=z[:, n, :], in0=psum[6][:], scalar=-1.0 / D, in1=z[:, n, :],
                                             op0=ALU.mult, op1=ALU.add).then_inc(centered, 1)
                name = ("ln_mix_g", "ln_ffn_g")[i % 2]
                normalize(("ln", i), [(z[:, n, :], z[:, n, :]) for n in range(KD)],
                          lambda n: col(name, KD * (i // 2) + n), 0, None)

            def feed_forward(i):
                layer = i // 2
                n0 = AT[("gate", layer, 0)]
                w = COLS["conv_w"] + layer * 3 * KF
                with dve.Fori(0, KF // 2) as it:
                    for par in range(2):
                        f1 = par + 1 + KF * layer
                        c, a = conv_t[:, par, :], psum[par]
                        dve.wait_ge(conv_mid, 2 * it + f1)
                        dve.scalar_tensor_tensor(out=c[:, 1:S], in0=a[:, 0:S - 1],
                                                 scalar=cols[:, bass.ds(2 * it + (w + par), 1)], in1=c[:, 1:S],
                                                 op0=ALU.mult, op1=ALU.add).then_inc(conv_mid2, 1)
                        dve.wait_ge(conv_mid2, 2 * it + f1)
                        dve.scalar_tensor_tensor(out=c[:, 0:S - 1], in0=a[:, 1:S],
                                                 scalar=cols[:, bass.ds(2 * it + (w + 2 * KF + par), 1)], in1=c[:, 0:S - 1],
                                                 op0=ALU.mult, op1=ALU.add).then_inc(conv_done, 1)
                        dve.wait_ge(gelu_done, 2 * it + f1)
                        dve.wait_ge(block_done, 4 * it + (n0 + 2 * par + 2))
                        dve.tensor_tensor(hid[:, 2 * it + par, :], gelu_t[:, par, :], psum[2 + par][:],
                                          ALU.mult).then_inc(hid_ready, 1)

            def per_layer(layer):
                for n in range(KD):
                    dve.wait_ge(ple_sig, KD * layer + n + 1)
                    dve.tensor_tensor(sig_p[:, n, :], sig_p[:, n, :], psum[4 + n % 4][:], ALU.mult).then_inc(ple_term, 1)
                dve.wait_ge(block_done, done(("plegate", layer, KD - 1)))
                dve.wait_ge(ple_term, KD * layer + KD)
                for n in range(KD):
                    dve.tensor_tensor(x[:, n, :], x[:, n, :], sig_p[:, n, :], ALU.add).then_inc(x_ple, 1)

            def mixer_c():
                for t in range(16):
                    rope(("qkC", t), qk_c[:, t, :], P, sin_a)

            def heads_c():
                def finish(u):
                    n = UNIT_AT[u]
                    dve.wait_ge(weighed, n + 1)
                    dve.tensor_copy(mix[:, u[1], :], psum[6 + n % 2][:]).then_inc(attended, 1)

                attention([u for u in UNITS if u[0] == "C"], finish, blend=True)
                for n in range(C_HEADS):
                    normalize(("C", n), [(mix[:, n, :], mix[:, n, :])], lambda _: neg_lam[:, 6:7], n % 2, None)

            def rms(i):
                dst = h2 if i < DEPTH else z
                name, lo = ("norm2_g", KD * i) if i < DEPTH else ("final_g", 0)
                normalize(("rms", i), [(dst[:, n, :], x[:, n, :]) for n in range(KD)], lambda n: col(name, lo + n), 0, None)

            def project_second(layer):
                stored_at = lambda key: dve.wait_ge(stored, T["stored"][(key, layer)])
                dve.wait_ge(cleared, 1 + N_CLEAR * (layer + 1))
                stored_at("kcvc")
                by_16 = kcvc.rearrange("p (n l) -> p l n", l=CMP_STRIDE)
                pos = cmp_pos[:, layer * CMP_LEN:layer * CMP_LEN + CMP_LEN]
                for j in range(2):
                    ins = dve.tensor_tensor(
                        blocks_x[:, 16 * j:16 * j + 16, 0:CMP_N - 1], by_16[:, :, j:j + CMP_N - 1],
                        pos[:, 16 * j:16 * j + 16].unsqueeze(2).broadcast_to([P, 16, CMP_N - 1]), ALU.add)
                ins.then_inc(prepared, 1)
                cos2, sin2 = tab("cos2", S), tab("sin2", S)
                rope(("ks", layer), ksw[:, 0, :], P, sin2)
                rope(("kw", layer), ksw[:, 1, :], P, sin2)
                rope(("nq0", layer), nq[:, 0, :], P, sin2)
                rope(("nq1", layer), nq[:, 1, :], P, sin2)
                dve.wait_ge(compress_step, 5 * layer + 2)
                for h in range(4):
                    rows = slice(32 * h, 32 * h + 32)
                    ins = dve.tensor_tensor(vc_bd[rows, h // 2, HD * (h % 2):HD * (h % 2) + HD], psum[3][rows, 0:HD],
                                            b2v[rows, layer * HD:layer * HD + HD], ALU.add)
                ins.then_inc(prepared, 1)
                rope(("kc", layer), kc, P, tab("sin2c", CMP_N), CMP_N)
                stored_at("pool1")
                u, a, b = pool_u, pool_a, pool_b
                end = PAD + S
                step = lambda dst, src, w: link(dve.tensor_tensor(dst[:, :, 2 * w:end], src[:, :, 2 * w:end],
                                                                  src[:, :, w:end - w], ALU.add))

                def mean(src, g):
                    rows = slice(HD * (g % 2), HD * (g % 2) + HD)
                    link(dve.tensor_tensor(mix[rows, 2 + g // 2, :], src[rows, g // 2, PAD:end],
                                           inv_count[rows, g // 2, :], ALU.mult))

                step(a, u, 1)
                step(b, a, 2)
                mean(a, 0)
                mean(b, 1)
                step(a, b, 4)
                step(b, a, 8)
                mean(a, 2)
                mean(b, 3)
                dve.tensor_tensor(mix[:, 2:4, :], mix[:, 2:4, :], u[:, :, PAD:end], ALU.subtract).then_inc(prepared, 1)
                stored_at("cb1")
                for t in range(2):
                    dve.wait_ge(block_done, done(("conv", layer, 4 + t)))
                    dve.tensor_tensor(conv_u[:, t, 2:2 + S], psum[2 + t][:],
                                      conv_x[:, t, :], ALU.mult).then_inc(prepared, 1)
                dve.wait_ge(prepared, T["prepared"][("cu1", layer)])
                for t in range(2):
                    y = mix[:, 4 + t, :]
                    wcol = lambda k: col("conv2_w", 6 * layer + 2 * k + t)
                    link(dve.tensor_scalar(y, conv_u[:, t, 0:S], wcol(0), None, ALU.mult))
                    for k in (1, 2):
                        link(dve.scalar_tensor_tensor(out=y, in0=conv_u[:, t, k:k + S], scalar=wcol(k), in1=y,
                                                      op0=ALU.mult, op1=ALU.add))
                    dve.tensor_tensor(y, y, conv_b[:, t, :], ALU.mult).then_inc(prepared, 1)
                stored_at("ln")
                link(dve.scalar_tensor_tensor(out=mix[:, 6, :], in0=mix[:, 6, :], scalar=0.0, in1=mix[:, 0, :],
                                              op0=ALU.min, op1=ALU.subtract))
                link(dve.tensor_tensor_scan(mix[:, 7, :], mix[:, 6, :], mix[:, 1, :], 0.0, ALU.add, ALU.add))
                dve.tensor_scalar(cq, mix[:, 7, :], col("cq_mul"), col("cq_add"), ALU.mult, ALU.add)
                dve.tensor_scalar(ck, mix[:, 7, :], col("ck_mul"), col("ck_add"), ALU.mult, ALU.add).then_inc(prepared, 1)
                dve.wait_ge(compress_step, 5 * layer + 3)
                for odd in range(2):
                    s8 = psum[6 + odd][:, 0:2 * P].rearrange("p (a n) -> p a n", n=CMP_N)
                    best = cmp_negmax[:, 8 * odd:8 * odd + 8]
                    link(dve.tensor_reduce(best, s8, AX_X, ALU.max, negate=True))
                    ins = dve.tensor_tensor(
                        std[:, 1, :].rearrange("p (a b n) -> p a b n", b=2, n=CMP_N)[:, :, odd, :], s8,
                        best.unsqueeze(2).broadcast_to([P, 8, CMP_N]), ALU.add)
                ins.then_inc(prepared, 1)
                dve.wait_ge(compress_step, 5 * layer + 4)
                dve.tensor_tensor(prob[:, 3, :], psum[7][:], tab("cmp_mask", S), ALU.mult).then_inc(prepared, 1)
                dve.wait_ge(compress_step, 5 * layer + 5)
                for j in range(2):
                    inv = rope_tmp[:, j, :]
                    link(dve.tensor_scalar(inv, psum[2 + j][:], 0.5, None, ALU.max))
                    link(dve.reciprocal(inv, inv))
                    link(dve.tensor_tensor(inv, inv, gates[:, 0, j, :], ALU.mult))
                    dve.tensor_tensor(mix[:, j, :], psum[j][:], inv, ALU.mult).then_inc(prepared, 1)
                dve.wait_ge(prepared, T["prepared"][("cmp_out", layer)])

            def heads_second(layer):
                def finish(u):
                    h = u[2]
                    if u[0] == "fox":
                        divided(u, mix[:, 6 + h // 2, :], h % 2)
                    else:
                        divided(u, mix[:, h // 2, :], h % 2, gates[:, 1 if u[0] == "slc" else 2, h // 2, :], True)

                attention([u for u in UNITS if len(u) == 3 and u[1] == layer], finish, causal=True)

            def merge(layer):
                n0 = AT[("merge", layer, 0, 0)]
                with dve.Fori(0, KD // 4) as it:
                    for d in range(4):
                        t = sig_m[:, d % 2]
                        dve.wait_ge(block_done, 20 * it + (n0 + 5 * d + N_BRANCH + 1))
                        dve.wait_ge(sig_ready, 16 * it + (4 * d + 4 + 4 + 32 * layer))
                        for i in range(N_BRANCH):
                            ins = dve.tensor_tensor(t[:, i, :], t[:, i, :], psum[4 + i][:], ALU.mult)
                        ins.then_inc(merge_link, 1)
                        dve.wait_ge(merge_link, 8 * it + (2 * d + 1 + 16 * layer))
                        ins = dve.tensor_tensor(t[:, 0:2, :], t[:, 0:2, :], t[:, 2:4, :], ALU.add)
                        ins.then_inc(merge_link, 1)
                        dve.wait_ge(merge_link, 8 * it + (2 * d + 2 + 16 * layer))
                        dve.tensor_tensor(acc[:, 4 * it + d, :], t[:, 0, :], t[:, 1, :], ALU.add).then_inc(merged, 1)
                for n in range(KD):
                    dve.wait_ge(block_done, done(("out2", layer, n)))
                    dve.tensor_tensor(x[:, n, :], psum[n % 4][:], x[:, n, :], ALU.add).then_inc(x_next, 1)

            turns_ = turns
            stages = [
                lambda: (setup(), mixer_a()), mixer_b, heads_ab, lambda: residual(0), lambda: norm(0),
                lambda: feed_forward(1), lambda: (residual(1), norm(1)), lambda: per_layer(0),
                mixer_c, heads_c, lambda: residual(2), lambda: norm(2),
                lambda: feed_forward(3), lambda: (residual(3), norm(3)), lambda: per_layer(1),
            ]
            for layer in range(DEPTH):
                stages += [lambda l=layer: rms(l), lambda l=layer: project_second(l), lambda: None,
                           lambda l=layer: heads_second(l), lambda l=layer: merge(l)]
            stages += [lambda: rms(DEPTH)]
            for stage in stages:
                stage()

        @block.gpsimd
        def _(pool):
            def rope(job, tile, cos):
                g = ROPE_AT[job]
                pool.wait_ge(rope_perm, g + 1)
                pool.tensor_tensor(tile, tile, cos, ALU.mult).then_inc(rope_cos, 1)

            def mixer_a():
                pool.memset(v_a.rearrange("p t j (c d) -> p (t j) c d", c=3)[:, :, 1, :], 1.0)
                pool.memset(v_b.rearrange("p t j (c d) -> p (t j) c d", c=3)[:, :, 1, :], 1.0).then_inc(cleared, 1)
                pool.wait_ge(setup_dve, SETUP["all"])
                for t in range(8):
                    rope(("qkA", t), qk_a[:, t, :], cos_a)
                rope(("kpe",), kpe[0:B_QK, :], cos_b[0:B_QK, :])

            def mixer_b():
                for h in range(B_HEADS):
                    rope(("qB", h), q_b[0:B_QK, h, :], cos_b[0:B_QK, :])

            def per_layer(layer):
                pool.wait_ge(x_ready, KD * (2 * layer) + KD)
                pool.dma_start(p_in_t, dram["p_t"][:, layer * 2 * S:layer * 2 * S + 2 * S].rearrange(
                    "p (t s) -> p t s", t=2)).then_inc(p_loaded, 16)

            def mixer_c():
                for t in range(16):
                    rope(("qkC", t), qk_c[:, t, :], cos_a)

            def project_second(layer):
                if layer == 0:
                    pool.wait_ge(x_ple, KD * DEPTH)
                else:
                    pool.wait_ge(x_next, KD * layer)
                for v in (v_s, v_w):
                    pool.memset(v.rearrange("p t (c d) -> p t c d", c=3)[:, :, 0:3:2, :], 1.0).then_inc(cleared, 1)
                pool.memset(v_f.rearrange("p t j (c d) -> p (t j) c d", c=3)[:, :, 1, :], 1.0).then_inc(cleared, 1)
                pool.memset(blocks_x[:, :, CMP_N - 1:CMP_N], 0.0).then_inc(cleared, 1)
                pool.memset(vc_bd, 0.0).then_inc(cleared, 1)
                pool.memset(pool_u[:, :, 0:PAD], 0.0).then_inc(cleared, 1)
                pool.memset(pool_a[:, :, 0:PAD], 0.0).then_inc(cleared, 1)
                pool.memset(pool_b[:, :, 0:PAD], 0.0).then_inc(cleared, 1)
                pool.memset(conv_u[:, :, 0:2], 0.0).then_inc(cleared, 1)
                pool.memset(mix[:, 1, :], 0.0).then_inc(cleared, 1)
                for key, tile in (("ks", ksw[:, 0, :]), ("kw", ksw[:, 1, :]), ("nq0", nq[:, 0, :]), ("nq1", nq[:, 1, :])):
                    rope((key, layer), tile, tab("cos2", S))
                rope(("kc", layer), kc, tab("cos2c", CMP_N))

            def gate(layer):
                for t in (2, 3, 4, 5, 0, 1, 6, 7):
                    if t in (2, 3):
                        pool.wait_ge(stored, T["stored"][("pm3", layer)])
                    elif t in (4, 5):
                        pool.wait_ge(prepared, T["prepared"][("convy1", layer)])
                    elif t in (0, 1):
                        pool.wait_ge(attended, UNIT_AT[("win", layer, 3)] + 1)
                    else:
                        pool.wait_ge(attended, UNIT_AT[("fox", layer, 3)] + 1)
                    pool.tensor_tensor(mix[:, t, :], mix[:, t, :], sg[:, t, :], ALU.mult).then_inc(gated, 1)

            stages = [mixer_a, mixer_b] + [lambda: None] * 3 + [lambda: per_layer(0)] + [lambda: None] * 2
            stages += [mixer_c] + [lambda: None] * 3 + [lambda: per_layer(1)] + [lambda: None] * 2
            for layer in range(DEPTH):
                stages += [lambda: None, lambda l=layer: project_second(l), lambda: None,
                           lambda l=layer: gate(l), lambda: None]
            for stage in stages:
                stage()


def kernel(**inputs):
    import concourse.bacc as bacc
    from concourse.bass_utils import run_bass_kernel_spmd

    nc = bacc.Bacc("TRN2", target_bir_lowering=False, num_devices=1)
    arrays = host_layout({k: np.asarray(v) for k, v in inputs.items()})
    dram = {name: nc.dram_tensor("in_" + name, a.shape, mybir.dt.from_np(a.dtype), kind="ExternalInput").ap()
            for name, a in arrays.items()}
    out = nc.dram_tensor("out", (P, KD, S), F32, kind="ExternalOutput").ap()
    build(nc, dram, out)
    got = run_bass_kernel_spmd(nc, [{"in_" + n: a for n, a in arrays.items()}], core_ids=[0]).results[0]["out"]
    return np.ascontiguousarray(got.transpose(2, 1, 0).reshape(1, S, D))
```

```python
import math
from contextlib import ExitStack

import numpy as np

import concourse.bass as bass
from concourse import mybir

F32 = mybir.dt.float32
F32R = mybir.dt.float32r
BF16 = mybir.dt.bfloat16
I32 = mybir.dt.int32
ALU = mybir.AluOpType
ACT = mybir.ActivationFunctionType
AX_X = mybir.AxisListType.X

P = 128
S = 512
D = 1024
KD = D // P
ST = S // P
DEPTH = 2
HD = 64
A_HEADS = 8
B_HEADS, B_NOPE, B_ROPE, B_QK = 8, 64, 32, 96
Q_LORA, KV_LORA = 384, 256
C_HEADS = 8
FF = 256 * math.ceil(8 * D / 3 / 256)
KF = FF // P
PLE = 256
LN_EPS, RMS_EPS = 1e-5, 1e-6
ALPHA = (2 * DEPTH) ** 0.25
LAMBDA_INIT = 0.8 - 0.6 * math.exp(-0.3)
ROPE_THETA, MASK = 500000.0, -1e30
N_BRANCH, BW = 4, 256
CMP_N, CMP_LEN, CMP_STRIDE = 32, 32, 16
PAD = 16
RING = 2
BLK = 1024
KB = 256


class Tally:

    def __init__(self, keys=()):
        self.value = {}
        for key in keys:
            self.add(key)

    def add(self, key):
        assert key not in self.value, key
        self.value[key] = len(self.value) + 1

    def __getitem__(self, key):
        return self.value[key]


def block_plan():
    keys = []
    keys += [("vA", i) for i in range(4)] + [("qkA", t) for t in range(8)]
    keys += [("lat", t) for t in range(5)] + [("kpe", 0)]
    keys += [("qup", i) for i in range(3)] + [("kvk", 0), ("kvv", 0)]
    for layer in range(DEPTH):
        if layer == 1:
            keys += [("vC", i) for i in range(8)] + [("qkC", t) for t in range(16)]
        keys += [("mixout", layer, n) for n in range(KD)]
        for f in range(KF):
            keys += [("gate", layer, f), ("up", layer, f)]
        keys += [("down", layer, h, i) for h in range(2) for i in range(KF // 2)]
        for half in range(2):
            keys += [("pleproj", layer, half)] + [("plegate", layer, half * 4 + n) for n in range(4)]
    for layer in range(DEPTH):
        keys += [("small", layer), ("kcvc", layer), ("vsvw", layer), ("ks", layer), ("kw", layer)]
        keys += [("nq", layer, t) for t in range(2)] + [("w1", layer, i) for i in range(4)]
        keys += [("fq", layer, t) for t in range(2)] + [("fk", layer, t) for t in range(2)]
        keys += [("fv", layer, t) for t in range(2)] + [("pool", layer, t) for t in range(2)]
        keys += [("conv", layer, t) for t in range(6)] + [("sgate", layer, t) for t in range(8)]
        for n in range(KD):
            keys += [("merge", layer, n, i) for i in range(N_BRANCH)] + [("branch", layer, n)]
        keys += [("out2", layer, n) for n in range(KD)]
    return keys


BLOCKS = block_plan()
AT = {key: n for n, key in enumerate(BLOCKS)}

COLS = {}
_at = 0
for _name, _width in [
    ("q_norm", 3), ("kv_norm", 2), ("subln", 1), ("ln_mix_g", 16), ("ln_mix_b", 16), ("conv_w", 2 * 3 * KF),
    ("conv_b", 2 * KF), ("ln_ffn_g", 16), ("ln_ffn_b", 16), ("norm2_g", 16), ("fox_bias", 2), ("cmp_b1", 4),
    ("cmp_b2k", 2), ("pool_scale", 4), ("conv2_w", 12), ("final_g", 8), ("inv_a", 1), ("inv_b", 1),
    ("eps_ln", 1), ("eps_rms", 1), ("cq_mul", 1), ("cq_add", 1), ("ck_mul", 1), ("ck_add", 1),
]:
    COLS[_name] = _at
    _at += _width
NCOLS = _at

TABS = {}
_at = 0
for _name, _width in [
    ("ident", P), ("ones", P), ("perm_a", P), ("perm_b", P), ("count", ST * S), ("cmp_bias", S), ("tri", P), ("cos2", S), ("sin2", S),
    ("cos2c", CMP_N), ("sin2c", CMP_N), ("inv_count", 2 * S), ("cmp_mask", S),
    ("sel", 6 * P), ("ones_bd", 2 * P),
]:
    TABS[_name] = _at
    _at += _width
NTABS = _at


def _tile(w):
    k, n = w.shape
    return w.reshape(k // P, P, n).transpose(1, 0, 2).reshape(P, -1)


def _column(v):
    return v.reshape(-1, P).T


def weight_stream(a):
    w_in, w_qkv = a["ab_w_in"][0], a["c_w_qkv"][0]
    o3 = 3 * A_HEADS * HD
    made = np.zeros((len(BLOCKS), P, BLK), np.float32)
    split2 = np.cumsum([256, 384, 12, 256, 768, 768, 4, 1024, 4096])

    def put(n, w):
        made[n, :, :w.shape[1]] = w

    for n, key in enumerate(BLOCKS):
        kind, at = key[0], key[1:]
        if kind == "vA":
            put(n, _tile(w_in[256 * at[0]:256 * at[0] + 256, 1024:1536]))
        elif kind == "qkA":
            put(n, _tile(w_in[:, P * at[0]:P * at[0] + P]))
        elif kind == "lat":
            put(n, _tile(w_in[:, o3 + P * at[0]:o3 + P * at[0] + P]))
        elif kind == "kpe":
            w = np.zeros((D, B_QK), np.float32)
            w[:, B_NOPE:] = w_in[:, o3 + Q_LORA + KV_LORA:]
            put(n, _tile(w))
        elif kind == "qup":
            heads = range(3 * at[0], min(3 * at[0] + 3, B_HEADS))
            put(n, np.concatenate([_tile(a["ab_w_q_up"][0][:, B_QK * h:B_QK * h + B_QK]) for h in heads], 1))
        elif kind == "kvk":
            w = a["ab_w_kv_up"][0].reshape(KV_LORA, B_HEADS // 2, 2, 2, HD)[:, :, :, 0]
            put(n, np.concatenate([_tile(w[:, j].reshape(KV_LORA, P)) for j in range(B_HEADS // 2)], 1))
        elif kind == "kvv":
            put(n, _tile(a["ab_w_kv_up"][0].reshape(KV_LORA, B_HEADS, 2, HD)[:, :, 1].reshape(KV_LORA, -1)))
        elif kind == "vC":
            half, i = divmod(at[0], 4)
            put(n, _tile(w_qkv[256 * i:256 * i + 256, 2048 + S * half:2048 + S * half + S]))
        elif kind == "qkC":
            put(n, _tile(w_qkv[:, P * at[0]:P * at[0] + P]))
        elif kind == "mixout":
            put(n, _tile((a["ab_w_out"][0], a["c_w_out"][0])[at[0]][:, P * at[1]:P * at[1] + P]))
        elif kind in ("gate", "up"):
            put(n, _tile(a["ffn_w_" + kind][at[0]][:, P * at[1]:P * at[1] + P]))
        elif kind == "down":
            layer, half, i = at
            put(n, _tile(a["ffn_w_down"][layer][256 * i:256 * i + 256, S * half:S * half + S]))
        elif kind == "plegate":
            put(n, _tile(a["ple_w_gate"][at[0]][:, P * at[1]:P * at[1] + P]))
        elif kind == "pleproj":
            put(n, _tile(a["ple_w_proj"][at[0]][:, S * at[1]:S * at[1] + S]))
        elif kind == "w1":
            w = a["cmp_w1_2"][at[0]].reshape(2, CMP_LEN, HD, P)[:, 8 * at[1]:8 * at[1] + 8]
            put(n, w.transpose(0, 2, 1, 3).reshape(P, BLK))
        elif kind == "branch":
            w = a["w_branch_2"][at[0]][:, :, P * at[1]:P * at[1] + P]
            put(n, _tile(w.reshape(N_BRANCH * BW, P)))
        elif kind == "out2":
            put(n, _tile(a["w_out_2"][at[0]][:, P * at[1]:P * at[1] + P]))
        else:
            nq, kv, ng, pool, conv, fox, ff, gate, merge = np.split(a["w_in_2"][at[0]], split2[:-1], axis=1)
            if kind == "small":
                w = np.zeros((D, P), np.float32)
                w[:, 0::32], w[:, 1::32], w[:, 8:20] = ff, ff, ng
            elif kind == "kcvc":
                w = kv[:, 0:P]
            elif kind == "vsvw":
                w = np.concatenate([kv[:, 192:256], kv[:, 320:384]], 1)
            elif kind == "ks":
                w = np.concatenate([kv[:, 128:192]] * 2, 1)
            elif kind == "kw":
                w = np.concatenate([kv[:, 256:320]] * 2, 1)
            elif kind == "nq":
                w = nq[:, P * at[1]:P * at[1] + P]
            elif kind == "fq":
                w = fox[:, P * at[1]:P * at[1] + P]
            elif kind == "fk":
                w = fox[:, 256 + P * at[1]:256 + P * at[1] + P]
            elif kind == "fv":
                w = fox[S * at[1]:S * at[1] + S, 512:768]
            elif kind == "pool":
                w = pool[:, P * at[1]:P * at[1] + P]
            elif kind == "conv":
                w = conv[:, P * at[1]:P * at[1] + P]
            elif kind == "sgate":
                w = gate[:, P * at[1]:P * at[1] + P]
            elif kind == "merge":
                lo = D * at[2] + P * at[1]
                w = merge[:, lo:lo + P]
            put(n, _tile(w))
    return made


def column_pack(a):
    made = np.zeros((P, NCOLS), np.float32)

    def put(name, v):
        made[:, COLS[name]:COLS[name] + v.shape[1]] = v

    put("q_norm", _column(a["ab_q_norm"][0]))
    put("kv_norm", _column(a["ab_kv_norm"][0]))
    put("subln", _column(a["c_subln"][0]))
    for name in ("ln_mix_g", "ln_mix_b", "ln_ffn_g", "ln_ffn_b"):
        put(name, _column(a[name].reshape(-1)))
    put("conv_w", _column(a["ffn_conv_w"].reshape(-1)))
    put("conv_b", _column(a["ffn_conv_b"].reshape(-1)))
    put("norm2_g", _column(a["norm_g_2"].reshape(-1)))
    bias = np.zeros((P, DEPTH), np.float32)
    bias[0::32], bias[1::32] = a["fox_f_bias_2"].T, a["fox_f_bias_2"].T
    put("fox_bias", bias)
    put("cmp_b1", _column(a["cmp_b1_2"].reshape(-1)))
    put("cmp_b2k", np.concatenate([a["cmp_b2_2"][:, 0].T] * 2, 0))
    put("pool_scale", _column(a["pool_scale_2"].reshape(-1)))
    put("conv2_w", _column(a["conv_w_2"].reshape(-1)))
    put("final_g", _column(a["final_norm_g_2"]))
    for name, rot, width in (("inv_a", HD // 4, HD), ("inv_b", B_ROPE, B_QK)):
        inv = (np.float32(1.0) / np.float32(ROPE_THETA) ** (np.arange(0, rot, 2, dtype=np.float32) / np.float32(rot)))
        col = np.zeros(P, np.float32)
        for lo in ((0, HD) if name == "inv_a" else (B_NOPE,)):
            col[lo:lo + rot] = np.concatenate([inv, inv])
        put(name, col[:, None])
    put("eps_ln", np.full((P, 1), LN_EPS, np.float32))
    put("eps_rms", np.full((P, 1), RMS_EPS, np.float32))
    for h in range(4):
        made[32 * h, COLS["cq_mul"]] = 1.0
        made[32 * h + 1, COLS["cq_add"]] = 1.0
        made[32 * h, COLS["ck_add"]] = 1.0
        made[32 * h + 1, COLS["ck_mul"]] = -1.0
    return made


def table_pack():
    made = np.zeros((P, NTABS), np.float32)

    def put(name, v):
        made[:v.shape[0], TABS[name]:TABS[name] + v.shape[1]] = v

    def swap(lo, half, m):
        for i in range(half):
            m[lo + half + i, lo + i] = -1.0
            m[lo + i, lo + half + i] = 1.0

    put("ident", np.eye(P, dtype=np.float32))
    put("ones", np.ones((P, P), np.float32))
    perm = np.zeros((P, P), np.float32)
    swap(0, 8, perm)
    swap(HD, 8, perm)
    put("perm_a", perm)
    perm = np.zeros((P, P), np.float32)
    swap(B_NOPE, 16, perm)
    put("perm_b", perm)
    i, j = np.arange(S)[:, None], np.arange(S)[None, :]
    count = np.zeros((S, S))
    for window, dilation in ((128, 1), (512, 4), (2048, 16)):
        side = window // (2 * dilation)
        count += ((i - j) % dilation == 0) & (np.abs(i - j) <= side * dilation)
    put("count", count.astype(np.float32).reshape(ST, P, S).transpose(1, 0, 2).reshape(P, -1))
    half = HD // 8
    inv = np.float32(ROPE_THETA) ** (-np.arange(half, dtype=np.float32) / np.float32(half))
    full = np.zeros(P, np.float32)
    for lo in (0, HD):
        full[lo:lo + 2 * half] = np.concatenate([inv, inv])
    for tag, pos in (("", np.arange(S)), ("c", np.arange(CMP_N) * CMP_STRIDE + CMP_LEN - 1)):
        ang = (pos.astype(np.float32)[None, :] * full[:, None]).astype(np.float64)
        put("cos2" + tag, np.cos(ang).astype(np.float32))
        put("sin2" + tag, np.sin(ang).astype(np.float32))
    inv_count = np.zeros((P, 2, S), np.float32)
    for g, w in enumerate((2, 4, 8, 16)):
        inv_count[64 * (g % 2):64 * (g % 2) + 64, g // 2] = 1.0 / np.minimum(np.arange(1, S + 1), w)
    put("inv_count", inv_count.reshape(P, -1))
    n = np.arange(CMP_N)
    end = n * CMP_STRIDE + CMP_LEN - 1
    seen = (end[None, :] <= np.arange(S)[:, None]) & (n < CMP_N - 1)[None, :]
    put("cmp_mask", np.tile(seen.T, (4, 1)).astype(np.float32))
    bias = np.where(seen, 0.0, MASK).astype(np.float32).reshape(ST, P, 1, CMP_N)
    put("cmp_bias", np.broadcast_to(bias, (ST, P, 4, CMP_N)).transpose(1, 0, 2, 3).reshape(P, -1))
    put("tri", np.where(np.arange(P)[None, :] <= np.arange(P)[:, None], 0.0, MASK).astype(np.float32))
    sel = np.zeros((P, 3, 2, P), np.float32)
    for b in range(3):
        for h in range(4):
            sel[8 + 4 * b + h, b, h // 2, 64 * (h % 2):64 * (h % 2) + 64] = 1.0
    put("sel", sel.reshape(P, -1))
    bd = np.zeros((P, 2, P), np.float32)
    for h in range(4):
        bd[32 * h:32 * h + 32, h // 2, 64 * (h % 2):64 * (h % 2) + 64] = 1.0
    put("ones_bd", bd.reshape(P, -1))
    return made


def small_weights(a):
    made = np.zeros((P, DEPTH, 320), np.float32)
    for l in range(DEPTH):
        made[:, l, 0:64] = made[:, l, 64:128] = a["cmp_w2_2"][l, 0]
        made[:, l, 128:192] = a["cmp_w2_2"][l, 1]
        for g in range(4):
            made[64 * (g % 2):64 * (g % 2) + 64, l, 192 + 64 * (g // 2):256 + 64 * (g // 2)] = a["pool_w_2"][l, g]
    return made.reshape(P, -1)


def host_layout(a):
    cmp_pos = a["cmp_pos_2"].transpose(1, 3, 0, 2).reshape(P, DEPTH * CMP_LEN)
    b2v = np.broadcast_to(a["cmp_b2_2"][:, 1].reshape(1, -1), (P, DEPTH * HD))
    c = np.ascontiguousarray
    return {
        "weights": weight_stream(a),
        "x_t": c(_tile(c(a["x"][0].T))),
        "p_t": c(np.concatenate([_tile(c(a["p"][l, 0].T)) for l in range(DEPTH)], 1)),
        "positions": c(np.broadcast_to(a["positions"], (P, S))),
        "columns": column_pack(a),
        "tables": table_pack(),
        "small_w": small_weights(a),
        "cmp_pos": c(cmp_pos),
        "b2v": c(b2v),
        "lam": c(np.broadcast_to(a["c_lambda"].reshape(1, -1), (P, 4 * HD))),
    }


def attention_units():
    units = [("A", h) for h in range(A_HEADS)] + [("B", h) for h in range(B_HEADS)]
    units += [("C", h) for h in range(C_HEADS)]
    for layer in range(DEPTH):
        units += [("slc", layer, h) for h in range(4)] + [("win", layer, h) for h in range(4)]
        units += [("fox", layer, h) for h in range(4)]
    return units


UNITS = attention_units()
SCORES = [(u, q, c) for u in UNITS for q in range(ST) for c in range(2 if u[0] == "C" else 1)]
SCORE_AT = {key: n for n, key in enumerate(SCORES)}
TURNS = [(u, q) for u in UNITS for q in range(ST)]
TURN_AT = {key: n for n, key in enumerate(TURNS)}
UNIT_AT = {u: n for n, u in enumerate(UNITS)}


def rope_jobs():
    jobs = [("qkA", t) for t in range(8)] + [("kpe",)] + [("qB", h) for h in range(B_HEADS)]
    jobs += [("qkC", t) for t in range(16)]
    for layer in range(DEPTH):
        jobs += [(kind, layer) for kind in ("ks", "kw", "nq0", "nq1", "kc")]
    return jobs


ROPES = rope_jobs()
ROPE_AT = {key: n for n, key in enumerate(ROPES)}

N_INPUTS = 9
N_CLEAR = 12
SETUP = {"rest": 8, "lam_sums": 10, "all": 13}
_c2 = round((2 * math.pi - 6.28125) * 2 ** 21) / 2 ** 21
TWO_PI = (6.28125, _c2, 2 * math.pi - 6.28125 - _c2)


MEAN_LAG = 2
AHEAD = 3
FINISH_LAG = 4
GATE_ORDER = (2, 3, 4, 5, 0, 1, 6, 7)


def build(nc, dram, out):
    ctx = ExitStack()
    with ctx:
        def sb(name, shape, dt=F32):
            return ctx.enter_context(nc.sbuf_tensor(name, shape, dt))

        def sem(name):
            return ctx.enter_context(nc.semaphore(name))

        REGION = 134

        ring = sb("ring", [P, RING, BLK])
        w_parts = [sb("w_hi", [P, RING, BLK], F32R), sb("w_lo", [P, RING, BLK], F32R)]
        x = sb("x", [P, KD, S])
        region_at = nc.sbuf_base
        region = sb("region", [P, REGION * KB])
        cols = sb("cols", [P, NCOLS])
        tabs = sb("tabs", [P, TABS["count"]])
        rope_a = sb("rope_a", [P, 2, S])
        small_w = sb("small_w", [P, DEPTH * 320])
        cmp_pos = sb("cmp_pos", [P, DEPTH * CMP_LEN])
        b2v = sb("b2v", [P, DEPTH * HD])
        prob_at = nc.sbuf_base
        prob = sb("prob", [P, 4, S])
        rope_tmp = sb("rope_tmp", [P, 2, S])
        std = sb("std", [P, 2, S])
        rstd = sb("rstd", [P, 2, S])
        unit = sb("unit", [P, 1])
        negmax = sb("negmax", [P, 8])
        rowsum = sb("rowsum", [P, 8])
        rownorm = sb("rownorm", [P, 8])
        inverse_tmp = sb("inverse_tmp", [P, S // 32])
        cmp_negmax = sb("cmp_negmax", [P, 16])
        neg_lam = sb("neg_lam", [P, 8])
        ident_bf = sb("ident_bf", [P, P], BF16)
        tri_bf = sb("tri_bf", [P, P], BF16)
        cmp_bias_bf = sb("cmp_bias_bf", [P, S], BF16)
        psum = [ctx.enter_context(nc.psum_tensor(f"bank{i}", [P, S], F32)) for i in range(8)]

        def place(kb, *shape):
            at, n = int(kb * KB), int(np.prod(shape))
            assert at + n <= REGION * KB
            v = region[:, at:at + n]
            if len(shape) == 2:
                return v.rearrange("p (a b) -> p a b", a=shape[0])
            if len(shape) == 3:
                return v.rearrange("p (a b c) -> p a b c", a=shape[0], b=shape[1])
            if len(shape) == 4:
                return v.rearrange("p (a b c d) -> p a b c d", a=shape[0], b=shape[1], c=shape[2])
            return v

        def parts(name, kb, *shape, base=region_at):
            size = 4 * int(np.prod(shape))
            return [nc.alloc_sbuf_tensor_at(f"{name}_{part}", [P, *shape], F32R, offset=base + int(1024 * kb) + i * size)
                    for i, part in enumerate(("hi", "lo"))]

        def parts_at(name, kbs, *shape):
            return [nc.alloc_sbuf_tensor_at(f"{name}_{part}", [P, *shape], F32R, offset=region_at + 1024 * kb)
                    for kb, part in zip(kbs, ("hi", "lo"))]

        def col(name, i=0, rows=slice(0, P)):
            return cols[rows, COLS[name] + i:COLS[name] + i + 1]

        LATE_KB = REGION - (NTABS - TABS["cos2"]) / KB
        late = place(LATE_KB, NTABS - TABS["cos2"])

        def tab(name, width):
            if TABS[name] >= TABS["cos2"]:
                return late[:, TABS[name] - TABS["cos2"]:TABS[name] - TABS["cos2"] + width]
            return tabs[:, TABS[name]:TABS[name] + width]

        ident, ones = tab("ident", P), tab("ones", P)
        perm_a, perm_b = tab("perm_a", P), tab("perm_b", P)
        sel = tab("sel", 6 * P).rearrange("p (b j m) -> p b j m", b=3, j=2)
        ones_bd = tab("ones_bd", 2 * P).rearrange("p (j m) -> p j m", j=2)
        inv_count = tab("inv_count", 2 * S).rearrange("p (t s) -> p t s", t=2)

        moving = parts("moving", 0, KD, S)
        z = place(32, KD, S)
        pt = place(32, 2, ST, S)
        mix = place(48, KD, S)
        pos_raw, pos_f = mix[:, 0, :].bitcast(I32), mix[:, 1, :]
        lam_in = mix[:, 2, 0:4 * HD]
        masks_in = place(48 + 6, S + P)
        angle, turns, rest = z[:, 0:2, :], z[:, 2:4, :], z[:, 4:6, :]
        kpe = z[:, 0, :]
        lat_square = z[:, 1:6, :]
        lat = mix[:, 3:8, :]
        qk_a = place(64, 8, S)
        q_b = place(64, 8, S)
        v_ab = place(80, ST, 4, 3 * HD)
        k_b = place(92, 8, S)
        count = place(108, ST, S)
        mask_a = place(120, ST * S // 2).bitcast(BF16).rearrange("p (q k) -> p q k", q=ST)
        cos_a, sin_a = rope_a[:, 0, :], rope_a[:, 1, :]
        cos_b, sin_b = place(116, S), place(118, S)
        qk_c = place(64, 16, S)
        v_c = place(96, ST, KD * P)
        square = place(64, KD, S)
        hid_kb = 2 * KF
        hid = parts("hid", 32, KF, S)
        conv_t = place(32 + 2 * hid_kb, 2, S)
        gelu_t = place(36 + 2 * hid_kb, 2, S)
        z_ffn = place(16, KD, S)
        p_in_t = place(40 + 2 * hid_kb, 2, S)
        p_parts = parts("p", 0, 2, S, base=prob_at)
        sig_p = place(96, KD, S)
        kcvc = prob[:, 0, :]
        blocks_x = prob[:, 1:3, :].rearrange("p t (l n) -> p (t l) n", n=CMP_N)
        blocks = nc.alloc_sbuf_tensor_at("blocks", [P, CMP_LEN, 2, 2, CMP_N], F32R, offset=region_at + 32 * 1024)
        hid_sum = place(116.5, 2, 2 * CMP_N)
        pool_u, pool_a, pool_b = (place(32 + i * 2 * (PAD + S) / KB, 2, PAD + S) for i in range(3))
        nq = place(64, 2, S)
        ksw = place(68, 2, S)
        fqk = place(72, 4, S)
        v_s = place(80, ST, 3 * HD)
        v_w = place(83, ST, 3 * HD)
        v_f = place(86, ST, 2, 3 * HD)
        cq = place(92, S)
        ck = place(94, S)
        gates = place(96, 3, 2, S)
        gate_sig = place(108, S)
        vc_bd = place(110, 2, P)
        hid_k = place(111, CMP_N)
        hid_v = place(111.125, 4, CMP_N)
        kc = place(111.625, CMP_N)
        conv_u = place(112, 2, 2 + S)
        conv_x, conv_b = prob[:, 0:2, :], prob[:, 2:4, :]
        sg = place(64, KD, S)
        branch = parts("branch", 80, KD, S)
        sig_m = place(32, 2, N_BRANCH, S)
        acc = parts_at("acc", (48, 64), KD, S)

        full = [sem(f"slot{i}_full") for i in range(RING)]
        split_hi, split_ready = sem("split_hi"), sem("split_ready")
        hi_ready, parts_ready = sem("hi_ready"), sem("parts_ready")
        x_in = [sem(f"x_in{i}") for i in range(KD // 2)]
        hid_hi, hid_parts = sem("hid_hi"), sem("hid_parts")
        late_in, unit_set = sem("late_in"), sem("unit_set")
        block_done = sem("block_done")
        inputs_in = sem("inputs_in")
        setup_dve, setup_act = sem("setup_dve"), sem("setup_act")
        link_dve, link_act = sem("link_dve"), sem("link_act")
        v_stored = sem("v_stored")
        rope_raw, rope_perm, roped = sem("rope_raw"), sem("rope_perm"), sem("roped")
        lat_raw, kb_stored = sem("lat_raw"), sem("kb_stored")
        squared, summed, std_ready, normed = sem("squared"), sem("summed"), sem("std_ready"), sem("normed")
        scored, maxed, exped, blended = sem("scored"), sem("maxed"), sem("exped"), sem("blended")
        turned, pt_stored, weighed, attended = sem("turned"), sem("pt_stored"), sem("weighed"), sem("attended")
        z_ready, mean_ready, centered = sem("z_ready"), sem("mean_ready"), sem("centered")
        conv_mid, conv_done, gelu_done, hid_ready = (sem("conv_mid"), sem("conv_done"), sem("gelu_done"),
                                                     sem("hid_ready"))
        conv_mid2 = sem("conv_mid2")
        p_loaded, ple_sig, ple_term, x_ple = sem("p_loaded"), sem("ple_sig"), sem("ple_term"), sem("x_ple")
        kpe_spread = sem("kpe_spread")
        constants_bf = sem("constants_bf")
        stored, prepared, spread = sem("stored"), sem("prepared"), sem("spread")
        compress_step, cleared, gated = sem("compress_step"), sem("cleared"), sem("gated")
        sig_ready, merged, merge_link, x_next = sem("sig_ready"), sem("merged"), sem("merge_link"), sem("x_next")
        out_stored = sem("out_stored")

        T = {}
        T["v"] = Tally([("A", i) for i in range(4)] + [("B", i) for i in range(4)] + [("C", i) for i in range(8)])
        T["squared"], T["summed"], T["std"], T["normed"] = Tally(), Tally(), Tally(), Tally()
        for n in range(5):
            T["squared"].add(("lat", n))
        for j in range(2):
            T["summed"].add(("lat", j)), T["std"].add(("lat", j))
        for n in range(5):
            T["normed"].add(("lat", n))

        def plan_ln(i):
            for n in range(KD):
                T["squared"].add(("ln", i, n)), T["normed"].add(("ln", i, n))
            T["summed"].add(("ln", i)), T["std"].add(("ln", i))

        plan_ln(0), plan_ln(1)
        for n in range(C_HEADS):
            for t in ("squared", "summed", "std", "normed"):
                T[t].add(("C", n))
        plan_ln(2), plan_ln(3)
        for i in range(DEPTH + 1):
            for n in range(KD):
                T["squared"].add(("rms", i, n)), T["normed"].add(("rms", i, n))
            T["summed"].add(("rms", i)), T["std"].add(("rms", i))

        T["parts"] = Tally([("x", 0, n) for n in range(KD)] + [("lat", n) for n in range(5)])
        for layer in range(DEPTH):
            keys = [("mix", layer, n) for n in range(KD)] + [("ln", 2 * layer, n) for n in range(KD)]
            keys += [("p", layer)] + [("ln", 2 * layer + 1, n) for n in range(KD)]
            keys += [("x", 1, n) for n in range(KD if layer == 0 else 0)]
            for key in keys:
                T["parts"].add(key)
        for layer in range(DEPTH):
            for key in [("h2", layer, n) for n in range(KD)] + [("blocks", layer)]:
                T["parts"].add(key)
            for t in GATE_ORDER:
                T["parts"].add(("branch", layer, t))

        T["stored"], T["prepared"] = Tally(), Tally()
        for layer in range(DEPTH):
            for key in ["gsig", "fl", "ln", "kcvc", "vs", "vw", "hidk", "hidv", "fq0", "fq1", "fk0", "fk1", "cmp_exp", "fv0", "fv1",
                        "fv2", "fv3", "pool0", "pool1", "cx0", "cx1", "cb0", "cb1", *[f"g{n}" for n in range(6)],
                        "pm0", "pm1", "pm2", "pm3", *[f"sg{t}" for t in range(8)]]:
                T["stored"].add((key, layer))
            for key in ["blocks", "hid", "vc", "decay", "cmp_shift", "cmp_pt", "pooled", "cu0", "cu1", "convy0", "convy1",
                        "cmp_out0", "cmp_out"]:
                T["prepared"].add((key, layer))

        block = ctx.enter_context(nc.Block())

        def done(key):
            return AT[key] + 1

        def both(parts, at):
            return parts[0][at], parts[1][at]

        @block.sync
        def _(sp):
            for s in range(RING):
                sp.dma_start(ring[:, s, :], dram["weights"][s]).then_inc(full[s], 16)
            with sp.Fori(1, len(BLOCKS) // RING) as it:
                for s in range(RING):
                    sp.wait_ge(split_ready, RING * it + (s - RING + 1))
                    sp.dma_start(ring[:, s, :], dram["weights"][RING * it + s]).then_inc(full[s], 16)
            for n in range(len(BLOCKS) // RING * RING, len(BLOCKS)):
                sp.wait_ge(split_ready, n - RING + 1)
                sp.dma_start(ring[:, n % RING, :], dram["weights"][n]).then_inc(full[n % RING], 16)

            for n in range(KD):
                sp.wait_ge(normed, T["normed"][("rms", DEPTH, n)])
                sp.dma_start(out[:, n, :], z[:, n, :]).then_inc(out_stored, 16)
            sp.wait_ge(out_stored, 16 * KD)

        @block.tensor
        def _(pe):
            def arrived(key):
                n = AT[key]
                pe.wait_ge(split_ready, n + 1)
                return both(w_parts, np.s_[:, n % RING, :])

            def passes(bank, lhs, rhs, start, stop):
                pe.matmul(bank, lhs[0], rhs[0], start=start, stop=False, skip_group_check=True)
                pe.matmul(bank, lhs[0], rhs[1], start=False, stop=False, skip_group_check=True)
                return pe.matmul(bank, lhs[1], rhs[0], start=False, stop=stop, skip_group_check=True)

            def cols_of(pair, lo, n):
                return pair[0][:, lo:lo + n], pair[1][:, lo:lo + n]

            def project(key, bank, rhs, kt=KD, ready=None):
                w = arrived(key)
                for k in range(kt):
                    if ready:
                        pe.wait_ge(parts_ready, T["parts"][ready + (k,)])
                    mm = passes(bank, cols_of(w, k * P, P), rhs(k), k == 0, k == kt - 1)
                mm.then_inc(block_done, 1)

            def moved(k):
                return both(moving, np.s_[:, k, :])

            def turn_pairs(job, matrix, rows, raw, n=S):
                g = ROPE_AT[job]
                pe.wait_ge(rope_raw, g + 1)
                if g >= 2:
                    pe.wait_ge(roped, g - 1)
                pe.matmul(psum[4 + g % 2][0:rows, 0:n], matrix[0:rows, 0:rows], raw, start=True,
                          stop=True).then_inc(rope_perm, 1)

            def tokens_values(keys, lhs, banks, width, per, ready=None):
                for i, key in enumerate(keys):
                    w = arrived(key)
                    if ready:
                        pe.wait_ge(parts_ready, T["parts"][ready + (i * per + per - 1,)])
                    for st in range(ST):
                        for j in range(per):
                            k = i * per + j
                            mm = passes(banks[st], cols_of(lhs(k), st * P, P), cols_of(w, j * width, width), k == 0,
                                        k == len(keys) * per - 1)
                    mm.then_inc(block_done, 1)

            def attention(units, q, k, v, extra, ahead, blend=False, causal=False):
                turns = [(u, i) for u in units for i in range(ST)]
                comps = 2 if blend else 1

                def scores(u, i):
                    for c in range(comps):
                        s = SCORE_AT[(u, i, c)]
                        if s >= 4:
                            pe.wait_ge(exped, s - 3)
                        w = (i + 1) * P if causal else S
                        bank = psum[s % 4]
                        more = extra(bank, u, i)
                        mm = pe.matmul(bank[:, 0:w], q(u, c)[:, i * P:i * P + P], k(u, c)[:, 0:w], start=True,
                                       stop=True)
                        for o, lhs, rhs in more:
                            mm = pe.matmul(o, lhs, rhs, start=False, stop=True, skip_group_check=True)
                        mm.then_inc(scored, 1)

                def values(u):
                    n = UNIT_AT[u]
                    pe.wait_ge(pt_stored, TURN_AT[(u, ST - 1)] + 1)
                    if n >= 2:
                        pe.wait_ge(attended, n - 1)
                    for t in range(ST):
                        lo = t * P if causal else 0
                        mm = pe.matmul(psum[6 + n % 2][:, lo:S], v(u, t), pt[:, n % 2, t, lo:S], start=(t == 0),
                                       stop=(t == ST - 1))
                    mm.then_inc(weighed, 1)

                for u, i in turns[:ahead]:
                    scores(u, i)
                for n, (u, i) in enumerate(turns):
                    if n + ahead < len(turns):
                        scores(*turns[n + ahead])
                    t = TURN_AT[(u, i)]
                    s = SCORE_AT[(u, i, 0)]
                    if blend:
                        pe.wait_ge(blended, t - TURN_AT[(("C", 0), 0)] + 1)
                    else:
                        pe.wait_ge(exped, s + 1)
                    if t >= 2:
                        pe.wait_ge(pt_stored, t - 1)
                    for kt in range(i + 1 if causal else ST):
                        mm = pe.transpose(psum[4 + t % 2][:, kt * P:kt * P + P], prob[:, s % 4, kt * P:kt * P + P], ident)
                    mm.then_inc(turned, 1)
                    if n and turns[n - 1][1] == ST - 1:
                        values(turns[n - 1][0])
                values(units[-1])

            def add_mean(i, n):
                pe.wait_ge(z_ready, KD * i + n + 1)
                return pe.matmul(psum[6][:], ones, (z_ffn if i % 2 else z)[:, n, :], start=(n == 0), stop=(n == KD - 1),
                                 skip_group_check=True)

            def residual_norm(i):
                for n in range(4 if i % 2 else KD - MEAN_LAG, KD):
                    mm = add_mean(i, n)
                mm.then_inc(mean_ready, 1)
                sum_squares(("ln", i), psum[7], KD, lambda n: square[:, n, :])

            def sum_squares(key, bank, count, tile, names=None):
                for n in range(count):
                    pe.wait_ge(squared, T["squared"][names(n) if names else key + (n,)])
                    mm = pe.matmul(bank[:], ones, tile(n), start=(n == 0), stop=(n == count - 1))
                mm.then_inc(summed, 1)

            def mixer_out(i):
                layer = i // 2
                for n in range(KD):
                    if n >= 4:
                        pe.wait_ge(z_ready, KD * i + n - 3)
                    project(("mixout", layer, n), psum[n % 4][:], moved, ready=("mix", layer) if n == 0 else None)
                    if n >= MEAN_LAG:
                        add_mean(i, n - MEAN_LAG)

            def feed_forward(i):
                layer = i // 2
                n0 = AT[("gate", layer, 0)]
                with pe.Fori(0, KF // 2) as it:
                    for par in range(2):
                        pe.wait_ge(hid_ready, 2 * it + (par + 1 + KF * layer))
                        for half in range(2):
                            b = n0 + 2 * par + half
                            pe.wait_ge(split_ready, 4 * it + (b + 1))
                            w = both(w_parts, np.s_[:, b % RING, :])
                            for k in range(KD):
                                if par == half == 0:
                                    pe.wait_ge(parts_ready, T["parts"][("ln", i - 1, k)])
                                mm = passes(psum[2 * half + par][:], cols_of(w, k * P, P), moved(k), k == 0, k == KD - 1)
                            mm.then_inc(block_done, 1)
                for h in range(2):
                    banks = psum[4:8] if h == 0 else psum[0:4]
                    d0 = AT[("down", layer, h, 0)]

                    def down(b, it, first=False, last=False):
                        pe.wait_ge(split_ready, 4 * it + (d0 + b + 1))
                        w = both(w_parts, np.s_[:, (d0 + b) % RING, :])
                        if h == 0:
                            pe.wait_ge(hid_parts, 8 * it + (2 * b + 2 + KF * layer))
                        for j in range(2):
                            tile = both(hid, np.s_[:, 8 * it + (2 * b + j), :])
                            for n in range(4):
                                mm = passes(banks[n][:], cols_of(w, j * S + n * P, P), tile, first and j == 0,
                                            last and j == 1)
                        mm.then_inc(block_done, 1)

                    for b in range(3):
                        down(b, 0, first=(b == 0))
                    if h == 1:
                        pe.wait_ge(z_ready, KD * i + 4)
                        for n in range(4):
                            add_mean(i, n)
                    with pe.Fori(0, 2) as it:
                        for b in range(3, 7):
                            down(b, it)

            def per_layer(layer):
                for half in range(2):
                    w = arrived(("pleproj", layer, half))
                    if half == 0:
                        pe.wait_ge(parts_ready, T["parts"][("p", layer)])
                        pe.wait_ge(std_ready, T["std"][("ln", 2 * layer + 1)])
                    else:
                        pe.wait_ge(ple_term, KD * layer + 4)
                    for n in range(4):
                        for k in range(2):
                            mm = passes(psum[4 + n][:], cols_of(w, k * S + n * P, P), both(p_parts, np.s_[:, k, :]), k == 0,
                                        k == 1)
                    mm.then_inc(block_done, 1)
                    for n in range(4 * half, 4 * half + 4):
                        if n >= 4:
                            pe.wait_ge(ple_sig, KD * layer + n - 3)
                        project(("plegate", layer, n), psum[n % 4][:], moved,
                                ready=("ln", 2 * layer + 1) if n == 0 else None)

            def mixer_a():
                tokens_values([("vA", i) for i in range(4)], moved, [psum[i][:] for i in range(4)], S, 2, ready=("x", 0))
                pe.wait_ge(inputs_in, 16 * N_INPUTS)
                for t in range(8):
                    if t < 4:
                        pe.wait_ge(v_stored, T["v"][("A", t)])
                    else:
                        pe.wait_ge(rope_raw, ROPE_AT[("qkA", t - 4)] + 1)
                    project(("qkA", t), psum[t % 4][:], moved)
                    if t:
                        turn_pairs(("qkA", t - 1), perm_a, P, qk_a[:, t - 1, :])
                for n in range(5):
                    if n < 4:
                        pe.wait_ge(rope_raw, ROPE_AT[("qkA", 4 + n)] + 1)
                    else:
                        pe.wait_ge(lat_raw, n - 3)
                    project(("lat", n), psum[n % 4][:], moved)
                    if n == 0:
                        turn_pairs(("qkA", 7), perm_a, P, qk_a[:, 7, :])
                w = arrived(("kpe", 0))
                pe.wait_ge(lat_raw, 2)
                for k in range(KD):
                    mm = passes(psum[1][0:B_QK, :], cols_of(w, k * B_QK, B_QK), moved(k), k == 0, k == KD - 1)
                mm.then_inc(block_done, 1)
                sum_squares(None, psum[6], 3, lambda n: lat_square[:, n, :], lambda n: ("lat", n))
                sum_squares(None, psum[7], 2, lambda n: lat_square[:, 3 + n, :], lambda n: ("lat", 3 + n))
                turn_pairs(("kpe",), perm_b, B_QK, kpe[0:B_QK, :])

            def mixer_b():
                pe.wait_ge(parts_ready, T["parts"][("lat", 4)])
                for i in range(3):
                    w = arrived(("qup", i))
                    heads = range(3 * i, min(3 * i + 3, B_HEADS))
                    for h in heads:
                        if h >= 4:
                            pe.wait_ge(rope_raw, ROPE_AT[("qB", h - 4)] + 1)
                        for k in range(3):
                            lo = (h - 3 * i) * 3 * B_QK + k * B_QK
                            mm = passes(psum[h % 4][0:B_QK, :], cols_of(w, lo, B_QK), moved(k), k == 0, k == 2)
                    mm.then_inc(block_done, 1)
                    if i:
                        for h in range(3 * i - 3, 3 * i):
                            turn_pairs(("qB", h), perm_b, B_QK, q_b[0:B_QK, h, :])
                w = arrived(("kvk", 0))
                pe.wait_ge(rope_raw, ROPE_AT[("qB", 7)] + 1)
                for j in range(4):
                    for k in range(2):
                        lo = j * 2 * P + k * P
                        mm = passes(psum[j][:], cols_of(w, lo, P), moved(3 + k), k == 0, k == 1)
                mm.then_inc(block_done, 1)
                for h in range(6, 8):
                    turn_pairs(("qB", h), perm_b, B_QK, q_b[0:B_QK, h, :])
                pe.wait_ge(kb_stored, 8)
                tokens_values([("kvv", 0)], lambda k: moved(3 + k), [psum[i][:] for i in range(4)], S, 2)

            def heads_ab(kind):
                if kind == "A":
                    pe.wait_ge(v_stored, T["v"][("A", 3)])
                    pe.wait_ge(lat_raw, 5)
                    pe.wait_ge(roped, ROPE_AT[("kpe",)] + 1)
                    pe.wait_ge(kpe_spread, 1)
                    pe.wait_ge(std_ready, T["std"][("lat", 1)])
                    pe.wait_ge(cleared, 1)
                    pe.wait_ge(constants_bf, 4)
                else:
                    pe.wait_ge(kb_stored, 8)
                    pe.wait_ge(v_stored, T["v"][("B", 3)])
                    pe.wait_ge(roped, ROPE_AT[("qB", 7)] + 1)
                half = lambda h: slice(HD * (h % 2), HD * (h % 2) + HD)

                def q(u, c):
                    h = u[1]
                    return qk_a[half(h), h // 2, :] if u[0] == "A" else q_b[0:B_QK, h, :]

                def k(u, c):
                    h = u[1]
                    return qk_a[half(h), 4 + h // 2, :] if u[0] == "A" else k_b[0:B_QK, h, :]

                def v(u, t):
                    h = u[1]
                    return v_ab[:, t, h // 2, HD * (h % 2):HD * (h % 2) + P]

                def mask(bank, u, i):
                    return [(bank[:], ident_bf[:], mask_a[:, i, :])] if u[0] == "A" else []

                attention([u for u in UNITS if u[0] == kind], q, k, v, mask, ahead=AHEAD)

            def mixer_c():
                for half in range(2):
                    pe.wait_ge(ple_term, KD)
                    tokens_values([("vC", 4 * half + i) for i in range(4)], moved,
                                  [psum[4 * half + i][:] for i in range(4)], S, 2, ready=("x", 1))
                for t in range(16):
                    if t < 4:
                        pe.wait_ge(v_stored, T["v"][("C", t)])
                    else:
                        pe.wait_ge(rope_raw, ROPE_AT[("qkC", t - 4)] + 1)
                    project(("qkC", t), psum[t % 4][:], moved)
                    if t:
                        if t == 1:
                            pe.wait_ge(v_stored, T["v"][("C", 7)])
                        turn_pairs(("qkC", t - 1), perm_a, P, qk_c[:, t - 1, :])
                turn_pairs(("qkC", 15), perm_a, P, qk_c[:, 15, :])

            def heads_c():
                pe.wait_ge(roped, ROPE_AT[("qkC", 15)] + 1)
                half = lambda c: slice(HD * c, HD * c + HD)
                attention([u for u in UNITS if u[0] == "C"], lambda u, c: qk_c[half(c), u[1], :],
                          lambda u, c: qk_c[half(c), 8 + u[1], :], lambda u, t: v_c[:, t, u[1] * P:u[1] * P + P],
                          lambda bank, u, i: [], ahead=2, blend=True)
                for n in range(C_HEADS):
                    if n >= 2:
                        pe.wait_ge(std_ready, T["std"][("C", n - 2)])
                    sum_squares(None, psum[4 + n % 2], 1, lambda _: square[:, n, :], lambda _: ("C", n))
            def sum_rms(i):
                if i == 0:
                    pe.wait_ge(ple_term, KD * DEPTH)
                sum_squares(("rms", i), psum[7], KD, lambda n: z[:, n, :])

            def compressed_scores(layer):
                pe.wait_ge(roped, ROPE_AT[("kc", layer)] + 1)
                pe.wait_ge(constants_bf, 3)
                for odd in range(2):
                    bank = psum[6 + odd]
                    mask = cmp_bias_bf[:].rearrange("p (i h n) -> p i h n", i=ST, h=4)[:, :, 0:2, :]
                    pe.matmul(bank[:, 0:2 * P], ident_bf[:], mask, start=True, stop=True)
                    rows = slice(HD * odd, HD * odd + HD)
                    for i in range(ST):
                        for j in range(2):
                            lo = (2 * i + j) * CMP_N
                            mm = pe.matmul(bank[:, lo:lo + CMP_N], nq[rows, j, i * P:i * P + P], kc[rows, :],
                                           start=False, stop=True, skip_group_check=True)
                mm.then_inc(compress_step, 1)

            def compressed_transposes(layer):
                pe.wait_ge(stored, T["stored"][("cmp_exp", layer)])
                for i in range(ST):
                    mm = pe.transpose(psum[7][:, i * P:i * P + P], rstd[:, 1, i * P:i * P + P], ident)
                mm.then_inc(compress_step, 1)

            def compressed_values(layer):
                pe.wait_ge(prepared, T["prepared"][("cmp_pt", layer)])
                for j in range(2):
                    pe.matmul(psum[4 + j][:], vc_bd[:, j, :], prob[:, 3, :], start=True, stop=True)
                    mm = pe.matmul(psum[6 + j][:], ones_bd[:, j, :], prob[:, 3, :], start=True, stop=True)
                mm.then_inc(compress_step, 1)

            def project_second(layer):
                stored_at = lambda key: pe.wait_ge(stored, T["stored"][(key, layer)])
                raw_at = lambda key: pe.wait_ge(rope_raw, ROPE_AT[(key, layer)] + 1)
                rhs = moved
                project(("small", layer), psum[0][:], rhs, ready=("h2", layer))
                project(("kcvc", layer), psum[1][:], rhs)
                w = arrived(("vsvw", layer))
                for st in range(ST):
                    for k in range(KD):
                        mm = passes(psum[2][:, st * P:st * P + P], cols_of(moved(k), st * P, P), cols_of(w, k * P, P), k == 0,
                                    k == KD - 1)
                mm.then_inc(block_done, 1)
                project(("ks", layer), psum[3][:], rhs)
                stored_at("fl")
                project(("kw", layer), psum[0][:], rhs)
                turn_pairs(("ks", layer), perm_a, P, ksw[:, 0, :])
                stored_at("kcvc")
                project(("nq", layer, 0), psum[1][:], rhs)
                turn_pairs(("kw", layer), perm_a, P, ksw[:, 1, :])
                stored_at("vw")
                project(("nq", layer, 1), psum[2][:], rhs)
                turn_pairs(("nq0", layer), perm_a, P, nq[:, 0, :])
                pe.wait_ge(parts_ready, T["parts"][("blocks", layer)])
                for i in range(4):
                    w = arrived(("w1", layer, i))
                    for l in range(8):
                        at, last = 8 * i + l, i == 3 and l == 7
                        pe.matmul(psum[3][:, 0:4 * CMP_N], w[0][:, l * P:l * P + P],
                                  blocks[:, at].rearrange("p a c n -> p (a c n)"), start=(at == 0), stop=last,
                                  skip_group_check=True)
                        mm = pe.matmul(psum[3][:, 0:2 * CMP_N], w[1][:, l * P:l * P + P],
                                       blocks[:, at, 0].rearrange("p c n -> p (c n)"), start=False, stop=last,
                                       skip_group_check=True)
                    mm.then_inc(block_done, 1)
                turn_pairs(("nq1", layer), perm_a, P, nq[:, 1, :])
                stored_at("hidk")
                lo = layer * 320
                pe.matmul(psum[7][:, 0:CMP_N], small_w[:, lo:lo + P], hid_k, start=True,
                          stop=True).then_inc(compress_step, 1)
                stored_at("hidv")
                pe.matmul(psum[3][:, 0:HD], hid_v.rearrange("p a n -> p (a n)"), small_w[:, lo + P:lo + P + HD],
                          start=True, stop=True).then_inc(compress_step, 1)
                raw_at("kw")
                project(("fq", layer, 0), psum[0][:], rhs)
                turn_pairs(("kc", layer), perm_a, P, kc, CMP_N)
                raw_at("nq0")
                project(("fq", layer, 1), psum[1][:], rhs)
                raw_at("nq1")
                project(("fk", layer, 0), psum[2][:], rhs)
                pe.wait_ge(prepared, T["prepared"][("vc", layer)])
                project(("fk", layer, 1), psum[3][:], rhs)
                compressed_scores(layer)
                stored_at("fk1")
                tokens_values([("fv", layer, i) for i in range(2)], rhs, [psum[i][:, 0:256] for i in range(4)], 256, 4)
                compressed_transposes(layer)
                for n, (key, before) in enumerate([(("pool", layer, 0), "fv0"), (("pool", layer, 1), "fv1"),
                                                   (("conv", layer, 0), "fv2"), (("conv", layer, 1), "fv3"),
                                                   (("conv", layer, 2), "pool0"), (("conv", layer, 3), "pool1"),
                                                   (("conv", layer, 4), "cx0"), (("conv", layer, 5), "cx1")]):
                    if n == 2:
                        compressed_values(layer)
                    stored_at(before)
                    project(key, psum[n % 4][:], rhs)
                stored_at("gsig")
                for n in range(6):
                    if n < 2:
                        stored_at(f"cb{n}")
                    elif n < 4:
                        pe.wait_ge(prepared, T["prepared"][(f"cu{n - 2}", layer)])
                    else:
                        stored_at(f"g{n - 4}")
                    pe.matmul(psum[n % 4][:], sel[:, n // 2, n % 2, :], gate_sig, start=True,
                              stop=True).then_inc(spread, 1)
                pe.wait_ge(prepared, T["prepared"][("pooled", layer)])
                for g in range(4):
                    stored_at(f"g{(g + 2) if g < 2 else g + 2}")
                    rows = slice(HD * (g % 2), HD * (g % 2) + HD)
                    at = lo + 192 + HD * (g // 2)
                    pe.matmul(psum[(g + 2) % 4][rows, :], small_w[rows, at:at + HD], mix[rows, 2 + g // 2, :], start=True,
                              stop=True).then_inc(spread, 1)

            def heads_second(layer):
                half = lambda h: slice(HD * (h % 2), HD * (h % 2) + HD)
                pe.wait_ge(stored, T["stored"][("pm3", layer)])
                pe.wait_ge(prepared, T["prepared"][("cmp_out", layer)])
                pe.wait_ge(cleared, 1 + N_CLEAR * (layer + 1))

                def q(u, c):
                    h = u[2]
                    return nq[half(h), h // 2, :] if u[0] != "fox" else fqk[half(h), h // 2, :]

                def k(u, c):
                    h = u[2]
                    return fqk[half(h), 2 + h // 2, :] if u[0] == "fox" else ksw[half(h), int(u[0] == "win"), :]

                def v(u, t):
                    h = u[2]
                    if u[0] == "fox":
                        return v_f[:, t, h // 2, HD * (h % 2):HD * (h % 2) + P]
                    lo = HD * (1 - h % 2)
                    return (v_s if u[0] == "slc" else v_w)[:, t, lo:lo + P]

                def extra(bank, u, i):
                    more = []
                    if u[0] == "fox":
                        rows = slice(32 * u[2], 32 * u[2] + 2)
                        more.append((bank[:, 0:i * P + P], cq[rows, i * P:i * P + P], ck[rows, 0:i * P + P]))
                    more.append((bank[:, i * P:i * P + P], ident_bf[:], tri_bf[:]))
                    return more

                attention([u for u in UNITS if len(u) == 3 and u[1] == layer], q, k, v, extra, ahead=AHEAD, causal=True)

            def merge(layer):
                for t in range(KD):
                    if t >= 6:
                        pe.wait_ge(attended, UNIT_AT[("fox", layer, t - 4)] + 1)
                    project(("sgate", layer, t), psum[t][:], moved)
                pe.wait_ge(stored, T["stored"][("sg3", layer)])
                n0 = AT[("merge", layer, 0, 0)]
                per = N_BRANCH + 1
                with pe.Fori(0, KD // 4) as it:
                    for d in range(4):
                        for i in range(N_BRANCH):
                            b = n0 + per * d + i
                            pe.wait_ge(split_ready, 4 * per * it + (b + 1))
                            pe.wait_ge(sig_ready, 16 * it + (4 * d + i + 1 + 32 * layer))
                            w = both(w_parts, np.s_[:, b % RING, :])
                            for k in range(KD):
                                mm = passes(psum[i][:], cols_of(w, k * P, P), moved(k), k == 0, k == KD - 1)
                            mm.then_inc(block_done, 1)
                        b = n0 + per * d + N_BRANCH
                        pe.wait_ge(split_ready, 4 * per * it + (b + 1))
                        pe.wait_ge(merged, 4 * it + (d + 2 + KD * layer))
                        pe.wait_ge(parts_ready, T["parts"][("branch", layer, GATE_ORDER[-1])])
                        w = both(w_parts, np.s_[:, b % RING, :])
                        for i in range(N_BRANCH):
                            for k in range(2):
                                j = 2 * i + k
                                mm = passes(psum[4 + i][:], cols_of(w, j * P, P), both(branch, np.s_[:, j, :]), k == 0, k == 1)
                        mm.then_inc(block_done, 1)
                pe.wait_ge(merged, 2 + KD * (layer + 1))
                for n in range(KD):
                    if n >= 4:
                        pe.wait_ge(x_next, KD * layer + n - 3)
                    project(("out2", layer, n), psum[n % 4][:], lambda k: both(acc, np.s_[:, k, :]))

            stages_pe2 = []
            for layer in range(DEPTH):
                stages_pe2 += [lambda l=layer: sum_rms(l), lambda l=layer: project_second(l),
                               lambda: None, lambda l=layer: heads_second(l),
                               lambda l=layer: merge(l)]
            stages_pe2 += [lambda: sum_rms(DEPTH)]

            stages = [
                mixer_a, lambda: (heads_ab("A"), mixer_b()), lambda: heads_ab("B"), lambda: mixer_out(0), lambda: residual_norm(0),
                lambda: feed_forward(1), lambda: residual_norm(1), lambda: per_layer(0),
                mixer_c, heads_c, lambda: mixer_out(2), lambda: residual_norm(2),
                lambda: feed_forward(3), lambda: residual_norm(3), lambda: per_layer(1),
            ]
            stages += stages_pe2
            for stage in stages:
                stage()

        @block.scalar
        def _(act):
            linked = [0]

            def link(ins):
                linked[0] += 1
                ins.then_inc(link_act, 1)
                act.wait_ge(link_act, linked[0])

            def raw(job, dst, src, scale=1.0, bias=None):
                if bias is None:
                    ins = act.activation(dst, src, ACT.Copy, scale=scale)
                else:
                    ins = act.activation(dst, src, ACT.Identity, bias=bias, scale=scale)
                ins.then_inc(rope_raw, 1)

            def upper(key, dst, src):
                act.activation(dst, src, ACT.Copy).then_inc(hi_ready, 1)

            def values(keys, blk, dst, src):
                act.wait_ge(block_done, done(blk))
                for i, _ in enumerate(keys):
                    act.activation(dst(i), src(i), ACT.Copy).then_inc(v_stored, 1)

            def pairs(v):
                return v.rearrange("p j (t d) -> p j t d", t=3)[:, :, 0:3:2, :]

            def deviation(key, bank, count, eps, buf):
                act.wait_ge(summed, T["summed"][key])
                act.activation(std[:, buf, :], bank[:], ACT.Sqrt, bias=eps, scale=1.0 / count).then_inc(std_ready, 1)

            def attention(units, blend=False, causal=False, copies=True):
                turns = [(u, i) for u in units for i in range(ST)]
                comps = 2 if blend else 1

                def copy_turned(u, i):
                    t, n = TURN_AT[(u, i)], UNIT_AT[u]
                    act.wait_ge(turned, t + 1)
                    if i == 0 and n >= 2:
                        act.wait_ge(weighed, n - 1)
                    kt = i + 1 if causal else ST
                    act.activation(pt[:, n % 2, 0:kt, i * P:i * P + P],
                                   psum[4 + t % 2][:, 0:kt * P].rearrange("p (k q) -> p k q", k=kt),
                                   ACT.Copy).then_inc(pt_stored, 1)

                for n, (u, i) in enumerate(turns):
                    for c in range(comps):
                        s = SCORE_AT[(u, i, c)]
                        act.wait_ge(maxed, s + 1)
                        t = TURN_AT[(u, i)]
                        back = 2 if blend else 4
                        if t >= back:
                            act.wait_ge(turned, t - back + 1)
                        w = (i + 1) * P if causal else S
                        act.activation(prob[:, s % 4, 0:w], psum[s % 4][:, 0:w], ACT.Exp, bias=negmax[:, s % 8:s % 8 + 1],
                                       accum_out=rowsum[:, s % 8:s % 8 + 1] if blend else None).then_inc(exped, 1)
                    if n and copies:
                        copy_turned(*turns[n - 1])
                if copies:
                    copy_turned(*turns[-1])

            def load_p(layer):
                act.dma_start(p_in_t, dram["p_t"][:, layer * 2 * S:layer * 2 * S + 2 * S].rearrange(
                    "p (t s) -> p t s", t=2)).then_inc(p_loaded, 16)

            def setup():
                for i in range(KD // 2):
                    act.dma_start(x[:, 2 * i:2 * i + 2, :], dram["x_t"][:, 2 * i * S:2 * i * S + 2 * S].rearrange(
                        "p (t s) -> p t s", t=2)).then_inc(x_in[i], 16)
                act.dma_start(pos_raw, dram["positions"]).then_inc(inputs_in, 16)
                act.dma_start(cols[:, :], dram["columns"]).then_inc(inputs_in, 16)
                lo = TABS["count"]
                act.dma_start(lam_in, dram["lam"]).then_inc(inputs_in, 16)
                act.dma_start(tabs[:, :], dram["tables"][:, 0:lo]).then_inc(inputs_in, 16)
                act.dma_start(masks_in, dram["tables"][:, lo + ST * S:lo + ST * S + S + P]).then_inc(inputs_in, 16)
                act.dma_start(count, dram["tables"][:, lo:lo + ST * S].rearrange("p (q k) -> p q k", q=ST)).then_inc(
                    inputs_in, 16)
                act.dma_start(small_w[:, :], dram["small_w"]).then_inc(inputs_in, 16)
                act.dma_start(cmp_pos[:, :], dram["cmp_pos"]).then_inc(inputs_in, 16)
                act.dma_start(b2v[:, :], dram["b2v"]).then_inc(inputs_in, 16)
                load_p(0)
                for n in range(KD):
                    act.wait_ge(x_in[n // 2], 16)
                    upper(("x", 0, n), moving[0][:, n, :], x[:, n, :])
                act.nop().then_inc(sig_ready, N_BRANCH)
                act.wait_ge(setup_dve, SETUP["rest"])
                act.activation(sin_a, rest[:, 0, :], ACT.Sin)
                act.activation(sin_b, rest[:, 1, :], ACT.Sin)
                act.activation(angle[:, :, :], rest[:, :, :], ACT.Sin, scale=0.5).then_inc(setup_act, 1)
                act.wait_ge(setup_dve, SETUP["lam_sums"])
                act.activation(neg_lam[:, 2:4], neg_lam[:, 0:2], ACT.Exp).then_inc(setup_act, 1)

            def mixer_a():
                act.wait_ge(cleared, 1)
                values(range(4), ("vA", 3), lambda i: pairs(v_ab[:, i]),
                       lambda i: psum[i][:].rearrange("p (j t d) -> p j t d", j=4, t=2))
                for t in range(8):
                    act.wait_ge(block_done, done(("qkA", t)))
                    raw(("qkA", t), qk_a[:, t, :], psum[t % 4][:], HD ** -0.5 if t < 4 else 1.0)
                for n in range(5):
                    act.wait_ge(block_done, done(("lat", n)))
                    act.activation(lat[:, n, :], psum[n % 4][:], ACT.Copy).then_inc(lat_raw, 1)
                act.wait_ge(block_done, done(("kpe", 0)))
                raw(("kpe",), kpe[0:B_QK, :], psum[1][0:B_QK, :])
                act.wait_ge(lat_raw, 5)
                for n in range(5):
                    act.activation(lat_square[:, n, :], lat[:, n, :], ACT.Square).then_inc(squared, 1)
                deviation(("lat", 0), psum[6], Q_LORA, col("eps_rms"), 0)
                deviation(("lat", 1), psum[7], KV_LORA, col("eps_rms"), 1)

            def mixer_b():
                for h in range(B_HEADS):
                    act.wait_ge(block_done, done(("qup", h // 3)))
                    raw(("qB", h), q_b[0:B_QK, h, :], psum[h % 4][0:B_QK, :], B_QK ** -0.5)
                act.wait_ge(block_done, done(("kvk", 0)))
                for h in range(B_HEADS):
                    act.activation(k_b[0:B_NOPE, h, :], psum[h // 2][HD * (h % 2):HD * (h % 2) + HD, :],
                                   ACT.Copy).then_inc(kb_stored, 1)
                values(range(4), ("kvv", 0), lambda i: pairs(v_ab[:, i]),
                       lambda i: psum[i][:].rearrange("p (j t d) -> p j t d", j=4, t=2))

            def split_mix(layer, last, tiles):
                act.wait_ge(block_done, done(last))
                for n in tiles:
                    if layer == 0:
                        act.wait_ge(attended, UNIT_AT[("A" if n < 4 else "B", 2 * (n % 4) + 1)] + 1)
                    else:
                        act.wait_ge(normed, T["normed"][("C", n)])
                    upper(("mix", layer, n), moving[0][:, n, :], mix[:, n, :])

            def norm_squares(i):
                src = z_ffn if i % 2 else z
                for n in range(KD):
                    act.wait_ge(centered, KD * i + n + 1)
                    act.activation(square[:, n, :], src[:, n, :], ACT.Square).then_inc(squared, 1)
                deviation(("ln", i), psum[7], D, col("eps_ln"), 0)
                name = ("ln_mix_b", "ln_ffn_b")[i % 2]
                for n in range(KD):
                    act.wait_ge(normed, T["normed"][("ln", i, n)])
                    act.activation(moving[0][:, n, :], src[:, n, :], ACT.Identity,
                                   bias=col(name, KD * (i // 2) + n)).then_inc(hi_ready, 1)

            def feed_forward(i):
                layer = i // 2
                n0 = AT[("gate", layer, 0)]
                act.wait_ge(p_loaded, 16 * (layer + 1))
                upper(("p", layer), p_parts[0][:, :, :], p_in_t)
                with act.Fori(0, KF // 2) as it:
                    for par in range(2):
                        w1 = COLS["conv_w"] + layer * 3 * KF + KF + par
                        b = COLS["conv_b"] + layer * KF + par
                        act.wait_ge(block_done, 4 * it + (n0 + 2 * par + 1))
                        act.activation(conv_t[:, par, :], psum[par][:], ACT.Identity,
                                       scale=cols[:, bass.ds(2 * it + w1, 1)],
                                       bias=cols[:, bass.ds(2 * it + b, 1)]).then_inc(conv_mid, 1)
                        act.wait_ge(conv_done, 2 * it + (par + 1 + KF * layer))
                        act.activation(gelu_t[:, par, :], conv_t[:, par, :], ACT.Gelu_apprx_tanh).then_inc(gelu_done, 1)
                        act.wait_ge(hid_ready, 2 * it + (par + 3 + KF * layer))
                        act.activation(hid[0][:, 2 * it + par, :], gelu_t[:, par, :], ACT.Copy).then_inc(hid_hi, 1)

            def per_layer(layer):
                for n in range(KD):
                    act.wait_ge(block_done, done(("plegate", layer, n)))
                    act.activation(sig_p[:, n, :], psum[n % 4][:], ACT.Sigmoid).then_inc(ple_sig, 1)
                if layer == 0:
                    act.wait_ge(parts_ready, T["parts"][("p", 0)])
                    load_p(1)
                    for n in range(KD):
                        act.wait_ge(x_ple, n + 1)
                        upper(("x", 1, n), moving[0][:, n, :], x[:, n, :])
                else:
                    act.wait_ge(parts_ready, T["parts"][("p", 1)])
                    act.dma_start(late, dram["tables"][:, TABS["cos2"]:NTABS]).then_inc(late_in, 16)

            def heads_ab(kind):
                attention([u for u in UNITS if u[0] == kind], copies=kind == "B")
                if kind == "B":
                    split_mix(0, ("kvv", 0), range(KD))

            def mixer_c():
                for half in range(2):
                    act.wait_ge(block_done, done(("vC", 4 * half + 3)))
                    for st in range(ST):
                        act.activation(v_c[:, st, S * half:S * half + S], psum[4 * half + st][:],
                                       ACT.Copy).then_inc(v_stored, 1)
                for t in range(16):
                    act.wait_ge(block_done, done(("qkC", t)))
                    raw(("qkC", t), qk_c[:, t, :], psum[t % 4][:], HD ** -0.5 if t < 8 else 1.0)

            def heads_c():
                units = [u for u in UNITS if u[0] == "C"]
                attention(units, blend=True)
                for n in range(C_HEADS):
                    act.wait_ge(attended, UNIT_AT[("C", n)] + 1)
                    act.activation(square[:, n, :], mix[:, n, :], ACT.Square).then_inc(squared, 1)
                for n in range(C_HEADS):
                    if n >= 2:
                        act.wait_ge(normed, T["normed"][("C", n - 2)])
                    deviation(("C", n), psum[4 + n % 2], P, col("eps_ln"), n % 2)
                    if n >= 2:
                        split_mix(1, ("qkC", 15), (n - 2,))
                split_mix(1, ("qkC", 15), (C_HEADS - 2, C_HEADS - 1))

            def rms(i):
                for n in range(KD):
                    if i == 0:
                        act.wait_ge(x_ple, KD * DEPTH - KD + n + 1)
                    else:
                        act.wait_ge(x_next, KD * (i - 1) + n + 1)
                    act.activation(z[:, n, :], x[:, n, :], ACT.Square).then_inc(squared, 1)
                deviation(("rms", i), psum[7], D, col("eps_rms"), 0)
                for n in range(KD if i < DEPTH else 0):
                    act.wait_ge(normed, T["normed"][("rms", i, n)])
                    upper(("h2", i, n), moving[0][:, n, :], z[:, n, :])

            def store(dst, src, func=ACT.Copy, **more):
                act.activation(dst, src, func, **more).then_inc(stored, 1)

            def project_second(layer):
                at = lambda key: act.wait_ge(block_done, done(key))
                at(("small", layer))
                store(gate_sig, psum[0][:], ACT.Sigmoid)
                store(mix[:, 6, :], psum[0][:], ACT.Identity, bias=col("fox_bias", layer))
                act.wait_ge(stored, T["stored"][("fl", layer)])
                link(act.activation(mix[:, 7, :], mix[:, 6, :], ACT.Abs))
                link(act.activation(mix[:, 7, :], mix[:, 7, :], ACT.Exp, scale=-1.0))
                store(mix[:, 0, :], mix[:, 7, :], ACT.Ln, bias=ones[:, 0:1])
                at(("kcvc", layer))
                store(kcvc, psum[1][:])
                at(("vsvw", layer))
                act.wait_ge(prepared, T["prepared"][("blocks", layer)])
                for c in range(2):
                    rows = slice(HD * c, HD * c + HD)
                    ins = act.activation(blocks[rows, :, 0, c, :], blocks_x[rows], ACT.Copy)
                ins.then_inc(hi_ready, 1)
                for c, v in ((0, v_s), (1, v_w)):
                    store(v[:, :, HD:2 * HD], psum[2][:].rearrange("p (t c d) -> p t c d", t=ST, c=2)[:, :, c, :])
                at(("ks", layer))
                raw(("ks", layer), ksw[:, 0, :], psum[3][:])
                at(("kw", layer))
                raw(("kw", layer), ksw[:, 1, :], psum[0][:])
                for t in range(2):
                    at(("nq", layer, t))
                    raw((f"nq{t}", layer), nq[:, t, :], psum[1 + t][:], HD ** -0.5)
                act.wait_ge(prepared, T["prepared"][("hid", layer)])
                store(hid_k, hid_sum[:, 0, 0:CMP_N], ACT.Silu, bias=col("cmp_b1", 2 * layer))
                store(hid_v, hid_sum[:, 0, CMP_N:2 * CMP_N].unsqueeze(1).broadcast_to([P, 4, CMP_N]), ACT.Silu,
                      bias=col("cmp_b1", 2 * layer + 1))
                act.wait_ge(compress_step, 5 * layer + 1)
                raw(("kc", layer), kc, psum[7][:, 0:CMP_N], 1.0, col("cmp_b2k", layer))
                for t in range(2):
                    at(("fq", layer, t))
                    store(fqk[:, t, :], psum[t][:], scale=HD ** -0.5)
                for t in range(2):
                    at(("fk", layer, t))
                    store(fqk[:, 2 + t, :], psum[2 + t][:])
                act.wait_ge(prepared, T["prepared"][("cmp_shift", layer)])
                store(rstd[:, 1, :], std[:, 1, :], ACT.Exp)
                at(("fv", layer, 1))
                for st in range(ST):
                    store(pairs(v_f[:, st]), psum[st][:, 0:256].rearrange("p (j t d) -> p j t d", j=2, t=2))
                for t in range(2):
                    at(("pool", layer, t))
                    store(pool_u[:, t, PAD:PAD + S], psum[t][:])
                for t in range(4):
                    at(("conv", layer, t))
                    store((conv_x if t < 2 else conv_b)[:, t % 2, :], psum[(2 + t) % 4][:])
                for n in range(6):
                    act.wait_ge(spread, 10 * layer + n + 1)
                    store(gates[:, n // 2, n % 2, :], psum[n % 4][:])
                for g in range(4):
                    act.wait_ge(spread, 10 * layer + 6 + g + 1)
                    rows = slice(HD * (g % 2), HD * (g % 2) + HD)
                    store(mix[rows, 2 + g // 2, :], psum[(g + 2) % 4][rows, :],
                          scale=col("pool_scale", 2 * layer + g // 2, rows))

            def heads_second(layer):
                attention([u for u in UNITS if len(u) == 3 and u[1] == layer], causal=True)

            def merge(layer):
                for t in range(KD):
                    act.wait_ge(block_done, done(("sgate", layer, t)))
                    store(sg[:, t, :], psum[t][:], ACT.Silu)
                for t in GATE_ORDER:
                    act.wait_ge(gated, KD * layer + GATE_ORDER.index(t) + 1)
                    upper(("branch", layer, t), branch[0][:, t, :], mix[:, t, :])
                n0 = AT[("merge", layer, 0, 0)]
                with act.Fori(0, KD // 4) as it:
                    for d in range(4):
                        act.wait_ge(merged, 4 * it + (d + 1 + KD * layer))
                        for i in range(N_BRANCH):
                            act.wait_ge(block_done, 20 * it + (n0 + 5 * d + i + 1))
                            act.activation(sig_m[:, d % 2, i, :], psum[i][:], ACT.Sigmoid).then_inc(sig_ready, 1)

            stages = [
                lambda: (setup(), mixer_a()), lambda: (heads_ab("A"), mixer_b()), lambda: heads_ab("B"), lambda: None, lambda: norm_squares(0),
                lambda: feed_forward(1), lambda: norm_squares(1), lambda: per_layer(0),
                mixer_c, heads_c, lambda: None, lambda: norm_squares(2),
                lambda: feed_forward(3), lambda: norm_squares(3), lambda: per_layer(1),
            ]
            for layer in range(DEPTH):
                stages += [lambda l=layer: rms(l), lambda l=layer: project_second(l), lambda: None,
                           lambda l=layer: heads_second(l), lambda l=layer: merge(l)]
            stages += [lambda: rms(DEPTH)]
            for stage in stages:
                stage()

        @block.vector
        def _(dve):
            linked = [0]

            def link(ins):
                linked[0] += 1
                ins.then_inc(link_dve, 1)
                dve.wait_ge(link_dve, linked[0])

            def rope(job, tile, rows, cos, sin, n=S):
                g = ROPE_AT[job]
                dve.wait_ge(rope_perm, g + 1)
                tmp = rope_tmp[0:rows, g % 2, 0:n]
                dve.tensor_tensor(tmp, psum[4 + g % 2][0:rows, 0:n], sin, ALU.mult)
                link(dve.tensor_tensor(tile, tile, cos, ALU.mult))
                dve.tensor_tensor(tile, tile, tmp, ALU.add).then_inc(roped, 1)

            def lower(key, pair, src):
                dve.wait_ge(hi_ready, T["parts"][key])
                dve.tensor_tensor(pair[1], src, pair[0].bitcast(F32), ALU.subtract).then_inc(parts_ready, 1)

            def inverse(dst, src, rows):
                link(dve.transpose(dst, src))
                few = inverse_tmp[rows, :]
                link(dve.reciprocal(few, dst.rearrange("p (b r) -> p b r", r=32)[:, :, 0]))
                link(dve.transpose(dst, few.unsqueeze(2).broadcast_to([rows.stop - rows.start, S // 32, 32])))

            def normalize(key, tiles, gains, buf, behind=None):
                dve.wait_ge(std_ready, T["std"][key])
                inverse(rstd[:, buf, :], std[:, buf, :], slice(0, P))
                for n, (dst, src) in enumerate(tiles):
                    dve.scalar_tensor_tensor(out=dst, in0=src, scalar=gains(n), in1=rstd[:, buf, :], op0=ALU.mult,
                                             op1=ALU.mult).then_inc(normed, 1)
                    if behind and n >= 2:
                        behind(n - 2)
                for n in range(max(len(tiles) - 2, 0) if behind else len(tiles), len(tiles)):
                    behind(n)

            def attention(units, finish, blend=False, causal=False, counts=False, first=()):
                turns = [(u, i) for u in units for i in range(ST)]
                comps = 2 if blend else 1

                def mixed(u, i):
                    s, t = SCORE_AT[(u, i, 0)], TURN_AT[(u, i)]
                    c = s % 8
                    dve.wait_ge(exped, s + 2)
                    link(dve.reciprocal(rownorm[:, c:c + 2], rowsum[:, c:c + 2]))
                    link(dve.tensor_tensor(rownorm[:, c + 1:c + 2], rownorm[:, c + 1:c + 2], neg_lam[:, 5:6], ALU.mult))
                    p0, p1 = prob[:, s % 4, :], prob[:, (s + 1) % 4, :]
                    link(dve.tensor_scalar(p0, p0, rownorm[:, c:c + 1], None, ALU.mult))
                    dve.scalar_tensor_tensor(out=p0, in0=p1, scalar=rownorm[:, c + 1:c + 2], in1=p0, op0=ALU.mult,
                                             op1=ALU.add).then_inc(blended, 1)

                def counted(u, i):
                    t, n = TURN_AT[(u, i)], UNIT_AT[u]
                    dve.wait_ge(turned, t + 1)
                    if i == 0 and n >= 2:
                        dve.wait_ge(weighed, n - 1)
                    dve.tensor_tensor(pt[:, n % 2, :, i * P:i * P + P], psum[4 + t % 2][:].rearrange("p (k q) -> p k q", k=ST),
                                      count[:, :, i * P:i * P + P], ALU.mult).then_inc(pt_stored, 1)

                pending = [(n, step) for n, step in enumerate(first)]
                for n, (u, i) in enumerate(turns):
                    for c in range(comps):
                        s = SCORE_AT[(u, i, c)]
                        w = (i + 1) * P if causal else S
                        dve.wait_ge(scored, s + 1)
                        dve.tensor_reduce(negmax[:, s % 8:s % 8 + 1], psum[s % 4][:, 0:w], AX_X, ALU.max,
                                          negate=True).then_inc(maxed, 1)
                    if blend and n:
                        mixed(*turns[n - 1])
                    if counts and n >= AHEAD:
                        counted(*turns[n - AHEAD])
                    if pending and pending[0][0] <= n:
                        pending.pop(0)[1]()
                    if i == ST - 1:
                        pending += [(n + FINISH_LAG + at, step) for at, step in enumerate(finish(u))]
                if blend:
                    mixed(*turns[-1])
                if counts:
                    for turn in turns[-AHEAD:]:
                        counted(*turn)
                for _, step in pending:
                    step()

            def divided(u, dst, odd, gate=None, add=False):
                n = UNIT_AT[u]
                own, other = (slice(HD, P), slice(0, HD)) if odd else (slice(0, HD), slice(HD, P))
                bank = psum[6 + n % 2]
                inv = rope_tmp[own, 0, :]

                def invert():
                    dve.wait_ge(weighed, n + 1)
                    inverse(inv, bank[other, :], own)

                def gated_inverse():
                    link(dve.tensor_tensor(inv, inv, gate[own], ALU.mult))

                def store():
                    if not add:
                        dve.tensor_tensor(dst[own], bank[own, :], inv, ALU.mult).then_inc(attended, 1)
                        return
                    link(dve.tensor_tensor(inv, bank[own, :], inv, ALU.mult))
                    dve.tensor_tensor(dst[own], dst[own], inv, ALU.add).then_inc(attended, 1)

                return [invert] + [gated_inverse] * (gate is not None) + [store]

            def setup():
                dve.nop().then_inc(hid_ready, 2)
                dve.nop().then_inc(merged, 2)
                for n in range(KD):
                    lower(("x", 0, n), both(moving, np.s_[:, n, :]), x[:, n, :])
                dve.wait_ge(inputs_in, 16 * N_INPUTS)
                n = [0]

                def step(ins):
                    n[0] += 1
                    ins.then_inc(setup_dve, 1)
                    dve.wait_ge(setup_dve, n[0])

                step(dve.tensor_copy(pos_f, pos_raw))
                for j, name in ((0, "inv_a"), (1, "inv_b")):
                    dve.tensor_scalar(angle[:, j, :], pos_f, col(name), None, ALU.mult)
                step(dve.memset(std[:, 0, 0:1], 0.0))
                step(dve.tensor_scalar(turns[:, :, :], angle[:, :, :], 1.0 / (2 * math.pi), 12582912.0, ALU.mult, ALU.add))
                step(dve.tensor_scalar(turns[:, :, :], turns[:, :, :], -12582912.0, None, ALU.add))
                step(dve.scalar_tensor_tensor(out=rest[:, :, :], in0=turns[:, :, :], scalar=-TWO_PI[0],
                                              in1=angle[:, :, :], op0=ALU.mult, op1=ALU.add))
                for part in TWO_PI[1:]:
                    step(dve.scalar_tensor_tensor(out=rest[:, :, :], in0=turns[:, :, :], scalar=-part,
                                                  in1=rest[:, :, :], op0=ALU.mult, op1=ALU.add))
                step(dve.tensor_scalar(rest[:, :, :], rest[:, :, :], 3.1415925, -3.1415925, ALU.min, ALU.max))
                assert n[0] == SETUP["rest"], n
                dve.tensor_tensor(lam_in[:, 0:HD], lam_in[:, 0:HD], lam_in[:, HD:2 * HD], ALU.mult)
                step(dve.tensor_tensor(lam_in[:, 2 * HD:3 * HD], lam_in[:, 2 * HD:3 * HD], lam_in[:, 3 * HD:4 * HD], ALU.mult))
                step(dve.tensor_reduce(neg_lam[:, 0:2], lam_in.rearrange("p (a b) -> p a b", a=2)[:, :, 0:HD], AX_X, ALU.add))
                assert n[0] == SETUP["lam_sums"], n
                dve.wait_ge(setup_act, 1)
                step(dve.tensor_tensor(angle[:, :, :], angle[:, :, :], angle[:, :, :], ALU.mult))
                dve.tensor_scalar(cos_a, angle[:, 0, :], -2.0, 1.0, ALU.mult, ALU.add)
                step(dve.tensor_scalar(cos_b, angle[:, 1, :], -2.0, 1.0, ALU.mult, ALU.add))
                dve.wait_ge(setup_act, 2)
                step(dve.tensor_tensor(neg_lam[:, 4:5], neg_lam[:, 3:4], neg_lam[:, 2:3], ALU.subtract))
                dve.tensor_scalar(neg_lam[:, 5:6], neg_lam[:, 4:5], -LAMBDA_INIT, None, ALU.add)
                dve.tensor_scalar(neg_lam[:, 6:7], col("subln"), 1.0 - LAMBDA_INIT, None, ALU.mult)
                dve.tensor_copy(ident_bf[:], ident).then_inc(constants_bf, 1)
                dve.tensor_copy(tri_bf[:], masks_in[:, S:S + P]).then_inc(constants_bf, 1)
                dve.tensor_copy(cmp_bias_bf[:], masks_in[:, 0:S]).then_inc(constants_bf, 1)
                dve.tensor_scalar(mask_a, count, 0.5, MASK, ALU.is_lt, ALU.mult).then_inc(constants_bf, 1)
                dve.wait_ge(constants_bf, 4)

            def mixer_a():
                for t in range(8):
                    rope(("qkA", t), qk_a[:, t, :], P, cos_a, sin_a)
                rope(("kpe",), kpe[0:B_QK, :], B_QK, cos_b[0:B_QK, :], sin_b[0:B_QK, :])
                dve.wait_ge(roped, ROPE_AT[("kpe",)] + 1)
                dve.tensor_copy(k_b[B_NOPE:B_QK, :, :], kpe[B_NOPE:B_QK, :].unsqueeze(1).broadcast_to(
                    [B_ROPE, B_HEADS, S])).then_inc(kpe_spread, 1)

            def mixer_b():
                for h in range(B_HEADS):
                    rope(("qB", h), q_b[0:B_QK, h, :], B_QK, cos_b[0:B_QK, :], sin_b[0:B_QK, :])

            def latent_steps():
                steps = []
                for j, (name, lo, hi) in enumerate((("q_norm", 0, 3), ("kv_norm", 3, 5))):
                    def scale(j=j, name=name, lo=lo, hi=hi):
                        normalize(("lat", j), [(lat[:, n, :], lat[:, n, :]) for n in range(lo, hi)],
                                  lambda n: col(name, n), j)
                    steps.append(scale)
                for n in range(5):
                    def split(n=n):
                        if n == 0:
                            dve.wait_ge(block_done, done(("kpe", 0)))
                            dve.wait_ge(normed, T["normed"][("lat", 4)])
                        dve.tensor_copy(moving[0][:, n, :], lat[:, n, :]).then_inc(hi_ready, 1)
                        lower(("lat", n), both(moving, np.s_[:, n, :]), lat[:, n, :])
                    steps.append(split)
                return steps

            def split_mix(layer, tiles):
                for n in tiles:
                    lower(("mix", layer, n), both(moving, np.s_[:, n, :]), mix[:, n, :])

            def heads_ab(kind):
                attention([u for u in UNITS if u[0] == kind],
                          lambda u: divided(u, mix[:, (0 if u[0] == "A" else 4) + u[1] // 2, :], u[1] % 2),
                          counts=kind == "A", first=latent_steps() if kind == "A" else ())
                if kind == "B":
                    split_mix(0, range(KD))

            def residual(i):
                layer = i // 2
                for n in range(KD):
                    if i % 2 == 0:
                        dve.wait_ge(block_done, done(("mixout", layer, n)))
                        bank = psum[n % 4]
                    else:
                        dve.wait_ge(block_done, done(("down", layer, n // 4, KF // 2 - 1)))
                        bank = psum[4 + n] if n < 4 else psum[n - 4]
                    dve.scalar_tensor_tensor(out=(z_ffn if i % 2 else z)[:, n, :], in0=x[:, n, :], scalar=ALPHA, in1=bank[:],
                                             op0=ALU.mult, op1=ALU.add).then_inc(z_ready, 1)

            def norm(i):
                t = z_ffn if i % 2 else z
                dve.wait_ge(mean_ready, i + 1)
                for n in range(KD):
                    dve.scalar_tensor_tensor(out=t[:, n, :], in0=psum[6][:], scalar=-1.0 / D, in1=t[:, n, :],
                                             op0=ALU.mult, op1=ALU.add).then_inc(centered, 1)
                gain, bias = (("ln_mix_g", "ln_mix_b"), ("ln_ffn_g", "ln_ffn_b"))[i % 2]

                def lower_biased(n):
                    hi, lo = both(moving, np.s_[:, n, :])
                    dve.wait_ge(hi_ready, T["parts"][("ln", i, n)])
                    dve.scalar_tensor_tensor(out=lo, in0=t[:, n, :], scalar=col(bias, KD * (i // 2) + n), in1=hi.bitcast(F32),
                                             op0=ALU.add, op1=ALU.subtract).then_inc(parts_ready, 1)

                normalize(("ln", i), [(t[:, n, :], t[:, n, :]) for n in range(KD)],
                          lambda n: col(gain, KD * (i // 2) + n), 0, lower_biased)
                dve.wait_ge(parts_ready, T["parts"][("ln", i, KD - 1)])
                for n in range(KD):
                    hi, lo = both(moving, np.s_[:, n, :])
                    dve.tensor_tensor(x[:, n, :], hi.bitcast(F32), lo.bitcast(F32), ALU.add)

            def feed_forward(i):
                layer = i // 2
                n0 = AT[("gate", layer, 0)]
                w = COLS["conv_w"] + layer * 3 * KF
                lower(("p", layer), both(p_parts, np.s_[:, :, :]), p_in_t)
                with dve.Fori(0, KF // 2) as it:
                    for par in range(2):
                        f1 = par + 1 + KF * layer
                        c, a = conv_t[:, par, :], psum[par]
                        dve.wait_ge(conv_mid, 2 * it + f1)
                        dve.scalar_tensor_tensor(out=c[:, 1:S], in0=a[:, 0:S - 1],
                                                 scalar=cols[:, bass.ds(2 * it + (w + par), 1)], in1=c[:, 1:S],
                                                 op0=ALU.mult, op1=ALU.add).then_inc(conv_mid2, 1)
                        dve.wait_ge(conv_mid2, 2 * it + f1)
                        dve.scalar_tensor_tensor(out=c[:, 0:S - 1], in0=a[:, 1:S],
                                                 scalar=cols[:, bass.ds(2 * it + (w + 2 * KF + par), 1)], in1=c[:, 0:S - 1],
                                                 op0=ALU.mult, op1=ALU.add).then_inc(conv_done, 1)
                        dve.wait_ge(gelu_done, 2 * it + f1)
                        dve.wait_ge(block_done, 4 * it + (n0 + 2 * par + 2))
                        dve.tensor_tensor(gelu_t[:, par, :], gelu_t[:, par, :], psum[2 + par][:],
                                          ALU.mult).then_inc(hid_ready, 1)
                        dve.wait_ge(hid_hi, 2 * it + f1)
                        tile = 2 * it + par
                        dve.tensor_tensor(hid[1][:, tile, :], gelu_t[:, par, :], hid[0][:, tile, :].bitcast(F32),
                                          ALU.subtract).then_inc(hid_parts, 1)

            def per_layer(layer):
                for n in range(KD):
                    dve.wait_ge(ple_sig, KD * layer + n + 1)
                    dve.wait_ge(block_done, done(("pleproj", layer, n // 4)))
                    dve.tensor_tensor(sig_p[:, n, :], sig_p[:, n, :], psum[4 + n % 4][:], ALU.mult).then_inc(ple_term, 1)
                    dve.wait_ge(ple_term, KD * layer + n + 1)
                    dve.tensor_tensor(x[:, n, :], x[:, n, :], sig_p[:, n, :], ALU.add).then_inc(x_ple, 1)
                for n in range(KD if layer == 0 else 0):
                    lower(("x", 1, n), both(moving, np.s_[:, n, :]), x[:, n, :])

            def mixer_c():
                for t in range(16):
                    rope(("qkC", t), qk_c[:, t, :], P, cos_a, sin_a)

            def heads_c():
                def finish(u):
                    n = UNIT_AT[u]

                    def store():
                        dve.wait_ge(weighed, n + 1)
                        dve.tensor_copy(mix[:, u[1], :], psum[6 + n % 2][:]).then_inc(attended, 1)

                    return [store]

                attention([u for u in UNITS if u[0] == "C"], finish, blend=True)
                for n in range(C_HEADS):
                    normalize(("C", n), [(mix[:, n, :], mix[:, n, :])], lambda _: neg_lam[:, 6:7], n % 2)
                    if n:
                        split_mix(1, (n - 1,))
                split_mix(1, (C_HEADS - 1,))

            def rms(i):
                name, lo = ("norm2_g", KD * i) if i < DEPTH else ("final_g", 0)
                behind = (lambda n: lower(("h2", i, n), both(moving, np.s_[:, n, :]), z[:, n, :])) if i < DEPTH else None
                normalize(("rms", i), [(z[:, n, :], x[:, n, :]) for n in range(KD)], lambda n: col(name, lo + n), 0, behind)

            def project_second(layer):
                stored_at = lambda key: dve.wait_ge(stored, T["stored"][(key, layer)])
                for v in (v_s, v_w):
                    dve.memset(v.rearrange("p t (c d) -> p t c d", c=3)[:, :, 0:3:2, :], 1.0).then_inc(cleared, 1)
                dve.memset(v_f.rearrange("p t j (c d) -> p (t j) c d", c=3)[:, :, 1, :], 1.0).then_inc(cleared, 1)
                dve.memset(vc_bd, 0.0).then_inc(cleared, 1)
                dve.memset(conv_u[:, :, 0:2], 0.0).then_inc(cleared, 1)
                dve.memset(mix[:, 1, :], 0.0).then_inc(cleared, 1)
                dve.wait_ge(parts_ready, T["parts"][("h2", layer, KD - 1)])
                for c in range(2):
                    dve.memset(blocks[HD * c:HD * c + HD, :, :, 1 - c, :].bitcast(F32), 0.0).then_inc(cleared, 1)
                dve.memset(blocks_x[:, :, CMP_N - 1:CMP_N], 0.0).then_inc(cleared, 1)
                dve.wait_ge(cleared, 1 + N_CLEAR * layer + 9)
                stored_at("kcvc")
                by_16 = kcvc.rearrange("p (n l) -> p l n", l=CMP_STRIDE)
                pos = cmp_pos[:, layer * CMP_LEN:layer * CMP_LEN + CMP_LEN]
                for j in range(2):
                    ins = dve.tensor_tensor(
                        blocks_x[:, 16 * j:16 * j + 16, 0:CMP_N - 1], by_16[:, :, j:j + CMP_N - 1],
                        pos[:, 16 * j:16 * j + 16].unsqueeze(2).broadcast_to([P, 16, CMP_N - 1]), ALU.add)
                ins.then_inc(prepared, 1)
                dve.wait_ge(hi_ready, T["parts"][("blocks", layer)])
                for c in range(2):
                    rows = slice(HD * c, HD * c + HD)
                    ins = dve.tensor_tensor(blocks[rows, :, 1, c, :], blocks_x[rows], blocks[rows, :, 0, c, :].bitcast(F32),
                                            ALU.subtract)
                ins.then_inc(parts_ready, 1)
                dve.wait_ge(late_in, 16)
                cos2, sin2 = tab("cos2", S), tab("sin2", S)
                rope(("ks", layer), ksw[:, 0, :], P, cos2, sin2)
                rope(("kw", layer), ksw[:, 1, :], P, cos2, sin2)
                rope(("nq0", layer), nq[:, 0, :], P, cos2, sin2)
                dve.wait_ge(block_done, done(("w1", layer, 3)))
                link(dve.tensor_copy(hid_sum[:, 1, :], psum[3][:, 2 * CMP_N:4 * CMP_N]))
                dve.tensor_tensor(hid_sum[:, 0, :], psum[3][:, 0:2 * CMP_N], hid_sum[:, 1, :], ALU.add).then_inc(prepared, 1)
                rope(("nq1", layer), nq[:, 1, :], P, cos2, sin2)
                dve.wait_ge(compress_step, 5 * layer + 2)
                for h in range(4):
                    rows = slice(32 * h, 32 * h + 32)
                    ins = dve.tensor_tensor(vc_bd[rows, h // 2, HD * (h % 2):HD * (h % 2) + HD], psum[3][rows, 0:HD],
                                            b2v[rows, layer * HD:layer * HD + HD], ALU.add)
                ins.then_inc(prepared, 1)
                rope(("kc", layer), kc, P, tab("cos2c", CMP_N), tab("sin2c", CMP_N), CMP_N)
                stored_at("ln")
                link(dve.scalar_tensor_tensor(out=mix[:, 6, :], in0=mix[:, 6, :], scalar=0.0, in1=mix[:, 0, :],
                                              op0=ALU.min, op1=ALU.subtract))
                link(dve.tensor_tensor_scan(mix[:, 7, :], mix[:, 6, :], mix[:, 1, :], 0.0, ALU.add, ALU.add))
                dve.tensor_scalar(cq, mix[:, 7, :], col("cq_mul"), col("cq_add"), ALU.mult, ALU.add)
                dve.tensor_scalar(ck, mix[:, 7, :], col("ck_mul"), col("ck_add"), ALU.mult, ALU.add).then_inc(prepared, 1)
                dve.wait_ge(compress_step, 5 * layer + 3)
                for odd in range(2):
                    s8 = psum[6 + odd][:, 0:2 * P].rearrange("p (a n) -> p a n", n=CMP_N)
                    best = cmp_negmax[:, 8 * odd:8 * odd + 8]
                    link(dve.tensor_reduce(best, s8, AX_X, ALU.max, negate=True))
                    ins = dve.tensor_tensor(
                        std[:, 1, :].rearrange("p (a b n) -> p a b n", b=2, n=CMP_N)[:, :, odd, :], s8,
                        best.unsqueeze(2).broadcast_to([P, 8, CMP_N]), ALU.add)
                ins.then_inc(prepared, 1)
                dve.wait_ge(compress_step, 5 * layer + 4)
                dve.tensor_tensor(prob[:, 3, :], psum[7][:], tab("cmp_mask", S), ALU.mult).then_inc(prepared, 1)
                for t in (pool_u, pool_a, pool_b):
                    dve.memset(t[:, :, 0:PAD], 0.0).then_inc(cleared, 1)
                dve.wait_ge(cleared, 1 + N_CLEAR * (layer + 1))
                stored_at("pool1")
                u, a, b = pool_u, pool_a, pool_b
                end = PAD + S
                step = lambda dst, src, w: link(dve.tensor_tensor(dst[:, :, 2 * w:end], src[:, :, 2 * w:end],
                                                                  src[:, :, w:end - w], ALU.add))

                def mean(src, g):
                    rows = slice(HD * (g % 2), HD * (g % 2) + HD)
                    link(dve.tensor_tensor(mix[rows, 2 + g // 2, :], src[rows, g // 2, PAD:end],
                                           inv_count[rows, g // 2, :], ALU.mult))

                step(a, u, 1)
                step(b, a, 2)
                mean(a, 0)
                mean(b, 1)
                step(a, b, 4)
                step(b, a, 8)
                mean(a, 2)
                mean(b, 3)
                dve.tensor_tensor(mix[:, 2:4, :], mix[:, 2:4, :], u[:, :, PAD:end], ALU.subtract).then_inc(prepared, 1)
                stored_at("cb1")
                for t in range(2):
                    dve.wait_ge(block_done, done(("conv", layer, 4 + t)))
                    dve.tensor_tensor(conv_u[:, t, 2:2 + S], psum[2 + t][:],
                                      conv_x[:, t, :], ALU.mult).then_inc(prepared, 1)
                dve.wait_ge(prepared, T["prepared"][("cu1", layer)])
                for t in range(2):
                    y = mix[:, 4 + t, :]
                    wcol = lambda k: col("conv2_w", 6 * layer + 2 * k + t)
                    link(dve.tensor_scalar(y, conv_u[:, t, 0:S], wcol(0), None, ALU.mult))
                    for k in (1, 2):
                        link(dve.scalar_tensor_tensor(out=y, in0=conv_u[:, t, k:k + S], scalar=wcol(k), in1=y,
                                                      op0=ALU.mult, op1=ALU.add))
                    dve.tensor_tensor(y, y, conv_b[:, t, :], ALU.mult).then_inc(prepared, 1)
                dve.wait_ge(compress_step, 5 * layer + 5)
                stored_at("g5")
                for j in range(2):
                    inv = rope_tmp[:, j, :]
                    link(dve.tensor_scalar(inv, psum[6 + j][:], 0.5, None, ALU.max))
                    inverse(std[:, j, :], inv, slice(0, P))
                    link(dve.tensor_tensor(inv, std[:, j, :], gates[:, 0, j, :], ALU.mult))
                    dve.tensor_tensor(mix[:, j, :], psum[4 + j][:], inv, ALU.mult).then_inc(prepared, 1)
                dve.wait_ge(prepared, T["prepared"][("cmp_out", layer)])

            def heads_second(layer):
                def finish(u):
                    h = u[2]
                    if u[0] == "fox":
                        return divided(u, mix[:, 6 + h // 2, :], h % 2)
                    else:
                        return divided(u, mix[:, h // 2, :], h % 2, gates[:, 1 if u[0] == "slc" else 2, h // 2, :], True)

                attention([u for u in UNITS if len(u) == 3 and u[1] == layer], finish, causal=True)

            def merge(layer):
                for t in GATE_ORDER:
                    if t in (0, 1, 6, 7):
                        dve.wait_ge(attended, UNIT_AT[("win" if t < 2 else "fox", layer, 2 * (t % 2) + 1)] + 1)
                    dve.wait_ge(stored, T["stored"][(f"sg{t}", layer)])
                    dve.tensor_tensor(mix[:, t, :], mix[:, t, :], sg[:, t, :], ALU.mult).then_inc(gated, 1)
                for t in GATE_ORDER:
                    lower(("branch", layer, t), both(branch, np.s_[:, t, :]), mix[:, t, :])
                n0 = AT[("merge", layer, 0, 0)]
                with dve.Fori(0, KD // 4) as it:
                    for d in range(4):
                        t = sig_m[:, d % 2]
                        dve.wait_ge(block_done, 20 * it + (n0 + 5 * d + N_BRANCH + 1))
                        dve.wait_ge(sig_ready, 16 * it + (4 * d + 4 + 4 + 32 * layer))
                        for i in range(N_BRANCH):
                            ins = dve.tensor_tensor(t[:, i, :], t[:, i, :], psum[4 + i][:], ALU.mult)
                        ins.then_inc(merge_link, 1)
                        dve.wait_ge(merge_link, 16 * it + (4 * d + 1 + 32 * layer))
                        ins = dve.tensor_tensor(t[:, 0:2, :], t[:, 0:2, :], t[:, 2:4, :], ALU.add)
                        ins.then_inc(merge_link, 1)
                        dve.wait_ge(merge_link, 16 * it + (4 * d + 2 + 32 * layer))
                        ins = dve.tensor_tensor(t[:, 0, :], t[:, 0, :], t[:, 1, :], ALU.add)
                        ins.then_inc(merge_link, 1)
                        dve.wait_ge(merge_link, 16 * it + (4 * d + 3 + 32 * layer))
                        hi, lo = both(acc, np.s_[:, 4 * it + d, :])
                        dve.tensor_copy(hi, t[:, 0, :]).then_inc(merge_link, 1)
                        dve.wait_ge(merge_link, 16 * it + (4 * d + 4 + 32 * layer))
                        dve.tensor_tensor(lo, t[:, 0, :], hi.bitcast(F32), ALU.subtract).then_inc(merged, 1)
                for n in range(KD):
                    dve.wait_ge(block_done, done(("out2", layer, n)))
                    dve.tensor_tensor(x[:, n, :], psum[n % 4][:], x[:, n, :], ALU.add).then_inc(x_next, 1)

            stages = [
                lambda: (setup(), mixer_a()), lambda: (heads_ab("A"), mixer_b()), lambda: heads_ab("B"), lambda: residual(0), lambda: norm(0),
                lambda: feed_forward(1), lambda: (residual(1), norm(1)), lambda: per_layer(0),
                mixer_c, heads_c, lambda: residual(2), lambda: norm(2),
                lambda: feed_forward(3), lambda: (residual(3), norm(3)), lambda: per_layer(1),
            ]
            for layer in range(DEPTH):
                stages += [lambda l=layer: rms(l), lambda l=layer: project_second(l), lambda: None,
                           lambda l=layer: heads_second(l), lambda l=layer: merge(l)]
            stages += [lambda: rms(DEPTH)]
            for stage in stages:
                stage()

        @block.gpsimd
        def _(pool):
            pool.memset(unit[:, :], 1.0).then_inc(unit_set, 1)
            pool.memset(v_ab.rearrange("p t j (c d) -> p (t j) c d", c=3)[:, :, 1, :], 1.0).then_inc(cleared, 1)
            pool.wait_ge(unit_set, 1)

            def split(s, n, used=None):
                pool.wait_ge(full[s], 16 * (n // RING) + 16 if isinstance(n, int) else used[0])
                if used:
                    pool.wait_ge(block_done, used[1])
                pool.tensor_tensor(w_parts[0][:, s, :], ring[:, s, :], unit[:, 0:1].broadcast_to([P, BLK]),
                                   ALU.mult).then_inc(split_hi, 1)
                pool.wait_ge(split_hi, n + 1)
                pool.tensor_tensor(w_parts[1][:, s, :], ring[:, s, :], w_parts[0][:, s, :].bitcast(F32),
                                   ALU.subtract).then_inc(split_ready, 1)

            for s in range(RING):
                split(s, s)
            with pool.Fori(1, len(BLOCKS) // RING) as it:
                for s in range(RING):
                    split(s, RING * it + s, (16 * it + 16, RING * it + (s - RING + 1)))
            for n in range(len(BLOCKS) // RING * RING, len(BLOCKS)):
                split(n % RING, n, (16 * (n // RING) + 16, n - RING + 1))


def kernel(**inputs):
    import concourse.bacc as bacc
    from concourse.bass_utils import run_bass_kernel_spmd

    nc = bacc.Bacc("TRN2", target_bir_lowering=False, num_devices=1)
    arrays = host_layout({k: np.asarray(v) for k, v in inputs.items()})
    dram = {name: nc.dram_tensor("in_" + name, a.shape, mybir.dt.from_np(a.dtype), kind="ExternalInput").ap()
            for name, a in arrays.items()}
    out = nc.dram_tensor("out", (P, KD, S), F32, kind="ExternalOutput").ap()
    build(nc, dram, out)
    got = run_bass_kernel_spmd(nc, [{"in_" + n: a for n, a in arrays.items()}], core_ids=[0]).results[0]["out"]
    return np.ascontiguousarray(got.transpose(2, 1, 0).reshape(1, S, D))
```

```python
import math
from contextlib import ExitStack

import numpy as np

import concourse.bass as bass
from concourse import mybir

F32 = mybir.dt.float32
F32R = mybir.dt.float32r
BF16 = mybir.dt.bfloat16
I32 = mybir.dt.int32
ALU = mybir.AluOpType
ACT = mybir.ActivationFunctionType
AX_X = mybir.AxisListType.X

P = 128
S = 512
D = 1024
KD = D // P
ST = S // P
DEPTH = 2
HD = 64
A_HEADS = 8
B_HEADS, B_NOPE, B_ROPE, B_QK = 8, 64, 32, 96
Q_LORA, KV_LORA = 384, 256
C_HEADS = 8
FF = 256 * math.ceil(8 * D / 3 / 256)
KF = FF // P
PLE = 256
LN_EPS, RMS_EPS = 1e-5, 1e-6
ALPHA = (2 * DEPTH) ** 0.25
LAMBDA_INIT = 0.8 - 0.6 * math.exp(-0.3)
ROPE_THETA, MASK = 500000.0, -1e30
N_BRANCH, BW = 4, 256
CMP_N, CMP_LEN, CMP_STRIDE = 32, 32, 16
PAD = 16
RING = 2
BLK = 1024
KB = 256


class Tally:

    def __init__(self, keys=()):
        self.value = {}
        for key in keys:
            self.add(key)

    def add(self, key):
        assert key not in self.value, key
        self.value[key] = len(self.value) + 1

    def __getitem__(self, key):
        return self.value[key]


def block_plan():
    keys = []
    keys += [("vA", i) for i in range(4)] + [("qkA", t) for t in range(8)]
    keys += [("lat", t) for t in range(5)] + [("kpe", 0)]
    keys += [("qup", i) for i in range(3)] + [("kvk", 0), ("kvv", 0)]
    for layer in range(DEPTH):
        if layer == 1:
            keys += [("vC", i) for i in range(8)] + [("qkC", t) for t in range(16)]
        keys += [("mixout", layer, n) for n in range(KD)]
        for f in range(KF):
            keys += [("gate", layer, f), ("up", layer, f)]
        keys += [("down", layer, h, i) for h in range(2) for i in range(KF // 2)]
        for half in range(2):
            keys += [("pleproj", layer, half)] + [("plegate", layer, half * 4 + n) for n in range(4)]
    for layer in range(DEPTH):
        keys += [("small", layer), ("kcvc", layer), ("vsvw", layer), ("kskw", layer)]
        for i, key in enumerate([("nq", layer, 0), ("nq", layer, 1), ("fq", layer, 0), ("fq", layer, 1)]):
            keys += [key, ("w1", layer, i)]
        keys += [("fk", layer, t) for t in range(2)]
        keys += [("fv", layer, t) for t in range(2)] + [("pool", layer, t) for t in range(2)]
        keys += [("conv", layer, t) for t in range(6)] + [("sgate", layer, t) for t in range(8)]
        for n in range(KD):
            keys += [("merge", layer, n, i) for i in range(N_BRANCH)] + [("branch", layer, n)]
        keys += [("out2", layer, n) for n in range(KD)]
    return keys


BLOCKS = block_plan()
AT = {key: n for n, key in enumerate(BLOCKS)}

COLS = {}
_at = 0
for _name, _width in [
    ("q_norm", 3), ("kv_norm", 2), ("subln", 1), ("ln_mix_g", 16), ("ln_mix_b", 16), ("conv_w", 2 * 3 * KF),
    ("conv_b", 2 * KF), ("ln_ffn_g", 16), ("ln_ffn_b", 16), ("norm2_g", 16), ("fox_bias", 2), ("cmp_b1", 4),
    ("cmp_b2k", 2), ("pool_scale", 4), ("conv2_w", 12), ("final_g", 8), ("inv_a", 1), ("inv_b", 1),
    ("eps_ln", 1), ("eps_rms", 1), ("fox_q", 3), ("fox_k", 3),
]:
    COLS[_name] = _at
    _at += _width
NCOLS = _at

TABS = {}
_at = 0
for _name, _width in [
    ("ident", P), ("ones", P), ("perm_a", P), ("perm_b", P), ("count", ST * S), ("cmp_bias", S), ("tri", P), ("cos2", S), ("sin2", S),
    ("cos2c", CMP_N), ("sin2c", CMP_N), ("inv_count", 2 * S), ("cmp_mask", S),
    ("sel", 6 * P), ("ones_bd", 2 * P),
]:
    TABS[_name] = _at
    _at += _width
NTABS = _at


def _tile(w):
    k, n = w.shape
    return w.reshape(k // P, P, n).transpose(1, 0, 2).reshape(P, -1)


def _column(v):
    return v.reshape(-1, P).T


def weight_stream(a):
    w_in, w_qkv = a["ab_w_in"][0], a["c_w_qkv"][0]
    o3 = 3 * A_HEADS * HD
    made = np.zeros((len(BLOCKS), P, BLK), np.float32)
    split2 = np.cumsum([256, 384, 12, 256, 768, 768, 4, 1024, 4096])

    def put(n, w):
        made[n, :, :w.shape[1]] = w

    for n, key in enumerate(BLOCKS):
        kind, at = key[0], key[1:]
        if kind == "vA":
            put(n, _tile(w_in[256 * at[0]:256 * at[0] + 256, 1024:1536]))
        elif kind == "qkA":
            put(n, _tile(w_in[:, P * at[0]:P * at[0] + P]))
        elif kind == "lat":
            put(n, _tile(w_in[:, o3 + P * at[0]:o3 + P * at[0] + P]))
        elif kind == "kpe":
            w = np.zeros((D, B_QK), np.float32)
            w[:, B_NOPE:] = w_in[:, o3 + Q_LORA + KV_LORA:]
            put(n, _tile(w))
        elif kind == "qup":
            w = a["ab_w_q_up"][0].reshape(Q_LORA, B_HEADS, B_QK)
            tiles = [w[:, 4 * r:4 * r + 4, B_NOPE:] for r in range(2)] + [w[:, 2 * r:2 * r + 2, :B_NOPE] for r in range(4)]
            put(n, np.concatenate([_tile(v.reshape(Q_LORA, P)) for v in tiles[2 * at[0]:2 * at[0] + 2]], 1))
        elif kind == "kvk":
            w = a["ab_w_kv_up"][0].reshape(KV_LORA, B_HEADS // 2, 2, 2, HD)[:, :, :, 0]
            put(n, np.concatenate([_tile(w[:, j].reshape(KV_LORA, P)) for j in range(B_HEADS // 2)], 1))
        elif kind == "kvv":
            put(n, _tile(a["ab_w_kv_up"][0].reshape(KV_LORA, B_HEADS, 2, HD)[:, :, 1].reshape(KV_LORA, -1)))
        elif kind == "vC":
            half, i = divmod(at[0], 4)
            put(n, _tile(w_qkv[256 * i:256 * i + 256, 2048 + S * half:2048 + S * half + S]))
        elif kind == "qkC":
            put(n, _tile(w_qkv[:, P * at[0]:P * at[0] + P]))
        elif kind == "mixout":
            put(n, _tile((a["ab_w_out"][0], a["c_w_out"][0])[at[0]][:, P * at[1]:P * at[1] + P]))
        elif kind in ("gate", "up"):
            put(n, _tile(a["ffn_w_" + kind][at[0]][:, P * at[1]:P * at[1] + P]))
        elif kind == "down":
            layer, half, i = at
            put(n, _tile(a["ffn_w_down"][layer][256 * i:256 * i + 256, S * half:S * half + S]))
        elif kind == "plegate":
            put(n, _tile(a["ple_w_gate"][at[0]][:, P * at[1]:P * at[1] + P]))
        elif kind == "pleproj":
            put(n, _tile(a["ple_w_proj"][at[0]][:, S * at[1]:S * at[1] + S]))
        elif kind == "w1":
            w = a["cmp_w1_2"][at[0]].reshape(2, CMP_LEN, HD, P)[:, 8 * at[1]:8 * at[1] + 8]
            put(n, w.transpose(0, 2, 1, 3).reshape(P, BLK))
        elif kind == "branch":
            w = a["w_branch_2"][at[0]][:, :, P * at[1]:P * at[1] + P]
            put(n, _tile(w.reshape(N_BRANCH * BW, P)))
        elif kind == "out2":
            put(n, _tile(a["w_out_2"][at[0]][:, P * at[1]:P * at[1] + P]))
        else:
            nq, kv, ng, pool, conv, fox, ff, gate, merge = np.split(a["w_in_2"][at[0]], split2[:-1], axis=1)
            if kind == "small":
                w = np.zeros((D, P), np.float32)
                for row in range(4):
                    w[:, row::32] = ff
                w[:, 8:20] = ng
            elif kind == "kcvc":
                w = kv[:, 0:P]
            elif kind == "vsvw":
                w = np.concatenate([kv[:, 192:256], kv[:, 320:384]], 1)
            elif kind == "kskw":
                w = np.concatenate([kv[:, 128:192], kv[:, 256:320]], 1)
            elif kind == "nq":
                w = nq[:, P * at[1]:P * at[1] + P]
            elif kind == "fq":
                w = fox[:, P * at[1]:P * at[1] + P]
            elif kind == "fk":
                w = fox[:, 256 + P * at[1]:256 + P * at[1] + P]
            elif kind == "fv":
                w = fox[S * at[1]:S * at[1] + S, 512:768]
            elif kind == "pool":
                w = pool[:, P * at[1]:P * at[1] + P]
            elif kind == "conv":
                w = conv[:, P * at[1]:P * at[1] + P]
            elif kind == "sgate":
                w = gate[:, P * at[1]:P * at[1] + P]
            elif kind == "merge":
                lo = D * at[2] + P * at[1]
                w = merge[:, lo:lo + P]
            put(n, _tile(w))
    return made


def column_pack(a):
    made = np.zeros((P, NCOLS), np.float32)

    def put(name, v):
        made[:, COLS[name]:COLS[name] + v.shape[1]] = v

    put("q_norm", _column(a["ab_q_norm"][0]))
    put("kv_norm", _column(a["ab_kv_norm"][0]))
    put("subln", _column(a["c_subln"][0]))
    for name in ("ln_mix_g", "ln_mix_b", "ln_ffn_g", "ln_ffn_b"):
        put(name, _column(a[name].reshape(-1)))
    put("conv_w", _column(a["ffn_conv_w"].reshape(-1)))
    put("conv_b", _column(a["ffn_conv_b"].reshape(-1)))
    put("norm2_g", _column(a["norm_g_2"].reshape(-1)))
    bias = np.zeros((P, DEPTH), np.float32)
    for row in range(4):
        bias[row::32] = a["fox_f_bias_2"].T
    put("fox_bias", bias)
    put("cmp_b1", _column(a["cmp_b1_2"].reshape(-1)))
    put("cmp_b2k", np.concatenate([a["cmp_b2_2"][:, 0].T] * 2, 0))
    put("pool_scale", _column(a["pool_scale_2"].reshape(-1)))
    put("conv2_w", _column(a["conv_w_2"].reshape(-1)))
    put("final_g", _column(a["final_norm_g_2"]))
    for name, rot, width in (("inv_a", HD // 4, HD), ("inv_b", B_ROPE, B_ROPE)):
        inv = (np.float32(1.0) / np.float32(ROPE_THETA) ** (np.arange(0, rot, 2, dtype=np.float32) / np.float32(rot)))
        col = np.zeros(P, np.float32)
        for lo in range(0, P, width):
            col[lo:lo + rot] = np.concatenate([inv, inv])
        put(name, col[:, None])
    put("eps_ln", np.full((P, 1), LN_EPS, np.float32))
    put("eps_rms", np.full((P, 1), RMS_EPS, np.float32))
    for h in range(4):
        for row, of_q, of_k in ((0, (1, 0, 0), (0, 0, 1)), (1, (0, 1, 0), (0, 0, 1)), (2, (0, 0, 1), (-1, 0, 0)),
                                (3, (0, 0, 1), (0, -1, 0))):
            made[32 * h + row, COLS["fox_q"]:COLS["fox_q"] + 3] = of_q
            made[32 * h + row, COLS["fox_k"]:COLS["fox_k"] + 3] = of_k
    return made


def table_pack():
    made = np.zeros((P, NTABS), np.float32)

    def put(name, v):
        made[:v.shape[0], TABS[name]:TABS[name] + v.shape[1]] = v

    def swap(lo, half, m):
        for i in range(half):
            m[lo + half + i, lo + i] = -1.0
            m[lo + i, lo + half + i] = 1.0

    put("ident", np.eye(P, dtype=np.float32))
    put("ones", np.ones((P, P), np.float32))
    perm = np.zeros((P, P), np.float32)
    swap(0, 8, perm)
    swap(HD, 8, perm)
    put("perm_a", perm)
    perm = np.zeros((P, P), np.float32)
    for lo in range(0, P, B_ROPE):
        swap(lo, B_ROPE // 2, perm)
    put("perm_b", perm)
    i, j = np.arange(S)[:, None], np.arange(S)[None, :]
    count = np.zeros((S, S))
    for window, dilation in ((128, 1), (512, 4), (2048, 16)):
        side = window // (2 * dilation)
        count += ((i - j) % dilation == 0) & (np.abs(i - j) <= side * dilation)
    put("count", count.astype(np.float32).reshape(ST, P, S).transpose(1, 0, 2).reshape(P, -1))
    half = HD // 8
    inv = np.float32(ROPE_THETA) ** (-np.arange(half, dtype=np.float32) / np.float32(half))
    full = np.zeros(P, np.float32)
    for lo in (0, HD):
        full[lo:lo + 2 * half] = np.concatenate([inv, inv])
    for tag, pos in (("", np.arange(S)), ("c", np.arange(CMP_N) * CMP_STRIDE + CMP_LEN - 1)):
        ang = (pos.astype(np.float32)[None, :] * full[:, None]).astype(np.float64)
        put("cos2" + tag, np.cos(ang).astype(np.float32))
        put("sin2" + tag, np.sin(ang).astype(np.float32))
    inv_count = np.zeros((P, 2, S), np.float32)
    for g, w in enumerate((2, 4, 8, 16)):
        inv_count[64 * (g % 2):64 * (g % 2) + 64, g // 2] = 1.0 / np.minimum(np.arange(1, S + 1), w)
    put("inv_count", inv_count.reshape(P, -1))
    n = np.arange(CMP_N)
    end = n * CMP_STRIDE + CMP_LEN - 1
    seen = (end[None, :] <= np.arange(S)[:, None]) & (n < CMP_N - 1)[None, :]
    put("cmp_mask", np.tile(seen.T, (4, 1)).astype(np.float32))
    bias = np.where(seen, 0.0, MASK).astype(np.float32).reshape(ST, P, 1, CMP_N)
    put("cmp_bias", np.broadcast_to(bias, (ST, P, 4, CMP_N)).transpose(1, 0, 2, 3).reshape(P, -1))
    put("tri", np.where(np.arange(P)[None, :] <= np.arange(P)[:, None], 0.0, MASK).astype(np.float32))
    sel = np.zeros((P, 3, 2, P), np.float32)
    for b in range(3):
        for h in range(4):
            sel[8 + 4 * b + h, b, h // 2, 64 * (h % 2):64 * (h % 2) + 64] = 1.0
    put("sel", sel.reshape(P, -1))
    bd = np.zeros((P, 2, P), np.float32)
    for h in range(4):
        bd[32 * h:32 * h + 32, h // 2, 64 * (h % 2):64 * (h % 2) + 64] = 1.0
    put("ones_bd", bd.reshape(P, -1))
    return made


def small_weights(a):
    made = np.zeros((P, DEPTH, 320), np.float32)
    for l in range(DEPTH):
        made[:, l, 0:64] = made[:, l, 64:128] = a["cmp_w2_2"][l, 0]
        made[:, l, 128:192] = a["cmp_w2_2"][l, 1]
        for g in range(4):
            made[64 * (g % 2):64 * (g % 2) + 64, l, 192 + 64 * (g // 2):256 + 64 * (g // 2)] = a["pool_w_2"][l, g]
    return made.reshape(P, -1)


def host_layout(a):
    cmp_pos = a["cmp_pos_2"].transpose(1, 3, 0, 2).reshape(P, DEPTH * CMP_LEN)
    b2v = np.broadcast_to(a["cmp_b2_2"][:, 1].reshape(1, -1), (P, DEPTH * HD))
    c = np.ascontiguousarray
    return {
        "weights": weight_stream(a),
        "x_t": c(_tile(c(a["x"][0].T))),
        "p_t": c(np.concatenate([_tile(c(a["p"][l, 0].T)) for l in range(DEPTH)], 1)),
        "positions": c(np.broadcast_to(a["positions"], (P, S))),
        "columns": column_pack(a),
        "tables": table_pack(),
        "small_w": small_weights(a),
        "cmp_pos": c(cmp_pos),
        "b2v": c(b2v),
        "lam": c(np.broadcast_to(a["c_lambda"].reshape(1, -1), (P, 4 * HD))),
    }


def attention_units():
    units = [("A", h) for h in range(A_HEADS)] + [("B", h) for h in range(B_HEADS)]
    units += [("C", h) for h in range(C_HEADS)]
    for layer in range(DEPTH):
        units += [("slc", layer, h) for h in range(4)] + [("win", layer, h) for h in range(4)]
        units += [("fox", layer, h) for h in range(4)]
    return units


UNITS = attention_units()
SCORES = [(u, q, c) for u in UNITS for q in range(ST) for c in range(2 if u[0] == "C" else 1)]
SCORE_AT = {key: n for n, key in enumerate(SCORES)}
TURNS = [(u, q) for u in UNITS for q in range(ST)]
TURN_AT = {key: n for n, key in enumerate(TURNS)}
UNIT_AT = {u: n for n, u in enumerate(UNITS)}


def rope_jobs():
    jobs = [("qkA", t) for t in range(8)] + [("kpe",)] + [("qB", r) for r in range(2)]
    jobs += [("qkC", t) for t in range(16)]
    for layer in range(DEPTH):
        jobs += [(kind, layer) for kind in ("ks", "kw", "nq0", "nq1", "kc")]
    return jobs


ROPES = rope_jobs()
ROPES_1 = len(ROPES) - 5 * DEPTH
ROPE_AT = {key: n for n, key in enumerate(ROPES)}

N_INPUTS, N_LATER = 5, 4
N_CLEAR = 12
SETUP = {"rest": 8, "lam_sums": 10, "all": 13}
_c2 = round((2 * math.pi - 6.28125) * 2 ** 21) / 2 ** 21
TWO_PI = (6.28125, _c2, 2 * math.pi - 6.28125 - _c2)


EARLY, EARLY_DOWN = 6, 4
AHEAD = 3
FINISH_LAG = 8
GATE_ORDER = (2, 3, 4, 5, 0, 1, 6, 7)


def build(nc, dram, out):
    ctx = ExitStack()
    with ctx:
        def sb(name, shape, dt=F32):
            return ctx.enter_context(nc.sbuf_tensor(name, shape, dt))

        def sem(name):
            return ctx.enter_context(nc.semaphore(name))

        REGION = 134

        ring = sb("ring", [P, RING, BLK])
        w_parts = [sb("w_hi", [P, RING, BLK], F32R), sb("w_lo", [P, RING, BLK], F32R)]
        x = sb("x", [P, KD, S])
        region_at = nc.sbuf_base
        region = sb("region", [P, REGION * KB])
        cols = sb("cols", [P, NCOLS])
        tabs = sb("tabs", [P, TABS["count"]])
        rope_a = sb("rope_a", [P, 2, S])
        small_w = sb("small_w", [P, DEPTH * 320])
        cmp_pos = sb("cmp_pos", [P, DEPTH * CMP_LEN])
        b2v = sb("b2v", [P, DEPTH * HD])
        prob_at = nc.sbuf_base
        prob = sb("prob", [P, 4, S])
        rope_tmp = sb("rope_tmp", [P, 2, S])
        std = sb("std", [P, 2, S])
        rstd = sb("rstd", [P, 2, S])
        early_sum = rope_tmp[:, 0, :]
        unit = sb("unit", [P, 1])
        negmax = sb("negmax", [P, 8])
        rowsum = sb("rowsum", [P, 8])
        rownorm = sb("rownorm", [P, 8])
        perm_r = sb("perm_r", [P, 2, P], F32R)
        inverse_tmp = sb("inverse_tmp", [P, S // 32])
        cmp_negmax = sb("cmp_negmax", [P, 16])
        neg_lam = sb("neg_lam", [P, 8])
        ident_bf = sb("ident_bf", [P, P], BF16)
        tri_bf = sb("tri_bf", [P, P], BF16)
        cmp_bias_bf = sb("cmp_bias_bf", [P, S], BF16)
        psum = [ctx.enter_context(nc.psum_tensor(f"bank{i}", [P, S], F32)) for i in range(8)]

        def place(kb, *shape):
            at, n = int(kb * KB), int(np.prod(shape))
            assert at + n <= REGION * KB
            v = region[:, at:at + n]
            if len(shape) == 2:
                return v.rearrange("p (a b) -> p a b", a=shape[0])
            if len(shape) == 3:
                return v.rearrange("p (a b c) -> p a b c", a=shape[0], b=shape[1])
            if len(shape) == 4:
                return v.rearrange("p (a b c d) -> p a b c d", a=shape[0], b=shape[1], c=shape[2])
            return v

        def parts(name, kb, *shape, base=region_at):
            size = 4 * int(np.prod(shape))
            return [nc.alloc_sbuf_tensor_at(f"{name}_{part}", [P, *shape], F32R, offset=base + int(1024 * kb) + i * size)
                    for i, part in enumerate(("hi", "lo"))]

        def parts_at(name, kbs, *shape):
            return [nc.alloc_sbuf_tensor_at(f"{name}_{part}", [P, *shape], F32R, offset=region_at + 1024 * kb)
                    for kb, part in zip(kbs, ("hi", "lo"))]

        def col(name, i=0, rows=slice(0, P)):
            return cols[rows, COLS[name] + i:COLS[name] + i + 1]

        LATE_KB = REGION - (NTABS - TABS["cos2"]) / KB
        late = place(LATE_KB, NTABS - TABS["cos2"])

        def tab(name, width):
            if TABS[name] >= TABS["cos2"]:
                return late[:, TABS[name] - TABS["cos2"]:TABS[name] - TABS["cos2"] + width]
            return tabs[:, TABS[name]:TABS[name] + width]

        ident, ones = tab("ident", P), tab("ones", P)
        perm_a, perm_b = tab("perm_a", P), tab("perm_b", P)
        sel = tab("sel", 6 * P).rearrange("p (b j m) -> p b j m", b=3, j=2)
        ones_bd = tab("ones_bd", 2 * P).rearrange("p (j m) -> p j m", j=2)
        inv_count = tab("inv_count", 2 * S).rearrange("p (t s) -> p t s", t=2)

        moving = parts("moving", 0, KD, S)
        z = place(32, KD, S)
        pt = place(32, 2, ST, S)
        mix = place(48, KD, S)
        pos_raw, pos_f = mix[:, 0, :].bitcast(I32), mix[:, 1, :]
        lam_in = mix[:, 2, 0:4 * HD]
        masks_in = place(48 + 6, S + P)
        angle, turns, rest = z[:, 0:2, :], z[:, 2:4, :], z[:, 4:6, :]
        kpe = place(132, S)
        lat_square = z[:, 1:6, :]
        lat = mix[:, 3:8, :]
        qk_a = place(64, 8, S)
        q_b = place(64, 8, S)
        v_ab = place(80, ST, 4, 3 * HD)
        k_b = place(92, 8, S)
        q_rope = place(124, 2, S)
        count = place(108, ST, S)
        mask_a = place(120, ST * S // 2).bitcast(BF16).rearrange("p (q k) -> p q k", q=ST)
        cos_a, sin_a = rope_a[:, 0, :], rope_a[:, 1, :]
        cos_b, sin_b = place(116, S), place(118, S)
        qk_c = place(64, 16, S)
        v_c = place(96, ST, KD * P)
        square = place(64, KD, S)
        hid_kb = 2 * KF
        hid = parts("hid", 32, KF, S)
        conv_t = place(32 + 2 * hid_kb, 2, S)
        gelu_t = place(36 + 2 * hid_kb, 2, S)
        z_ffn = place(16, KD, S)
        p_in_t = place(40 + 2 * hid_kb, 2, S)
        p_parts = parts("p", 0, 2, S, base=prob_at)
        rope_parts = parts("rope", 0, 2, S, base=prob_at)
        sig_p = place(96, KD, S)
        kcvc = prob[:, 0, :]
        blocks_x = prob[:, 1:3, :].rearrange("p t (l n) -> p (t l) n", n=CMP_N)
        blocks = nc.alloc_sbuf_tensor_at("blocks", [P, CMP_LEN, 2, 2, CMP_N], F32R, offset=region_at + 32 * 1024)
        hid_sum = place(116.5, 2, 2 * CMP_N)
        pool_u, pool_a, pool_b = (place(32 + i * 2 * (PAD + S) / KB, 2, PAD + S) for i in range(3))
        nq = place(64, 2, S)
        ksw = place(68, 2, S)
        fqk = place(72, 4, S)
        v_s = place(80, ST, 3 * HD)
        v_w = place(83, ST, 3 * HD)
        v_f = place(86, ST, 2, 3 * HD)
        decay_q, decay_k = parts("decay", 92, S)
        gates = place(96, 3, 2, S)
        gate_sig = place(108, S)
        vc_bd = place(110, 2, P)
        hid_k = place(111, CMP_N)
        hid_v = place(111.125, 4, CMP_N)
        kc = place(111.625, CMP_N)
        conv_u = place(112, 2, 2 + S)
        conv_x, conv_b = prob[:, 0:2, :], rstd
        sg = place(64, KD, S)
        branch = parts("branch", 80, KD, S)
        sig_m = place(32, 2, N_BRANCH, S)
        acc = parts_at("acc", (48, 64), KD, S)

        full = [sem(f"slot{i}_full") for i in range(RING)]
        split_hi, split_ready = sem("split_hi"), sem("split_ready")
        hi_ready, parts_ready = sem("hi_ready"), sem("parts_ready")
        x_in = [sem(f"x_in{i}") for i in range(KD // 2)]
        hid_hi, hid_parts = sem("hid_hi"), sem("hid_parts")
        later_in, late_in, unit_set = sem("later_in"), sem("late_in"), sem("unit_set")
        block_done = sem("block_done")
        inputs_in = sem("inputs_in")
        setup_dve, setup_act = sem("setup_dve"), sem("setup_act")
        link_dve, link_act = sem("link_dve"), sem("link_act")
        v_stored = sem("v_stored")
        rope_raw, rope_split, rope_perm, roped = sem("rope_raw"), sem("rope_split"), sem("rope_perm"), sem("roped")
        lat_raw, qb_stored, kb_stored = sem("lat_raw"), sem("qb_stored"), sem("kb_stored")
        squared, summed, std_ready, normed = sem("squared"), sem("summed"), sem("std_ready"), sem("normed")
        scored, maxed, exped, blended = sem("scored"), sem("maxed"), sem("exped"), sem("blended")
        turned, pt_stored, weighed, attended = sem("turned"), sem("pt_stored"), sem("weighed"), sem("attended")
        z_ready, mean_ready, centered = sem("z_ready"), sem("mean_ready"), sem("centered")
        z_summed, squares_summed = sem("z_summed"), sem("squares_summed")
        conv_mid, conv_done, gelu_done, hid_ready = (sem("conv_mid"), sem("conv_done"), sem("gelu_done"),
                                                     sem("hid_ready"))
        conv_mid2 = sem("conv_mid2")
        p_loaded, ple_sig, ple_term, x_ple = sem("p_loaded"), sem("ple_sig"), sem("ple_term"), sem("x_ple")
        kpe_spread = sem("kpe_spread")
        constants_bf = sem("constants_bf")
        stored, prepared, spread = sem("stored"), sem("prepared"), sem("spread")
        compress_step, cleared, gated = sem("compress_step"), sem("cleared"), sem("gated")
        sig_ready, merged, merge_link, x_next = sem("sig_ready"), sem("merged"), sem("merge_link"), sem("x_next")
        out_stored = sem("out_stored")

        T = {}
        T["v"] = Tally([("A", i) for i in range(4)] + [("B", i) for i in range(4)] + [("C", i) for i in range(8)])
        T["squared"], T["summed"], T["std"], T["normed"] = Tally(), Tally(), Tally(), Tally()
        for n in range(5):
            T["squared"].add(("lat", n))
        for j in range(2):
            T["summed"].add(("lat", j)), T["std"].add(("lat", j))
        for n in range(5):
            T["normed"].add(("lat", n))

        def plan_ln(i):
            for n in range(KD):
                T["squared"].add(("ln", i, n)), T["normed"].add(("ln", i, n))
            T["summed"].add(("ln", i)), T["std"].add(("ln", i))

        plan_ln(0), plan_ln(1)
        for n in range(C_HEADS):
            for t in ("squared", "summed", "std", "normed"):
                T[t].add(("C", n))
        plan_ln(2), plan_ln(3)
        for i in range(DEPTH + 1):
            for n in range(KD):
                T["squared"].add(("rms", i, n)), T["normed"].add(("rms", i, n))
            T["summed"].add(("rms", i)), T["std"].add(("rms", i))

        T["parts"] = Tally([("x", 0, n) for n in range(KD)] + [("lat", n) for n in range(5)])
        for layer in range(DEPTH):
            keys = [("mix", layer, n) for n in range(KD)] + [("ln", 2 * layer, n) for n in range(KD)]
            keys += [("p", layer)] + [("ln", 2 * layer + 1, n) for n in range(KD)]
            keys += [("x", 1, n) for n in range(KD if layer == 0 else 0)]
            for key in keys:
                T["parts"].add(key)
        for layer in range(DEPTH):
            for key in [("h2", layer, n) for n in range(KD)] + [("blocks", layer)]:
                T["parts"].add(key)
            for t in GATE_ORDER:
                T["parts"].add(("branch", layer, t))

        T["stored"], T["prepared"] = Tally(), Tally()
        for layer in range(DEPTH):
            for key in ["gsig", "fl", "ln", "kcvc", "vs", "vw", *[f"g{n}" for n in range(6)], "fq0", "fq1", "hidk", "hidv", "fk0", "fk1", "cmp_exp", "fv0", "fv1",
                        "fv2", "fv3", "pool0", "pool1", "cx0", "cx1", "cb0", "cb1",
                        "pm0", "pm1", "pm2", "pm3", *[f"sg{t}" for t in range(8)]]:
                T["stored"].add((key, layer))
            for key in ["blocks", "hid", "vc", "decay", "cmp_shift", "cmp_pt", "pooled", "cmp_out0", "cmp_out",
                        "cu0", "cu1", "convy0", "convy1"]:
                T["prepared"].add((key, layer))

        block = ctx.enter_context(nc.Block())

        def done(key):
            return AT[key] + 1

        def both(parts, at):
            return parts[0][at], parts[1][at]

        @block.sync
        def _(sp):
            for s in range(RING):
                sp.dma_start(ring[:, s, :], dram["weights"][s]).then_inc(full[s], 16)
            lo = TABS["count"]
            sp.dma_start(pos_raw, dram["positions"]).then_inc(inputs_in, 16)
            sp.dma_start(cols[:, :], dram["columns"]).then_inc(inputs_in, 16)
            sp.dma_start(lam_in, dram["lam"]).then_inc(inputs_in, 16)
            sp.dma_start(tabs[:, :], dram["tables"][:, 0:lo]).then_inc(inputs_in, 16)
            sp.dma_start(masks_in, dram["tables"][:, lo + ST * S:lo + ST * S + S + P]).then_inc(inputs_in, 16)
            with sp.Fori(1, len(BLOCKS) // RING) as it:
                for s in range(RING):
                    sp.wait_ge(split_ready, RING * it + (s - RING + 1))
                    sp.dma_start(ring[:, s, :], dram["weights"][RING * it + s]).then_inc(full[s], 16)
            for n in range(len(BLOCKS) // RING * RING, len(BLOCKS)):
                sp.wait_ge(split_ready, n - RING + 1)
                sp.dma_start(ring[:, n % RING, :], dram["weights"][n]).then_inc(full[n % RING], 16)

            for n in range(KD):
                sp.wait_ge(normed, T["normed"][("rms", DEPTH, n)])
                sp.dma_start(out[:, n, :], z[:, n, :]).then_inc(out_stored, 16)
            sp.wait_ge(out_stored, 16 * KD)

        @block.tensor
        def _(pe):
            def arrived(key):
                n = AT[key]
                pe.wait_ge(split_ready, n + 1)
                return both(w_parts, np.s_[:, n % RING, :])

            def passes(bank, lhs, rhs, start, stop):
                pe.matmul(bank, lhs[0], rhs[0], start=start, stop=False, skip_group_check=True)
                pe.matmul(bank, lhs[0], rhs[1], start=False, stop=False, skip_group_check=True)
                return pe.matmul(bank, lhs[1], rhs[0], start=False, stop=stop, skip_group_check=True)

            def cols_of(pair, lo, n):
                return pair[0][:, lo:lo + n], pair[1][:, lo:lo + n]

            def project(key, bank, rhs, kt=KD, ready=None):
                w = arrived(key)
                for k in range(kt):
                    if ready:
                        pe.wait_ge(parts_ready, T["parts"][ready + (k,)])
                    mm = passes(bank, cols_of(w, k * P, P), rhs(k), k == 0, k == kt - 1)
                mm.then_inc(block_done, 1)

            def moved(k):
                return both(moving, np.s_[:, k, :])

            def turn_pairs(job, matrix, rows, raw, n=S):
                g = ROPE_AT[job]
                pe.wait_ge(rope_raw, g + 1)
                if g >= 2:
                    pe.wait_ge(roped, g - 1)
                bank = psum[4 + g % 2][0:rows, 0:n]
                if g >= ROPES_1:
                    pe.matmul(bank, matrix[0:rows, 0:rows], raw, start=True, stop=True).then_inc(rope_perm, 1)
                    return
                pe.wait_ge(rope_split, g + 1)
                lhs = perm_r[0:rows, 0 if matrix is perm_a else 1, 0:rows]
                pe.matmul(bank, lhs, rope_parts[0][0:rows, g % 2, :], start=True, stop=False)
                pe.matmul(bank, lhs, rope_parts[1][0:rows, g % 2, :], start=False, stop=True).then_inc(rope_perm, 1)

            def tokens_values(keys, lhs, banks, width, per, ready=None):
                for i, key in enumerate(keys):
                    w = arrived(key)
                    if ready:
                        pe.wait_ge(parts_ready, T["parts"][ready + (i * per + per - 1,)])
                    for st in range(ST):
                        for j in range(per):
                            k = i * per + j
                            mm = passes(banks[st], cols_of(lhs(k), st * P, P), cols_of(w, j * width, width), k == 0,
                                        k == len(keys) * per - 1)
                    mm.then_inc(block_done, 1)

            def attention(units, q, k, v, extra, ahead, blend=False, causal=False):
                turns = [(u, i) for u in units for i in range(ST)]
                comps = 2 if blend else 1

                def scores(u, i):
                    for c in range(comps):
                        s = SCORE_AT[(u, i, c)]
                        if s >= 4:
                            pe.wait_ge(exped, s - 3)
                        w = (i + 1) * P if causal else S
                        bank = psum[s % 4]
                        more = extra(bank, u, i)
                        mm = pe.matmul(bank[:, 0:w], q(u, c)[:, i * P:i * P + P], k(u, c)[:, 0:w], start=True,
                                       stop=True)
                        for o, lhs, rhs in more:
                            mm = pe.matmul(o, lhs, rhs, start=False, stop=True, skip_group_check=True)
                        mm.then_inc(scored, 1)

                def values(u, t):
                    n = UNIT_AT[u]
                    if t == 0:
                        pe.wait_ge(pt_stored, TURN_AT[(u, ST - 1)] + 1)
                        if n >= 2:
                            pe.wait_ge(attended, n - 1)
                    lo = t * P if causal else 0
                    mm = pe.matmul(psum[6 + n % 2][:, lo:S], v(u, t), pt[:, n % 2, t, lo:S], start=(t == 0),
                                   stop=(t == ST - 1), skip_group_check=True)
                    if t == ST - 1:
                        mm.then_inc(weighed, 1)

                for u, i in turns[:ahead]:
                    scores(u, i)
                for n, (u, i) in enumerate(turns):
                    if n + ahead < len(turns):
                        scores(*turns[n + ahead])
                    t = TURN_AT[(u, i)]
                    s = SCORE_AT[(u, i, 0)]
                    if blend:
                        pe.wait_ge(blended, t - TURN_AT[(("C", 0), 0)] + 1)
                    else:
                        pe.wait_ge(exped, s + 1)
                    if t >= 2:
                        pe.wait_ge(pt_stored, t - 1)
                    for kt in range(i + 1 if causal else ST):
                        mm = pe.transpose(psum[4 + t % 2][:, kt * P:kt * P + P], prob[:, s % 4, kt * P:kt * P + P], ident)
                    mm.then_inc(turned, 1)
                    if n >= ST:
                        values(turns[n - ST][0], i)
                for i in range(ST):
                    values(units[-1], i)

            def add_mean(i, tile, first=False, last=False):
                return pe.matmul(psum[6][:], ones, tile, start=first, stop=last, skip_group_check=True)

            def add_early_mean(i):
                pe.wait_ge(z_summed, i + 1)
                add_mean(i, early_sum, first=True)

            def residual_norm(i):
                if i % 2 == 0:
                    add_early_mean(i)
                for n in range(EARLY_DOWN if i % 2 else EARLY, KD):
                    pe.wait_ge(z_ready, KD * i + n + 1)
                    mm = add_mean(i, (z_ffn if i % 2 else z)[:, n, :], last=(n == KD - 1))
                mm.then_inc(mean_ready, 1)
                sum_squares(("ln", i), psum[7], KD, lambda n: square[:, n, :])

            def sum_squares(key, bank, count, tile, names=None):
                for n in range(count):
                    pe.wait_ge(squared, T["squared"][names(n) if names else key + (n,)])
                    mm = pe.matmul(bank[:], ones, tile(n), start=(n == 0), stop=(n == count - 1))
                mm.then_inc(summed, 1)

            def mixer_out(i):
                layer = i // 2
                for n in range(KD):
                    if n >= 4:
                        pe.wait_ge(z_ready, KD * i + n - 3)
                    project(("mixout", layer, n), psum[n % 4][:], moved, ready=("mix", layer) if n == 0 else None)

            def feed_forward(i):
                layer = i // 2
                n0 = AT[("gate", layer, 0)]
                with pe.Fori(0, KF // 2) as it:
                    for par in range(2):
                        pe.wait_ge(hid_ready, 2 * it + (par + 1 + KF * layer))
                        for half in range(2):
                            b = n0 + 2 * par + half
                            pe.wait_ge(split_ready, 4 * it + (b + 1))
                            w = both(w_parts, np.s_[:, b % RING, :])
                            for k in range(KD):
                                if par == half == 0:
                                    pe.wait_ge(parts_ready, T["parts"][("ln", i - 1, k)])
                                mm = passes(psum[2 * half + par][:], cols_of(w, k * P, P), moved(k), k == 0, k == KD - 1)
                            mm.then_inc(block_done, 1)
                for h in range(2):
                    banks = psum[4:8] if h == 0 else psum[0:4]
                    d0 = AT[("down", layer, h, 0)]

                    def down(b, it, first=False, last=False):
                        pe.wait_ge(split_ready, 4 * it + (d0 + b + 1))
                        w = both(w_parts, np.s_[:, (d0 + b) % RING, :])
                        if h == 0:
                            pe.wait_ge(hid_parts, 8 * it + (2 * b + 2 + KF * layer))
                        for j in range(2):
                            tile = both(hid, np.s_[:, 8 * it + (2 * b + j), :])
                            for n in range(4):
                                mm = passes(banks[n][:], cols_of(w, j * S + n * P, P), tile, first and j == 0,
                                            last and j == 1)
                        mm.then_inc(block_done, 1)

                    for b in range(3):
                        down(b, 0, first=(b == 0))
                    if h == 1:
                        add_early_mean(i)
                    with pe.Fori(0, 2) as it:
                        for b in range(3, 7):
                            down(b, it)

            def per_layer(layer):
                for half in range(2):
                    w = arrived(("pleproj", layer, half))
                    if half == 0:
                        pe.wait_ge(parts_ready, T["parts"][("p", layer)])
                        pe.wait_ge(std_ready, T["std"][("ln", 2 * layer + 1)])
                    else:
                        pe.wait_ge(ple_term, KD * layer + 4)
                    for n in range(4):
                        for k in range(2):
                            mm = passes(psum[4 + n][:], cols_of(w, k * S + n * P, P), both(p_parts, np.s_[:, k, :]), k == 0,
                                        k == 1)
                    mm.then_inc(block_done, 1)
                    for n in range(4 * half, 4 * half + 4):
                        if n >= 4:
                            pe.wait_ge(ple_sig, KD * layer + n - 3)
                        project(("plegate", layer, n), psum[n % 4][:], moved,
                                ready=("ln", 2 * layer + 1) if n == 0 else None)

            def mixer_a():
                tokens_values([("vA", i) for i in range(4)], moved, [psum[i][:] for i in range(4)], S, 2, ready=("x", 0))
                pe.wait_ge(inputs_in, 16 * N_INPUTS)
                for t in range(8):
                    if t < 4:
                        pe.wait_ge(v_stored, T["v"][("A", t)])
                    else:
                        pe.wait_ge(rope_raw, ROPE_AT[("qkA", t - 4)] + 1)
                    project(("qkA", t), psum[t % 4][:], moved)
                    if t:
                        turn_pairs(("qkA", t - 1), perm_a, P, qk_a[:, t - 1, :])
                for n in range(5):
                    if n < 4:
                        pe.wait_ge(rope_raw, ROPE_AT[("qkA", 4 + n)] + 1)
                    else:
                        pe.wait_ge(lat_raw, n - 3)
                    project(("lat", n), psum[n % 4][:], moved)
                    if n == 0:
                        turn_pairs(("qkA", 7), perm_a, P, qk_a[:, 7, :])
                w = arrived(("kpe", 0))
                pe.wait_ge(lat_raw, 2)
                for k in range(KD):
                    mm = passes(psum[1][0:B_QK, :], cols_of(w, k * B_QK, B_QK), moved(k), k == 0, k == KD - 1)
                mm.then_inc(block_done, 1)
                sum_squares(None, psum[6], 3, lambda n: lat_square[:, n, :], lambda n: ("lat", n))
                sum_squares(None, psum[7], 2, lambda n: lat_square[:, 3 + n, :], lambda n: ("lat", 3 + n))
                turn_pairs(("kpe",), perm_b, B_QK, kpe[0:B_QK, :])

            def mixer_b():
                pe.wait_ge(parts_ready, T["parts"][("lat", 4)])
                for i in range(3):
                    w = arrived(("qup", i))
                    for c in range(2):
                        n = 2 * i + c
                        if n >= 4:
                            pe.wait_ge(attended, UNIT_AT[("A", n + 2)] + 1)
                        for k in range(3):
                            mm = passes(psum[n if n < 4 else n + 2][:], cols_of(w, (3 * c + k) * P, P), moved(k), k == 0, k == 2)
                    mm.then_inc(block_done, 1)
                    if i:
                        turn_pairs(("qB", i - 1), perm_b, P, q_rope[:, i - 1, :])
                w = arrived(("kvk", 0))
                for j in range(4):
                    if j < 2:
                        pe.wait_ge(rope_raw, ROPE_AT[("qB", j)] + 1)
                    else:
                        pe.wait_ge(qb_stored, 2 * j - 2)
                    for k in range(2):
                        lo = j * 2 * P + k * P
                        mm = passes(psum[j][:], cols_of(w, lo, P), moved(3 + k), k == 0, k == 1)
                mm.then_inc(block_done, 1)
                pe.wait_ge(roped, ROPE_AT[("qB", 1)] + 1)
                pe.wait_ge(qb_stored, 8)
                tokens_values([("kvv", 0)], lambda k: moved(3 + k), [psum[4 + i][:] for i in range(4)], S, 2)

            def heads_ab(kind):
                if kind == "A":
                    pe.wait_ge(v_stored, T["v"][("A", 3)])
                    pe.wait_ge(lat_raw, 5)
                    pe.wait_ge(roped, ROPE_AT[("kpe",)] + 1)
                    pe.wait_ge(cleared, 1)
                    pe.wait_ge(constants_bf, 4)
                else:
                    pe.wait_ge(kb_stored, 8)
                    pe.wait_ge(kpe_spread, B_HEADS // 2)
                    pe.wait_ge(v_stored, T["v"][("B", 3)])
                half = lambda h: slice(HD * (h % 2), HD * (h % 2) + HD)

                def q(u, c):
                    h = u[1]
                    return qk_a[half(h), h // 2, :] if u[0] == "A" else q_b[0:B_QK, h, :]

                def k(u, c):
                    h = u[1]
                    return qk_a[half(h), 4 + h // 2, :] if u[0] == "A" else k_b[0:B_QK, h, :]

                def v(u, t):
                    h = u[1]
                    return v_ab[:, t, h // 2, HD * (h % 2):HD * (h % 2) + P]

                def mask(bank, u, i):
                    return [(bank[:], ident_bf[:], mask_a[:, i, :])] if u[0] == "A" else []

                attention([u for u in UNITS if u[0] == kind], q, k, v, mask, ahead=AHEAD)

            def mixer_c():
                for half in range(2):
                    pe.wait_ge(ple_term, KD)
                    tokens_values([("vC", 4 * half + i) for i in range(4)], moved,
                                  [psum[4 * half + i][:] for i in range(4)], S, 2, ready=("x", 1))
                for t in range(16):
                    if t < 4:
                        pe.wait_ge(v_stored, T["v"][("C", t)])
                    else:
                        pe.wait_ge(rope_raw, ROPE_AT[("qkC", t - 4)] + 1)
                    project(("qkC", t), psum[t % 4][:], moved)
                    if t:
                        if t == 1:
                            pe.wait_ge(v_stored, T["v"][("C", 7)])
                        turn_pairs(("qkC", t - 1), perm_a, P, qk_c[:, t - 1, :])
                turn_pairs(("qkC", 15), perm_a, P, qk_c[:, 15, :])

            def heads_c():
                pe.wait_ge(roped, ROPE_AT[("qkC", 15)] + 1)
                half = lambda c: slice(HD * c, HD * c + HD)
                attention([u for u in UNITS if u[0] == "C"], lambda u, c: qk_c[half(c), u[1], :],
                          lambda u, c: qk_c[half(c), 8 + u[1], :], lambda u, t: v_c[:, t, u[1] * P:u[1] * P + P],
                          lambda bank, u, i: [], ahead=2, blend=True)
                for n in range(C_HEADS):
                    if n >= 2:
                        pe.wait_ge(std_ready, T["std"][("C", n - 2)])
                    sum_squares(None, psum[4 + n % 2], 1, lambda _: square[:, n, :], lambda _: ("C", n))
            def sum_rms(i):
                if i == 0:
                    pe.wait_ge(ple_term, KD * DEPTH)
                else:
                    pe.wait_ge(squares_summed, i)
                    pe.matmul(psum[7][:], ones, early_sum, start=True, stop=False, skip_group_check=True)
                for n in range(EARLY if i else 0, KD):
                    pe.wait_ge(squared, T["squared"][("rms", i, n)])
                    mm = pe.matmul(psum[7][:], ones, z[:, n, :], start=(i == n == 0), stop=(n == KD - 1), skip_group_check=True)
                mm.then_inc(summed, 1)

            def compress(layer, i):
                if i == 0:
                    pe.wait_ge(parts_ready, T["parts"][("blocks", layer)])
                w = arrived(("w1", layer, i))
                for l in range(8):
                    at, last = 8 * i + l, i == 3 and l == 7
                    pe.matmul(psum[3][:, 0:4 * CMP_N], w[0][:, l * P:l * P + P],
                              blocks[:, at].rearrange("p a c n -> p (a c n)"), start=(at == 0), stop=last,
                              skip_group_check=True)
                    mm = pe.matmul(psum[3][:, 0:2 * CMP_N], w[1][:, l * P:l * P + P],
                                   blocks[:, at, 0].rearrange("p c n -> p (c n)"), start=False, stop=last,
                                   skip_group_check=True)
                mm.then_inc(block_done, 1)

            def spread_gate(layer, n):
                pe.wait_ge(stored, T["stored"][(f"g{n - 1}" if n else "gsig", layer)])
                pe.matmul(psum[6][:], sel[:, n // 2, n % 2, :], gate_sig, start=True, stop=True).then_inc(spread, 1)

            def compressed_scores(layer):
                pe.wait_ge(roped, ROPE_AT[("kc", layer)] + 1)
                pe.wait_ge(stored, T["stored"][("g5", layer)])
                for odd in range(2):
                    bank = psum[6 + odd]
                    mask = cmp_bias_bf[:].rearrange("p (i h n) -> p i h n", i=ST, h=4)[:, :, 0:2, :]
                    pe.matmul(bank[:, 0:2 * P], ident_bf[:], mask, start=True, stop=True)
                    rows = slice(HD * odd, HD * odd + HD)
                    for i in range(ST):
                        for j in range(2):
                            lo = (2 * i + j) * CMP_N
                            mm = pe.matmul(bank[:, lo:lo + CMP_N], nq[rows, j, i * P:i * P + P], kc[rows, :],
                                           start=False, stop=True, skip_group_check=True)
                mm.then_inc(compress_step, 1)

            def compressed_transposes(layer):
                pe.wait_ge(stored, T["stored"][("cmp_exp", layer)])
                for i in range(ST):
                    mm = pe.transpose(psum[7][:, i * P:i * P + P], rstd[:, 1, i * P:i * P + P], ident)
                mm.then_inc(compress_step, 1)

            def compressed_values(layer):
                pe.wait_ge(prepared, T["prepared"][("cmp_pt", layer)])
                for j in range(2):
                    pe.matmul(psum[4 + j][:], vc_bd[:, j, :], prob[:, 3, :], start=True, stop=True)
                    mm = pe.matmul(psum[6 + j][:], ones_bd[:, j, :], prob[:, 3, :], start=True, stop=True)
                mm.then_inc(compress_step, 1)

            def project_second(layer):
                stored_at = lambda key: pe.wait_ge(stored, T["stored"][(key, layer)])
                raw_at = lambda key: pe.wait_ge(rope_raw, ROPE_AT[(key, layer)] + 1)
                rhs = moved
                project(("small", layer), psum[0][:], rhs, ready=("h2", layer))
                project(("kcvc", layer), psum[1][:], rhs)
                w = arrived(("vsvw", layer))
                for st in range(ST):
                    for k in range(KD):
                        mm = passes(psum[2][:, st * P:st * P + P], cols_of(moved(k), st * P, P), cols_of(w, k * P, P), k == 0,
                                    k == KD - 1)
                mm.then_inc(block_done, 1)
                pe.wait_ge(late_in, 16)
                spread_gate(layer, 0)
                project(("kskw", layer), psum[3][:], rhs)
                spread_gate(layer, 1)
                stored_at("kcvc")
                project(("nq", layer, 0), psum[1][:], rhs)
                spread_gate(layer, 2)
                turn_pairs(("ks", layer), perm_a, P, ksw[:, 0, :])
                turn_pairs(("kw", layer), perm_a, P, ksw[:, 1, :])
                stored_at("vw")
                compress(layer, 0)
                spread_gate(layer, 3)
                project(("nq", layer, 1), psum[2][:], rhs)
                spread_gate(layer, 4)
                turn_pairs(("nq0", layer), perm_a, P, nq[:, 0, :])
                compress(layer, 1)
                project(("fq", layer, 0), psum[0][:], rhs)
                spread_gate(layer, 5)
                turn_pairs(("nq1", layer), perm_a, P, nq[:, 1, :])
                compress(layer, 2)
                raw_at("nq0")
                project(("fq", layer, 1), psum[1][:], rhs)
                compress(layer, 3)
                raw_at("nq1")
                project(("fk", layer, 0), psum[2][:], rhs)
                stored_at("hidk")
                lo = layer * 320
                pe.matmul(psum[7][:, 0:CMP_N], small_w[:, lo:lo + P], hid_k, start=True,
                          stop=True).then_inc(compress_step, 1)
                stored_at("hidv")
                pe.matmul(psum[3][:, 0:HD], hid_v.rearrange("p a n -> p (a n)"), small_w[:, lo + P:lo + P + HD],
                          start=True, stop=True).then_inc(compress_step, 1)
                turn_pairs(("kc", layer), perm_a, P, kc, CMP_N)
                pe.wait_ge(prepared, T["prepared"][("vc", layer)])
                project(("fk", layer, 1), psum[3][:], rhs)
                compressed_scores(layer)
                stored_at("fk1")
                tokens_values([("fv", layer, i) for i in range(2)], rhs, [psum[i][:, 0:256] for i in range(4)], 256, 4)
                compressed_transposes(layer)
                for n, (key, before) in enumerate([(("pool", layer, 0), "fv0"), (("pool", layer, 1), "fv1"),
                                                   (("conv", layer, 0), "fv2"), (("conv", layer, 1), "fv3"),
                                                   (("conv", layer, 2), "pool0"), (("conv", layer, 3), "pool1"),
                                                   (("conv", layer, 4), "cx0"), (("conv", layer, 5), "cx1")]):
                    if n == 2:
                        compressed_values(layer)
                    stored_at(before)
                    project(key, psum[n % 4][:], rhs)
                pe.wait_ge(prepared, T["prepared"][("pooled", layer)])
                for g in range(4):
                    if g < 2:
                        stored_at(f"cb{g}")
                    else:
                        pe.wait_ge(prepared, T["prepared"][(f"cu{g - 2}", layer)])
                    rows = slice(HD * (g % 2), HD * (g % 2) + HD)
                    at = lo + 192 + HD * (g // 2)
                    pe.matmul(psum[g][rows, :], small_w[rows, at:at + HD], mix[rows, 2 + g // 2, :], start=True,
                              stop=True).then_inc(spread, 1)

            def heads_second(layer):
                half = lambda h: slice(HD * (h % 2), HD * (h % 2) + HD)
                pe.wait_ge(stored, T["stored"][("pm3", layer)])
                pe.wait_ge(prepared, T["prepared"][("cmp_out", layer)])
                pe.wait_ge(cleared, 1 + N_CLEAR * (layer + 1))

                def q(u, c):
                    h = u[2]
                    return nq[half(h), h // 2, :] if u[0] != "fox" else fqk[half(h), h // 2, :]

                def k(u, c):
                    h = u[2]
                    return fqk[half(h), 2 + h // 2, :] if u[0] == "fox" else ksw[half(h), int(u[0] == "win"), :]

                def v(u, t):
                    h = u[2]
                    if u[0] == "fox":
                        return v_f[:, t, h // 2, HD * (h % 2):HD * (h % 2) + P]
                    lo = HD * (1 - h % 2)
                    return (v_s if u[0] == "slc" else v_w)[:, t, lo:lo + P]

                def extra(bank, u, i):
                    more = []
                    if u[0] == "fox":
                        rows = slice(32 * u[2], 32 * u[2] + 4)
                        more.append((bank[:, 0:i * P + P], decay_q[rows, i * P:i * P + P], decay_k[rows, 0:i * P + P]))
                    more.append((bank[:, i * P:i * P + P], ident_bf[:], tri_bf[:]))
                    return more

                attention([u for u in UNITS if len(u) == 3 and u[1] == layer], q, k, v, extra, ahead=AHEAD, causal=True)

            def merge(layer):
                for t in range(KD):
                    if t >= 6:
                        pe.wait_ge(attended, UNIT_AT[("fox", layer, t - 4)] + 1)
                    project(("sgate", layer, t), psum[t][:], moved)
                pe.wait_ge(stored, T["stored"][("sg3", layer)])
                n0 = AT[("merge", layer, 0, 0)]
                per = N_BRANCH + 1
                with pe.Fori(0, KD // 4) as it:
                    for d in range(4):
                        for i in range(N_BRANCH):
                            b = n0 + per * d + i
                            pe.wait_ge(split_ready, 4 * per * it + (b + 1))
                            pe.wait_ge(sig_ready, 16 * it + (4 * d + i + 1 + 32 * layer))
                            w = both(w_parts, np.s_[:, b % RING, :])
                            for k in range(KD):
                                mm = passes(psum[i][:], cols_of(w, k * P, P), moved(k), k == 0, k == KD - 1)
                            mm.then_inc(block_done, 1)
                        b = n0 + per * d + N_BRANCH
                        pe.wait_ge(split_ready, 4 * per * it + (b + 1))
                        pe.wait_ge(merged, 4 * it + (d + 2 + KD * layer))
                        pe.wait_ge(parts_ready, T["parts"][("branch", layer, GATE_ORDER[-1])])
                        w = both(w_parts, np.s_[:, b % RING, :])
                        for i in range(N_BRANCH):
                            for k in range(2):
                                j = 2 * i + k
                                mm = passes(psum[4 + i][:], cols_of(w, j * P, P), both(branch, np.s_[:, j, :]), k == 0, k == 1)
                        mm.then_inc(block_done, 1)
                pe.wait_ge(sig_ready, N_BRANCH + 32 * (layer + 1))
                for n in range(KD):
                    if n >= 4:
                        pe.wait_ge(x_next, KD * layer + n - 3)
                    w = arrived(("out2", layer, n))
                    for k in range(KD):
                        if n == 0:
                            pe.wait_ge(merged, 2 + KD * layer + k + 1)
                        mm = passes(psum[n % 4][:], cols_of(w, k * P, P), both(acc, np.s_[:, k, :]), k == 0, k == KD - 1)
                    mm.then_inc(block_done, 1)

            stages_pe2 = []
            for layer in range(DEPTH):
                stages_pe2 += [lambda l=layer: sum_rms(l), lambda l=layer: project_second(l),
                               lambda: None, lambda l=layer: heads_second(l),
                               lambda l=layer: merge(l)]
            stages_pe2 += [lambda: sum_rms(DEPTH)]

            stages = [
                mixer_a, lambda: (heads_ab("A"), mixer_b()), lambda: heads_ab("B"), lambda: mixer_out(0), lambda: residual_norm(0),
                lambda: feed_forward(1), lambda: residual_norm(1), lambda: per_layer(0),
                mixer_c, heads_c, lambda: mixer_out(2), lambda: residual_norm(2),
                lambda: feed_forward(3), lambda: residual_norm(3), lambda: per_layer(1),
            ]
            stages += stages_pe2
            for stage in stages:
                stage()

        @block.scalar
        def _(act):
            linked = [0]

            def link(ins):
                linked[0] += 1
                ins.then_inc(link_act, 1)
                act.wait_ge(link_act, linked[0])

            def raw(job, dst, src, scale=1.0, bias=None):
                g = ROPE_AT[job]
                if bias is None:
                    ins = act.activation(dst, src, ACT.Copy, scale=scale)
                else:
                    ins = act.activation(dst, src, ACT.Identity, bias=bias, scale=scale)
                if g < ROPES_1:
                    if g >= 2:
                        act.wait_ge(rope_perm, g - 1)
                    rows = dst.shape[0]
                    ins = act.activation(rope_parts[0][0:rows, g % 2, :], src, ACT.Copy, scale=scale)
                ins.then_inc(rope_raw, 1)

            def upper(key, dst, src):
                act.activation(dst, src, ACT.Copy).then_inc(hi_ready, 1)

            def values(keys, blk, dst, src):
                act.wait_ge(block_done, done(blk))
                for i, _ in enumerate(keys):
                    act.activation(dst(i), src(i), ACT.Copy).then_inc(v_stored, 1)

            def pairs(v):
                return v.rearrange("p j (t d) -> p j t d", t=3)[:, :, 0:3:2, :]

            def deviation(key, bank, count, eps, buf):
                act.wait_ge(summed, T["summed"][key])
                act.activation(std[:, buf, :], bank[:], ACT.Sqrt, bias=eps, scale=1.0 / count).then_inc(std_ready, 1)

            def attention(units, blend=False, causal=False, copies=True):
                turns = [(u, i) for u in units for i in range(ST)]
                comps = 2 if blend else 1

                def copy_turned(u, i):
                    t, n = TURN_AT[(u, i)], UNIT_AT[u]
                    act.wait_ge(turned, t + 1)
                    if i == 0 and n >= 2:
                        act.wait_ge(weighed, n - 1)
                    kt = i + 1 if causal else ST
                    act.activation(pt[:, n % 2, 0:kt, i * P:i * P + P],
                                   psum[4 + t % 2][:, 0:kt * P].rearrange("p (k q) -> p k q", k=kt),
                                   ACT.Copy).then_inc(pt_stored, 1)

                for n, (u, i) in enumerate(turns):
                    for c in range(comps):
                        s = SCORE_AT[(u, i, c)]
                        act.wait_ge(maxed, s + 1)
                        t = TURN_AT[(u, i)]
                        back = 2 if blend else 4
                        if t >= back:
                            act.wait_ge(turned, t - back + 1)
                        w = (i + 1) * P if causal else S
                        act.activation(prob[:, s % 4, 0:w], psum[s % 4][:, 0:w], ACT.Exp, bias=negmax[:, s % 8:s % 8 + 1],
                                       accum_out=rowsum[:, s % 8:s % 8 + 1] if blend else None).then_inc(exped, 1)
                    if n and copies:
                        copy_turned(*turns[n - 1])
                if copies:
                    copy_turned(*turns[-1])

            def load_p(layer):
                act.dma_start(p_in_t, dram["p_t"][:, layer * 2 * S:layer * 2 * S + 2 * S].rearrange(
                    "p (t s) -> p t s", t=2)).then_inc(p_loaded, 16)

            def setup():
                for i in range(KD // 2):
                    act.dma_start(x[:, 2 * i:2 * i + 2, :], dram["x_t"][:, 2 * i * S:2 * i * S + 2 * S].rearrange(
                        "p (t s) -> p t s", t=2)).then_inc(x_in[i], 16)
                for n in range(KD):
                    act.wait_ge(x_in[n // 2], 16)
                    upper(("x", 0, n), moving[0][:, n, :], x[:, n, :])
                lo = TABS["count"]
                act.dma_start(count, dram["tables"][:, lo:lo + ST * S].rearrange("p (q k) -> p q k", q=ST)).then_inc(
                    later_in, 16)
                act.dma_start(small_w[:, :], dram["small_w"]).then_inc(later_in, 16)
                act.dma_start(cmp_pos[:, :], dram["cmp_pos"]).then_inc(later_in, 16)
                act.dma_start(b2v[:, :], dram["b2v"]).then_inc(later_in, 16)
                load_p(0)
                act.nop().then_inc(sig_ready, N_BRANCH)
                act.wait_ge(setup_dve, SETUP["rest"])
                act.activation(sin_a, rest[:, 0, :], ACT.Sin)
                act.activation(sin_b, rest[:, 1, :], ACT.Sin)
                act.activation(angle[:, :, :], rest[:, :, :], ACT.Sin, scale=0.5).then_inc(setup_act, 1)
                act.wait_ge(setup_dve, SETUP["lam_sums"])
                act.activation(neg_lam[:, 2:4], neg_lam[:, 0:2], ACT.Exp).then_inc(setup_act, 1)

            def mixer_a():
                act.wait_ge(cleared, 1)
                values(range(4), ("vA", 3), lambda i: pairs(v_ab[:, i]),
                       lambda i: psum[i][:].rearrange("p (j t d) -> p j t d", j=4, t=2))
                for t in range(8):
                    act.wait_ge(block_done, done(("qkA", t)))
                    raw(("qkA", t), qk_a[:, t, :], psum[t % 4][:], HD ** -0.5 if t < 4 else 1.0)
                for n in range(5):
                    act.wait_ge(block_done, done(("lat", n)))
                    act.activation(lat[:, n, :], psum[n % 4][:], ACT.Copy).then_inc(lat_raw, 1)
                act.wait_ge(block_done, done(("kpe", 0)))
                raw(("kpe",), kpe[0:B_QK, :], psum[1][0:B_QK, :])
                act.wait_ge(lat_raw, 5)
                for n in range(5):
                    act.activation(lat_square[:, n, :], lat[:, n, :], ACT.Square).then_inc(squared, 1)
                deviation(("lat", 0), psum[6], Q_LORA, col("eps_rms"), 0)
                deviation(("lat", 1), psum[7], KV_LORA, col("eps_rms"), 1)

            def mixer_b():
                act.wait_ge(block_done, done(("qup", 0)))
                for r in range(2):
                    raw(("qB", r), q_rope[:, r, :], psum[r][:], B_QK ** -0.5)
                for h in range(B_HEADS):
                    act.wait_ge(block_done, done(("qup", 1 + h // 4)))
                    bank = psum[2 + h // 2 if h < 4 else 4 + h // 2]
                    act.activation(q_b[0:B_NOPE, h, :], bank[HD * (h % 2):HD * (h % 2) + HD, :], ACT.Copy,
                                   scale=B_QK ** -0.5).then_inc(qb_stored, 1)
                act.wait_ge(block_done, done(("kvk", 0)))
                for h in range(B_HEADS):
                    act.activation(k_b[0:B_NOPE, h, :], psum[h // 2][HD * (h % 2):HD * (h % 2) + HD, :],
                                   ACT.Copy).then_inc(kb_stored, 1)
                values(range(4), ("kvv", 0), lambda i: pairs(v_ab[:, i]),
                       lambda i: psum[4 + i][:].rearrange("p (j t d) -> p j t d", j=4, t=2))

            def split_mix(layer, last, tiles):
                act.wait_ge(block_done, done(last))
                for n in tiles:
                    act.wait_ge(normed, T["normed"][("C", n)])
                    upper(("mix", layer, n), moving[0][:, n, :], mix[:, n, :])

            def norm_squares(i):
                src = z_ffn if i % 2 else z
                for n in range(KD):
                    act.wait_ge(centered, KD * i + n + 1)
                    act.activation(square[:, n, :], src[:, n, :], ACT.Square).then_inc(squared, 1)
                deviation(("ln", i), psum[7], D, col("eps_ln"), 0)
                name = ("ln_mix_b", "ln_ffn_b")[i % 2]
                for n in range(KD):
                    act.wait_ge(normed, T["normed"][("ln", i, n)])
                    act.activation(moving[0][:, n, :], src[:, n, :], ACT.Identity,
                                   bias=col(name, KD * (i // 2) + n)).then_inc(hi_ready, 1)

            def feed_forward(i):
                layer = i // 2
                n0 = AT[("gate", layer, 0)]
                act.wait_ge(p_loaded, 16 * (layer + 1))
                upper(("p", layer), p_parts[0][:, :, :], p_in_t)
                with act.Fori(0, KF // 2) as it:
                    for par in range(2):
                        w1 = COLS["conv_w"] + layer * 3 * KF + KF + par
                        b = COLS["conv_b"] + layer * KF + par
                        act.wait_ge(block_done, 4 * it + (n0 + 2 * par + 1))
                        act.activation(conv_t[:, par, :], psum[par][:], ACT.Identity,
                                       scale=cols[:, bass.ds(2 * it + w1, 1)],
                                       bias=cols[:, bass.ds(2 * it + b, 1)]).then_inc(conv_mid, 1)
                        act.wait_ge(conv_done, 2 * it + (par + 1 + KF * layer))
                        act.activation(gelu_t[:, par, :], conv_t[:, par, :], ACT.Gelu_apprx_tanh).then_inc(gelu_done, 1)
                        act.wait_ge(hid_ready, 2 * it + (par + 3 + KF * layer))
                        act.activation(hid[0][:, 2 * it + par, :], gelu_t[:, par, :], ACT.Copy).then_inc(hid_hi, 1)

            def per_layer(layer):
                for n in range(KD):
                    act.wait_ge(block_done, done(("plegate", layer, n)))
                    act.activation(sig_p[:, n, :], psum[n % 4][:], ACT.Sigmoid).then_inc(ple_sig, 1)
                if layer == 0:
                    act.wait_ge(parts_ready, T["parts"][("p", 0)])
                    load_p(1)
                    for n in range(KD):
                        act.wait_ge(x_ple, n + 1)
                        upper(("x", 1, n), moving[0][:, n, :], x[:, n, :])
                else:
                    act.wait_ge(parts_ready, T["parts"][("p", 1)])
                    act.dma_start(late, dram["tables"][:, TABS["cos2"]:NTABS]).then_inc(late_in, 16)

            def heads_ab(kind):
                attention([u for u in UNITS if u[0] == kind], copies=kind == "B")

            def mixer_c():
                for half in range(2):
                    act.wait_ge(block_done, done(("vC", 4 * half + 3)))
                    for st in range(ST):
                        act.activation(v_c[:, st, S * half:S * half + S], psum[4 * half + st][:],
                                       ACT.Copy).then_inc(v_stored, 1)
                for t in range(16):
                    act.wait_ge(block_done, done(("qkC", t)))
                    raw(("qkC", t), qk_c[:, t, :], psum[t % 4][:], HD ** -0.5 if t < 8 else 1.0)

            def heads_c():
                units = [u for u in UNITS if u[0] == "C"]
                attention(units, blend=True)
                for n in range(C_HEADS):
                    act.wait_ge(attended, UNIT_AT[("C", n)] + 1)
                    act.activation(square[:, n, :], mix[:, n, :], ACT.Square).then_inc(squared, 1)
                for n in range(C_HEADS):
                    if n >= 2:
                        act.wait_ge(normed, T["normed"][("C", n - 2)])
                    deviation(("C", n), psum[4 + n % 2], P, col("eps_ln"), n % 2)
                    if n >= 2:
                        split_mix(1, ("qkC", 15), (n - 2,))
                split_mix(1, ("qkC", 15), (C_HEADS - 2, C_HEADS - 1))

            def rms(i):
                for n in range(KD):
                    if i == 0:
                        act.wait_ge(x_ple, KD * DEPTH - KD + n + 1)
                    else:
                        act.wait_ge(x_next, KD * (i - 1) + n + 1)
                    act.activation(z[:, n, :], x[:, n, :], ACT.Square).then_inc(squared, 1)
                deviation(("rms", i), psum[7], D, col("eps_rms"), 0)
                for n in range(KD if i < DEPTH else 0):
                    act.wait_ge(normed, T["normed"][("rms", i, n)])
                    upper(("h2", i, n), moving[0][:, n, :], z[:, n, :])

            def store(dst, src, func=ACT.Copy, **more):
                act.activation(dst, src, func, **more).then_inc(stored, 1)

            def project_second(layer):
                at = lambda key: act.wait_ge(block_done, done(key))

                def gate(n):
                    act.wait_ge(spread, 10 * layer + n + 1)
                    store(gates[:, n // 2, n % 2, :], psum[6][:])

                at(("small", layer))
                store(gate_sig, psum[0][:], ACT.Sigmoid)
                store(mix[:, 6, :], psum[0][:], ACT.Identity, bias=col("fox_bias", layer))
                act.wait_ge(stored, T["stored"][("fl", layer)])
                link(act.activation(mix[:, 7, :], mix[:, 6, :], ACT.Abs))
                link(act.activation(mix[:, 7, :], mix[:, 7, :], ACT.Exp, scale=-1.0))
                store(mix[:, 0, :], mix[:, 7, :], ACT.Ln, bias=ones[:, 0:1])
                at(("kcvc", layer))
                store(kcvc, psum[1][:])
                at(("vsvw", layer))
                act.wait_ge(prepared, T["prepared"][("blocks", layer)])
                for c in range(2):
                    rows = slice(HD * c, HD * c + HD)
                    ins = act.activation(blocks[rows, :, 0, c, :], blocks_x[rows], ACT.Copy)
                ins.then_inc(hi_ready, 1)
                for c, v in ((0, v_s), (1, v_w)):
                    store(v[:, :, HD:2 * HD], psum[2][:].rearrange("p (t c d) -> p t c d", t=ST, c=2)[:, :, c, :])
                gate(0)
                at(("kskw", layer))
                for c, key in enumerate(("ks", "kw")):
                    rows = slice(HD * c, HD * c + HD)
                    act.activation(ksw[0:HD, c, :], psum[3][rows, :], ACT.Copy)
                    raw((key, layer), ksw[HD:P, c, :], psum[3][rows, :])
                gate(1)
                gate(2)
                for t in range(2):
                    at(("nq", layer, t))
                    raw((f"nq{t}", layer), nq[:, t, :], psum[1 + t][:], HD ** -0.5)
                    gate(3 + t)
                gate(5)
                for t in range(2):
                    at(("fq", layer, t))
                    store(fqk[:, t, :], psum[t][:], scale=HD ** -0.5)
                act.wait_ge(prepared, T["prepared"][("hid", layer)])
                store(hid_k, hid_sum[:, 0, 0:CMP_N], ACT.Silu, bias=col("cmp_b1", 2 * layer))
                store(hid_v, hid_sum[:, 0, CMP_N:2 * CMP_N].unsqueeze(1).broadcast_to([P, 4, CMP_N]), ACT.Silu,
                      bias=col("cmp_b1", 2 * layer + 1))
                act.wait_ge(compress_step, 5 * layer + 1)
                raw(("kc", layer), kc, psum[7][:, 0:CMP_N], 1.0, col("cmp_b2k", layer))
                for t in range(2):
                    at(("fk", layer, t))
                    store(fqk[:, 2 + t, :], psum[2 + t][:])
                act.wait_ge(prepared, T["prepared"][("cmp_shift", layer)])
                store(rstd[:, 1, :], std[:, 1, :], ACT.Exp)
                at(("fv", layer, 1))
                for st in range(ST):
                    store(pairs(v_f[:, st]), psum[st][:, 0:256].rearrange("p (j t d) -> p j t d", j=2, t=2))
                for t in range(2):
                    at(("pool", layer, t))
                    store(pool_u[:, t, PAD:PAD + S], psum[t][:])
                for t in range(4):
                    at(("conv", layer, t))
                    store((conv_x if t < 2 else conv_b)[:, t % 2, :], psum[(2 + t) % 4][:])
                for g in range(4):
                    act.wait_ge(spread, 10 * layer + 6 + g + 1)
                    rows = slice(HD * (g % 2), HD * (g % 2) + HD)
                    store(mix[rows, 2 + g // 2, :], psum[g][rows, :],
                          scale=col("pool_scale", 2 * layer + g // 2, rows))

            def heads_second(layer):
                attention([u for u in UNITS if len(u) == 3 and u[1] == layer], causal=True)

            def merge(layer):
                for t in range(KD):
                    act.wait_ge(block_done, done(("sgate", layer, t)))
                    store(sg[:, t, :], psum[t][:], ACT.Silu)
                for t in GATE_ORDER:
                    act.wait_ge(gated, KD * layer + GATE_ORDER.index(t) + 1)
                    upper(("branch", layer, t), branch[0][:, t, :], mix[:, t, :])
                n0 = AT[("merge", layer, 0, 0)]
                with act.Fori(0, KD // 4) as it:
                    for d in range(4):
                        act.wait_ge(merged, 4 * it + (d + 1 + KD * layer))
                        for i in range(N_BRANCH):
                            act.wait_ge(block_done, 20 * it + (n0 + 5 * d + i + 1))
                            act.activation(sig_m[:, d % 2, i, :], psum[i][:], ACT.Sigmoid).then_inc(sig_ready, 1)

            stages = [
                lambda: (setup(), mixer_a()), lambda: (heads_ab("A"), mixer_b()), lambda: heads_ab("B"), lambda: None, lambda: norm_squares(0),
                lambda: feed_forward(1), lambda: norm_squares(1), lambda: per_layer(0),
                mixer_c, heads_c, lambda: None, lambda: norm_squares(2),
                lambda: feed_forward(3), lambda: norm_squares(3), lambda: per_layer(1),
            ]
            for layer in range(DEPTH):
                stages += [lambda l=layer: rms(l), lambda l=layer: project_second(l), lambda: None,
                           lambda l=layer: heads_second(l), lambda l=layer: merge(l)]
            stages += [lambda: rms(DEPTH)]
            for stage in stages:
                stage()

        @block.vector
        def _(dve):
            linked = [0]

            def link(ins):
                linked[0] += 1
                ins.then_inc(link_dve, 1)
                dve.wait_ge(link_dve, linked[0])

            def rope(job, tile, rows, cos, sin, n=S, outs=None):
                g = ROPE_AT[job]
                if g < ROPES_1:
                    dve.wait_ge(rope_raw, g + 1)
                    dve.tensor_tensor(rope_parts[1][0:rows, g % 2, :], tile, rope_parts[0][0:rows, g % 2, :].bitcast(F32),
                                      ALU.subtract).then_inc(rope_split, 1)
                dve.wait_ge(rope_perm, g + 1)
                tmp = rope_tmp[0:rows, g % 2, 0:n]
                dve.tensor_tensor(tmp, psum[4 + g % 2][0:rows, 0:n], sin, ALU.mult)
                link(dve.tensor_tensor(tile, tile, cos, ALU.mult))
                for out, at in outs or [(tile, slice(0, rows))]:
                    ins = dve.tensor_tensor(out, tile[at], tmp[at], ALU.add)
                ins.then_inc(roped, 1)

            def lower(key, pair, src):
                dve.wait_ge(hi_ready, T["parts"][key])
                dve.tensor_tensor(pair[1], src, pair[0].bitcast(F32), ALU.subtract).then_inc(parts_ready, 1)

            def inverse(dst, src, rows):
                link(dve.transpose(dst, src))
                few = inverse_tmp[rows, :]
                link(dve.reciprocal(few, dst.rearrange("p (b r) -> p b r", r=32)[:, :, 0]))
                link(dve.transpose(dst, few.unsqueeze(2).broadcast_to([rows.stop - rows.start, S // 32, 32])))

            def normalize(key, tiles, gains, buf, behind=None):
                dve.wait_ge(std_ready, T["std"][key])
                inverse(rstd[:, buf, :], std[:, buf, :], slice(0, P))
                for n, (dst, src) in enumerate(tiles):
                    dve.scalar_tensor_tensor(out=dst, in0=src, scalar=gains(n), in1=rstd[:, buf, :], op0=ALU.mult,
                                             op1=ALU.mult).then_inc(normed, 1)
                    if behind and n >= 2:
                        behind(n - 2)
                for n in range(max(len(tiles) - 2, 0) if behind else len(tiles), len(tiles)):
                    behind(n)

            def attention(units, finish, blend=False, causal=False, counts=False, first=()):
                turns = [(u, i) for u in units for i in range(ST)]
                comps = 2 if blend else 1

                def mixed(u, i):
                    s, t = SCORE_AT[(u, i, 0)], TURN_AT[(u, i)]
                    c = s % 8
                    dve.wait_ge(exped, s + 2)
                    link(dve.reciprocal(rownorm[:, c:c + 2], rowsum[:, c:c + 2]))
                    link(dve.tensor_tensor(rownorm[:, c + 1:c + 2], rownorm[:, c + 1:c + 2], neg_lam[:, 5:6], ALU.mult))
                    p0, p1 = prob[:, s % 4, :], prob[:, (s + 1) % 4, :]
                    link(dve.tensor_scalar(p0, p0, rownorm[:, c:c + 1], None, ALU.mult))
                    dve.scalar_tensor_tensor(out=p0, in0=p1, scalar=rownorm[:, c + 1:c + 2], in1=p0, op0=ALU.mult,
                                             op1=ALU.add).then_inc(blended, 1)

                def counted(u, i):
                    t, n = TURN_AT[(u, i)], UNIT_AT[u]
                    dve.wait_ge(turned, t + 1)
                    if i == 0 and n >= 2:
                        dve.wait_ge(weighed, n - 1)
                    dve.tensor_tensor(pt[:, n % 2, :, i * P:i * P + P], psum[4 + t % 2][:].rearrange("p (k q) -> p k q", k=ST),
                                      count[:, :, i * P:i * P + P], ALU.mult).then_inc(pt_stored, 1)

                pending = [(n, step) for n, step in enumerate(first)]
                for n, (u, i) in enumerate(turns):
                    for c in range(comps):
                        s = SCORE_AT[(u, i, c)]
                        w = (i + 1) * P if causal else S
                        dve.wait_ge(scored, s + 1)
                        dve.tensor_reduce(negmax[:, s % 8:s % 8 + 1], psum[s % 4][:, 0:w], AX_X, ALU.max,
                                          negate=True).then_inc(maxed, 1)
                    if blend and n:
                        mixed(*turns[n - 1])
                    if counts and n >= AHEAD:
                        counted(*turns[n - AHEAD])
                    if pending and pending[0][0] <= n:
                        pending.pop(0)[1]()
                    if i == ST - 1:
                        pending += [(n + FINISH_LAG + at, step) for at, step in enumerate(finish(u))]
                if blend:
                    mixed(*turns[-1])
                if counts:
                    for turn in turns[-AHEAD:]:
                        counted(*turn)
                for _, step in pending:
                    step()

            def divided(u, dst, odd, gate=None, add=False):
                n = UNIT_AT[u]
                own, other = (slice(HD, P), slice(0, HD)) if odd else (slice(0, HD), slice(HD, P))
                bank = psum[6 + n % 2]
                inv = rope_tmp[own, 0, :]

                def invert():
                    dve.wait_ge(weighed, n + 1)
                    inverse(inv, bank[other, :], own)

                def gated_inverse():
                    link(dve.tensor_tensor(inv, inv, gate[own], ALU.mult))

                def store():
                    if not add:
                        dve.tensor_tensor(dst[own], bank[own, :], inv, ALU.mult).then_inc(attended, 1)
                        return
                    link(dve.tensor_tensor(inv, bank[own, :], inv, ALU.mult))
                    dve.tensor_tensor(dst[own], dst[own], inv, ALU.add).then_inc(attended, 1)

                return [invert] + [gated_inverse] * (gate is not None) + [store]

            def setup():
                dve.nop().then_inc(hid_ready, 2)
                dve.nop().then_inc(merged, 2)
                for n in range(KD):
                    lower(("x", 0, n), both(moving, np.s_[:, n, :]), x[:, n, :])
                dve.wait_ge(inputs_in, 16 * N_INPUTS)
                n = [0]

                def step(ins):
                    n[0] += 1
                    ins.then_inc(setup_dve, 1)
                    dve.wait_ge(setup_dve, n[0])

                step(dve.tensor_copy(pos_f, pos_raw))
                for j, name in ((0, "inv_a"), (1, "inv_b")):
                    dve.tensor_scalar(angle[:, j, :], pos_f, col(name), None, ALU.mult)
                step(dve.memset(std[:, 0, 0:1], 0.0))
                step(dve.tensor_scalar(turns[:, :, :], angle[:, :, :], 1.0 / (2 * math.pi), 12582912.0, ALU.mult, ALU.add))
                step(dve.tensor_scalar(turns[:, :, :], turns[:, :, :], -12582912.0, None, ALU.add))
                step(dve.scalar_tensor_tensor(out=rest[:, :, :], in0=turns[:, :, :], scalar=-TWO_PI[0],
                                              in1=angle[:, :, :], op0=ALU.mult, op1=ALU.add))
                for part in TWO_PI[1:]:
                    step(dve.scalar_tensor_tensor(out=rest[:, :, :], in0=turns[:, :, :], scalar=-part,
                                                  in1=rest[:, :, :], op0=ALU.mult, op1=ALU.add))
                step(dve.tensor_scalar(rest[:, :, :], rest[:, :, :], 3.1415925, -3.1415925, ALU.min, ALU.max))
                assert n[0] == SETUP["rest"], n
                dve.tensor_tensor(lam_in[:, 0:HD], lam_in[:, 0:HD], lam_in[:, HD:2 * HD], ALU.mult)
                step(dve.tensor_tensor(lam_in[:, 2 * HD:3 * HD], lam_in[:, 2 * HD:3 * HD], lam_in[:, 3 * HD:4 * HD], ALU.mult))
                step(dve.tensor_reduce(neg_lam[:, 0:2], lam_in.rearrange("p (a b) -> p a b", a=2)[:, :, 0:HD], AX_X, ALU.add))
                assert n[0] == SETUP["lam_sums"], n
                dve.wait_ge(setup_act, 1)
                step(dve.tensor_tensor(angle[:, :, :], angle[:, :, :], angle[:, :, :], ALU.mult))
                dve.tensor_scalar(cos_a, angle[:, 0, :], -2.0, 1.0, ALU.mult, ALU.add)
                step(dve.tensor_scalar(cos_b, angle[:, 1, :], -2.0, 1.0, ALU.mult, ALU.add))
                dve.wait_ge(setup_act, 2)
                step(dve.tensor_tensor(neg_lam[:, 4:5], neg_lam[:, 3:4], neg_lam[:, 2:3], ALU.subtract))
                dve.tensor_scalar(neg_lam[:, 5:6], neg_lam[:, 4:5], -LAMBDA_INIT, None, ALU.add)
                dve.tensor_scalar(neg_lam[:, 6:7], col("subln"), 1.0 - LAMBDA_INIT, None, ALU.mult)
                dve.tensor_copy(perm_r[:, 0, :], perm_a)
                dve.tensor_copy(perm_r[:, 1, :], perm_b)
                dve.tensor_copy(ident_bf[:], ident).then_inc(constants_bf, 1)
                dve.tensor_copy(tri_bf[:], masks_in[:, S:S + P]).then_inc(constants_bf, 1)
                dve.tensor_copy(cmp_bias_bf[:], masks_in[:, 0:S]).then_inc(constants_bf, 1)
                dve.wait_ge(later_in, 16 * N_LATER)
                dve.tensor_scalar(mask_a, count, 0.5, MASK, ALU.is_lt, ALU.mult).then_inc(constants_bf, 1)
                dve.wait_ge(constants_bf, 4)

            def mixer_a():
                for t in range(8):
                    rope(("qkA", t), qk_a[:, t, :], P, cos_a, sin_a)
                rope(("kpe",), kpe[0:B_QK, :], B_QK, cos_b[0:B_QK, :], sin_b[0:B_QK, :])
            def mixer_b():
                for r in range(2):
                    outs = [(q_b[B_NOPE:B_QK, 4 * r + c, :], slice(B_ROPE * c, B_ROPE * c + B_ROPE)) for c in range(4)]
                    rope(("qB", r), q_rope[:, r, :], P, cos_b, sin_b, outs=outs)

            def split_here(key, n, src):
                dve.tensor_copy(moving[0][:, n, :], src).then_inc(hi_ready, 1)
                lower(key, both(moving, np.s_[:, n, :]), src)

            def mixed_steps(tiles):
                def split(n):
                    dve.wait_ge(block_done, done(("kvv", 0)))
                    dve.wait_ge(attended, UNIT_AT[("A" if n < 4 else "B", 2 * (n % 4) + 1)] + 1)
                    split_here(("mix", 0, n), n, mix[:, n, :])
                return [lambda n=n: split(n) for n in tiles]

            def latent_steps():
                steps = []
                for j, (name, lo, hi) in enumerate((("q_norm", 0, 3), ("kv_norm", 3, 5))):
                    def scale(j=j, name=name, lo=lo, hi=hi):
                        normalize(("lat", j), [(lat[:, n, :], lat[:, n, :]) for n in range(lo, hi)],
                                  lambda n: col(name, n), j)
                    steps.append(scale)
                for n in range(5):
                    def split(n=n):
                        if n == 0:
                            dve.wait_ge(block_done, done(("kpe", 0)))
                            dve.wait_ge(normed, T["normed"][("lat", 4)])
                        split_here(("lat", n), n, lat[:, n, :])
                    steps.append(split)
                for j in range(B_HEADS // 2):
                    def spread(j=j):
                        dve.wait_ge(roped, ROPE_AT[("kpe",)] + 1)
                        dve.tensor_copy(k_b[B_NOPE:B_QK, 2 * j:2 * j + 2, :], kpe[B_NOPE:B_QK, :].unsqueeze(1).broadcast_to(
                            [B_ROPE, 2, S])).then_inc(kpe_spread, 1)
                    steps.append(spread)
                return steps

            def split_mix(layer, tiles):
                for n in tiles:
                    lower(("mix", layer, n), both(moving, np.s_[:, n, :]), mix[:, n, :])

            def heads_ab(kind):
                def finish(u):
                    steps = divided(u, mix[:, (0 if u[0] == "A" else 4) + u[1] // 2, :], u[1] % 2)
                    return steps + (mixed_steps((4 + u[1] // 2,)) if kind == "B" and u[1] % 2 else [])

                attention([u for u in UNITS if u[0] == kind], finish, counts=kind == "A",
                          first=latent_steps() if kind == "A" else mixed_steps(range(4)))

            def add_early(tiles, n, early, summed_all):
                ins = dve.tensor_tensor(early_sum, tiles[:, 0, :] if n == 1 else early_sum, tiles[:, n, :], ALU.add)
                if n == early - 1:
                    ins.then_inc(summed_all, 1)
                else:
                    link(ins)

            def residual(i):
                layer = i // 2
                for n in range(KD):
                    if i % 2 == 0:
                        dve.wait_ge(block_done, done(("mixout", layer, n)))
                        bank = psum[n % 4]
                    else:
                        dve.wait_ge(block_done, done(("down", layer, n // 4, KF // 2 - 1)))
                        bank = psum[4 + n] if n < 4 else psum[n - 4]
                    tiles = z_ffn if i % 2 else z
                    dve.scalar_tensor_tensor(out=tiles[:, n, :], in0=x[:, n, :], scalar=ALPHA, in1=bank[:],
                                             op0=ALU.mult, op1=ALU.add).then_inc(z_ready, 1)
                    early = EARLY_DOWN if i % 2 else EARLY
                    if 0 < n < early:
                        dve.wait_ge(z_ready, KD * i + n + 1)
                        add_early(tiles, n, early, z_summed)

            def norm(i):
                t = z_ffn if i % 2 else z
                dve.wait_ge(mean_ready, i + 1)
                for n in range(KD):
                    dve.scalar_tensor_tensor(out=t[:, n, :], in0=psum[6][:], scalar=-1.0 / D, in1=t[:, n, :],
                                             op0=ALU.mult, op1=ALU.add).then_inc(centered, 1)
                gain, bias = (("ln_mix_g", "ln_mix_b"), ("ln_ffn_g", "ln_ffn_b"))[i % 2]

                def lower_biased(n):
                    hi, lo = both(moving, np.s_[:, n, :])
                    dve.wait_ge(hi_ready, T["parts"][("ln", i, n)])
                    dve.scalar_tensor_tensor(out=lo, in0=t[:, n, :], scalar=col(bias, KD * (i // 2) + n), in1=hi.bitcast(F32),
                                             op0=ALU.add, op1=ALU.subtract).then_inc(parts_ready, 1)

                normalize(("ln", i), [(t[:, n, :], t[:, n, :]) for n in range(KD)],
                          lambda n: col(gain, KD * (i // 2) + n), 0, lower_biased)
                dve.wait_ge(parts_ready, T["parts"][("ln", i, KD - 1)])
                for n in range(KD):
                    hi, lo = both(moving, np.s_[:, n, :])
                    dve.tensor_tensor(x[:, n, :], hi.bitcast(F32), lo.bitcast(F32), ALU.add)

            def feed_forward(i):
                layer = i // 2
                n0 = AT[("gate", layer, 0)]
                w = COLS["conv_w"] + layer * 3 * KF
                lower(("p", layer), both(p_parts, np.s_[:, :, :]), p_in_t)
                with dve.Fori(0, KF // 2) as it:
                    for par in range(2):
                        f1 = par + 1 + KF * layer
                        c, a = conv_t[:, par, :], psum[par]
                        dve.wait_ge(conv_mid, 2 * it + f1)
                        dve.scalar_tensor_tensor(out=c[:, 1:S], in0=a[:, 0:S - 1],
                                                 scalar=cols[:, bass.ds(2 * it + (w + par), 1)], in1=c[:, 1:S],
                                                 op0=ALU.mult, op1=ALU.add).then_inc(conv_mid2, 1)
                        dve.wait_ge(conv_mid2, 2 * it + f1)
                        dve.scalar_tensor_tensor(out=c[:, 0:S - 1], in0=a[:, 1:S],
                                                 scalar=cols[:, bass.ds(2 * it + (w + 2 * KF + par), 1)], in1=c[:, 0:S - 1],
                                                 op0=ALU.mult, op1=ALU.add).then_inc(conv_done, 1)
                        dve.wait_ge(gelu_done, 2 * it + f1)
                        dve.wait_ge(block_done, 4 * it + (n0 + 2 * par + 2))
                        dve.tensor_tensor(gelu_t[:, par, :], gelu_t[:, par, :], psum[2 + par][:],
                                          ALU.mult).then_inc(hid_ready, 1)
                        dve.wait_ge(hid_hi, 2 * it + f1)
                        tile = 2 * it + par
                        dve.tensor_tensor(hid[1][:, tile, :], gelu_t[:, par, :], hid[0][:, tile, :].bitcast(F32),
                                          ALU.subtract).then_inc(hid_parts, 1)

            def per_layer(layer):
                for n in range(KD):
                    dve.wait_ge(ple_sig, KD * layer + n + 1)
                    dve.wait_ge(block_done, done(("pleproj", layer, n // 4)))
                    dve.tensor_tensor(sig_p[:, n, :], sig_p[:, n, :], psum[4 + n % 4][:], ALU.mult).then_inc(ple_term, 1)
                    dve.wait_ge(ple_term, KD * layer + n + 1)
                    dve.tensor_tensor(x[:, n, :], x[:, n, :], sig_p[:, n, :], ALU.add).then_inc(x_ple, 1)
                for n in range(KD if layer == 0 else 0):
                    lower(("x", 1, n), both(moving, np.s_[:, n, :]), x[:, n, :])

            def mixer_c():
                for t in range(16):
                    rope(("qkC", t), qk_c[:, t, :], P, cos_a, sin_a)

            def heads_c():
                def finish(u):
                    n = UNIT_AT[u]

                    def store():
                        dve.wait_ge(weighed, n + 1)
                        dve.tensor_copy(mix[:, u[1], :], psum[6 + n % 2][:]).then_inc(attended, 1)

                    return [store]

                attention([u for u in UNITS if u[0] == "C"], finish, blend=True)
                for n in range(C_HEADS):
                    normalize(("C", n), [(mix[:, n, :], mix[:, n, :])], lambda _: neg_lam[:, 6:7], n % 2)
                    if n:
                        split_mix(1, (n - 1,))
                split_mix(1, (C_HEADS - 1,))

            def rms(i):
                name, lo = ("norm2_g", KD * i) if i < DEPTH else ("final_g", 0)
                behind = (lambda n: lower(("h2", i, n), both(moving, np.s_[:, n, :]), z[:, n, :])) if i < DEPTH else None
                normalize(("rms", i), [(z[:, n, :], x[:, n, :]) for n in range(KD)], lambda n: col(name, lo + n), 0, behind)

            def project_second(layer):
                stored_at = lambda key: dve.wait_ge(stored, T["stored"][(key, layer)])
                for v in (v_s, v_w):
                    dve.memset(v.rearrange("p t (c d) -> p t c d", c=3)[:, :, 0:3:2, :], 1.0).then_inc(cleared, 1)
                dve.memset(v_f.rearrange("p t j (c d) -> p (t j) c d", c=3)[:, :, 1, :], 1.0).then_inc(cleared, 1)
                dve.memset(vc_bd, 0.0).then_inc(cleared, 1)
                dve.memset(conv_u[:, :, 0:2], 0.0).then_inc(cleared, 1)
                dve.memset(mix[:, 1, :], 0.0).then_inc(cleared, 1)
                dve.wait_ge(parts_ready, T["parts"][("h2", layer, KD - 1)])
                for c in range(2):
                    dve.memset(blocks[HD * c:HD * c + HD, :, :, 1 - c, :].bitcast(F32), 0.0).then_inc(cleared, 1)
                dve.memset(blocks_x[:, :, CMP_N - 1:CMP_N], 0.0).then_inc(cleared, 1)
                dve.wait_ge(cleared, 1 + N_CLEAR * layer + 9)
                stored_at("kcvc")
                by_16 = kcvc.rearrange("p (n l) -> p l n", l=CMP_STRIDE)
                pos = cmp_pos[:, layer * CMP_LEN:layer * CMP_LEN + CMP_LEN]
                for j in range(2):
                    ins = dve.tensor_tensor(
                        blocks_x[:, 16 * j:16 * j + 16, 0:CMP_N - 1], by_16[:, :, j:j + CMP_N - 1],
                        pos[:, 16 * j:16 * j + 16].unsqueeze(2).broadcast_to([P, 16, CMP_N - 1]), ALU.add)
                ins.then_inc(prepared, 1)
                dve.wait_ge(hi_ready, T["parts"][("blocks", layer)])
                for c in range(2):
                    rows = slice(HD * c, HD * c + HD)
                    ins = dve.tensor_tensor(blocks[rows, :, 1, c, :], blocks_x[rows], blocks[rows, :, 0, c, :].bitcast(F32),
                                            ALU.subtract)
                ins.then_inc(parts_ready, 1)
                dve.wait_ge(late_in, 16)
                cos2, sin2 = tab("cos2", S), tab("sin2", S)
                rope(("ks", layer), ksw[:, 0, :], P, cos2, sin2)
                rope(("kw", layer), ksw[:, 1, :], P, cos2, sin2)
                rope(("nq0", layer), nq[:, 0, :], P, cos2, sin2)
                rope(("nq1", layer), nq[:, 1, :], P, cos2, sin2)
                dve.wait_ge(block_done, done(("w1", layer, 3)))
                link(dve.tensor_copy(hid_sum[:, 1, :], psum[3][:, 2 * CMP_N:4 * CMP_N]))
                dve.tensor_tensor(hid_sum[:, 0, :], psum[3][:, 0:2 * CMP_N], hid_sum[:, 1, :], ALU.add).then_inc(prepared, 1)
                dve.wait_ge(compress_step, 5 * layer + 2)
                for h in range(4):
                    rows = slice(32 * h, 32 * h + 32)
                    ins = dve.tensor_tensor(vc_bd[rows, h // 2, HD * (h % 2):HD * (h % 2) + HD], psum[3][rows, 0:HD],
                                            b2v[rows, layer * HD:layer * HD + HD], ALU.add)
                ins.then_inc(prepared, 1)
                rope(("kc", layer), kc, P, tab("cos2c", CMP_N), tab("sin2c", CMP_N), CMP_N)
                stored_at("ln")
                link(dve.scalar_tensor_tensor(out=mix[:, 6, :], in0=mix[:, 6, :], scalar=0.0, in1=mix[:, 0, :],
                                              op0=ALU.min, op1=ALU.subtract))
                link(dve.tensor_tensor_scan(mix[:, 7, :], mix[:, 6, :], mix[:, 1, :], 0.0, ALU.add, ALU.add))
                hi, lo = decay_q[:, :], mix[:, 6, :]
                link(dve.tensor_copy(hi, mix[:, 7, :]))
                link(dve.tensor_tensor(lo, mix[:, 7, :], hi.bitcast(F32), ALU.subtract))
                for name, rows in (("fox_k", decay_k[:, :]), ("fox_q", decay_q[:, :])):
                    link(dve.tensor_scalar(rows, hi.bitcast(F32), col(name, 0), col(name, 2), ALU.mult, ALU.add))
                    ins = dve.scalar_tensor_tensor(out=rows, in0=lo, scalar=col(name, 1), in1=rows.bitcast(F32), op0=ALU.mult,
                                                   op1=ALU.add)
                ins.then_inc(prepared, 1)
                dve.wait_ge(compress_step, 5 * layer + 3)
                for odd in range(2):
                    s8 = psum[6 + odd][:, 0:2 * P].rearrange("p (a n) -> p a n", n=CMP_N)
                    best = cmp_negmax[:, 8 * odd:8 * odd + 8]
                    link(dve.tensor_reduce(best, s8, AX_X, ALU.max, negate=True))
                    ins = dve.tensor_tensor(
                        std[:, 1, :].rearrange("p (a b n) -> p a b n", b=2, n=CMP_N)[:, :, odd, :], s8,
                        best.unsqueeze(2).broadcast_to([P, 8, CMP_N]), ALU.add)
                ins.then_inc(prepared, 1)
                dve.wait_ge(compress_step, 5 * layer + 4)
                dve.tensor_tensor(prob[:, 3, :], psum[7][:], tab("cmp_mask", S), ALU.mult).then_inc(prepared, 1)
                for t in (pool_u, pool_a, pool_b):
                    dve.memset(t[:, :, 0:PAD], 0.0).then_inc(cleared, 1)
                dve.wait_ge(cleared, 1 + N_CLEAR * (layer + 1))
                stored_at("pool1")
                u, a, b = pool_u, pool_a, pool_b
                end = PAD + S
                step = lambda dst, src, w: link(dve.tensor_tensor(dst[:, :, 2 * w:end], src[:, :, 2 * w:end],
                                                                  src[:, :, w:end - w], ALU.add))

                def mean(src, g):
                    rows = slice(HD * (g % 2), HD * (g % 2) + HD)
                    link(dve.tensor_tensor(mix[rows, 2 + g // 2, :], src[rows, g // 2, PAD:end],
                                           inv_count[rows, g // 2, :], ALU.mult))

                step(a, u, 1)
                step(b, a, 2)
                mean(a, 0)
                mean(b, 1)
                step(a, b, 4)
                step(b, a, 8)
                mean(a, 2)
                mean(b, 3)
                dve.tensor_tensor(mix[:, 2:4, :], mix[:, 2:4, :], u[:, :, PAD:end], ALU.subtract).then_inc(prepared, 1)
                dve.wait_ge(compress_step, 5 * layer + 5)
                stored_at("g5")
                for j in range(2):
                    inv = rope_tmp[:, j, :]
                    link(dve.tensor_scalar(inv, psum[6 + j][:], 0.5, None, ALU.max))
                    inverse(std[:, j, :], inv, slice(0, P))
                    link(dve.tensor_tensor(inv, std[:, j, :], gates[:, 0, j, :], ALU.mult))
                    dve.tensor_tensor(mix[:, j, :], psum[4 + j][:], inv, ALU.mult).then_inc(prepared, 1)
                stored_at("cb1")
                for t in range(2):
                    dve.wait_ge(block_done, done(("conv", layer, 4 + t)))
                    dve.tensor_tensor(conv_u[:, t, 2:2 + S], psum[2 + t][:],
                                      conv_x[:, t, :], ALU.mult).then_inc(prepared, 1)

            def convolution_steps(layer):
                steps = []
                for t in range(2):
                    def taps(t=t):
                        y = mix[:, 4 + t, :]
                        wcol = lambda k: col("conv2_w", 6 * layer + 2 * k + t)
                        link(dve.tensor_scalar(y, conv_u[:, t, 0:S], wcol(0), None, ALU.mult))
                        link(dve.scalar_tensor_tensor(out=y, in0=conv_u[:, t, 1:1 + S], scalar=wcol(1), in1=y, op0=ALU.mult,
                                                      op1=ALU.add))

                    def last_tap(t=t):
                        y = mix[:, 4 + t, :]
                        link(dve.scalar_tensor_tensor(out=y, in0=conv_u[:, t, 2:2 + S],
                                                      scalar=col("conv2_w", 6 * layer + 4 + t), in1=y, op0=ALU.mult,
                                                      op1=ALU.add))
                        dve.tensor_tensor(y, y, conv_b[:, t, :], ALU.mult).then_inc(prepared, 1)

                    steps += [taps, last_tap]
                return steps

            def heads_second(layer):
                def finish(u):
                    h = u[2]
                    if u[0] == "fox":
                        return divided(u, mix[:, 6 + h // 2, :], h % 2)
                    else:
                        return divided(u, mix[:, h // 2, :], h % 2, gates[:, 1 if u[0] == "slc" else 2, h // 2, :], True)

                dve.wait_ge(prepared, T["prepared"][("cu1", layer)])
                attention([u for u in UNITS if len(u) == 3 and u[1] == layer], finish, causal=True,
                          first=convolution_steps(layer))

            def merge(layer):
                for t in GATE_ORDER:
                    if t in (0, 1, 6, 7):
                        dve.wait_ge(attended, UNIT_AT[("win" if t < 2 else "fox", layer, 2 * (t % 2) + 1)] + 1)
                    dve.wait_ge(stored, T["stored"][(f"sg{t}", layer)])
                    dve.tensor_tensor(mix[:, t, :], mix[:, t, :], sg[:, t, :], ALU.mult).then_inc(gated, 1)
                for t in GATE_ORDER:
                    lower(("branch", layer, t), both(branch, np.s_[:, t, :]), mix[:, t, :])
                n0 = AT[("merge", layer, 0, 0)]
                with dve.Fori(0, KD // 4) as it:
                    for d in range(4):
                        t = sig_m[:, d % 2]
                        dve.wait_ge(block_done, 20 * it + (n0 + 5 * d + N_BRANCH + 1))
                        dve.wait_ge(sig_ready, 16 * it + (4 * d + 4 + 4 + 32 * layer))
                        for i in range(N_BRANCH):
                            ins = dve.tensor_tensor(t[:, i, :], t[:, i, :], psum[4 + i][:], ALU.mult)
                        ins.then_inc(merge_link, 1)
                        dve.wait_ge(merge_link, 16 * it + (4 * d + 1 + 32 * layer))
                        ins = dve.tensor_tensor(t[:, 0:2, :], t[:, 0:2, :], t[:, 2:4, :], ALU.add)
                        ins.then_inc(merge_link, 1)
                        dve.wait_ge(merge_link, 16 * it + (4 * d + 2 + 32 * layer))
                        ins = dve.tensor_tensor(t[:, 0, :], t[:, 0, :], t[:, 1, :], ALU.add)
                        ins.then_inc(merge_link, 1)
                        dve.wait_ge(merge_link, 16 * it + (4 * d + 3 + 32 * layer))
                        hi, lo = both(acc, np.s_[:, 4 * it + d, :])
                        dve.tensor_copy(hi, t[:, 0, :]).then_inc(merge_link, 1)
                        dve.wait_ge(merge_link, 16 * it + (4 * d + 4 + 32 * layer))
                        dve.tensor_tensor(lo, t[:, 0, :], hi.bitcast(F32), ALU.subtract).then_inc(merged, 1)
                for n in range(KD):
                    dve.wait_ge(block_done, done(("out2", layer, n)))
                    dve.tensor_tensor(x[:, n, :], psum[n % 4][:], x[:, n, :], ALU.add).then_inc(x_next, 1)
                    if 2 <= n <= EARLY:
                        dve.wait_ge(squared, T["squared"][("rms", layer + 1, n - 1)])
                        add_early(z, n - 1, EARLY, squares_summed)

            stages = [
                lambda: (setup(), mixer_a()), lambda: (heads_ab("A"), mixer_b()), lambda: heads_ab("B"), lambda: residual(0), lambda: norm(0),
                lambda: feed_forward(1), lambda: (residual(1), norm(1)), lambda: per_layer(0),
                mixer_c, heads_c, lambda: residual(2), lambda: norm(2),
                lambda: feed_forward(3), lambda: (residual(3), norm(3)), lambda: per_layer(1),
            ]
            for layer in range(DEPTH):
                stages += [lambda l=layer: rms(l), lambda l=layer: project_second(l), lambda: None,
                           lambda l=layer: heads_second(l), lambda l=layer: merge(l)]
            stages += [lambda: rms(DEPTH)]
            for stage in stages:
                stage()

        @block.gpsimd
        def _(pool):
            pool.memset(unit[:, :], 1.0).then_inc(unit_set, 1)
            pool.memset(v_ab.rearrange("p t j (c d) -> p (t j) c d", c=3)[:, :, 1, :], 1.0).then_inc(cleared, 1)
            pool.wait_ge(unit_set, 1)

            def split(s, n, used=None):
                pool.wait_ge(full[s], 16 * (n // RING) + 16 if isinstance(n, int) else used[0])
                if used:
                    pool.wait_ge(block_done, used[1])
                pool.tensor_tensor(w_parts[0][:, s, :], ring[:, s, :], unit[:, 0:1].broadcast_to([P, BLK]),
                                   ALU.mult).then_inc(split_hi, 1)
                pool.wait_ge(split_hi, n + 1)
                pool.tensor_tensor(w_parts[1][:, s, :], ring[:, s, :], w_parts[0][:, s, :].bitcast(F32),
                                   ALU.subtract).then_inc(split_ready, 1)

            for s in range(RING):
                split(s, s)
            with pool.Fori(1, len(BLOCKS) // RING) as it:
                for s in range(RING):
                    split(s, RING * it + s, (16 * it + 16, RING * it + (s - RING + 1)))
            for n in range(len(BLOCKS) // RING * RING, len(BLOCKS)):
                split(n % RING, n, (16 * (n // RING) + 16, n - RING + 1))


def kernel(**inputs):
    import concourse.bacc as bacc
    from concourse.bass_utils import run_bass_kernel_spmd

    nc = bacc.Bacc("TRN2", target_bir_lowering=False, num_devices=1)
    arrays = host_layout({k: np.asarray(v) for k, v in inputs.items()})
    dram = {name: nc.dram_tensor("in_" + name, a.shape, mybir.dt.from_np(a.dtype), kind="ExternalInput").ap()
            for name, a in arrays.items()}
    out = nc.dram_tensor("out", (P, KD, S), F32, kind="ExternalOutput").ap()
    build(nc, dram, out)
    got = run_bass_kernel_spmd(nc, [{"in_" + n: a for n, a in arrays.items()}], core_ids=[0]).results[0]["out"]
    return np.ascontiguousarray(got.transpose(2, 1, 0).reshape(1, S, D))
```
